# Optimizing a Trainium2 kernel written in Bass

```python
import jax
import jax.numpy as jnp
from jax import lax
import numpy as np

D_MODEL = 1024
BATCH = 1
SEQ = 1024
DEPTH = 1
DEC_BATCH = 8
DEC_SEQ = 8
PAST_LEN = 1024
PAGE_SIZE = 128

A_HEADS = 4
A_HEAD_DIM = 128
A_WIDTH = A_HEADS * A_HEAD_DIM
MLSTM_CHUNK = 128
B_HEADS = 8
B_KV_HEADS = 2
B_HEAD_DIM = 64
B_WIDTH = B_HEADS * B_HEAD_DIM
B_KV_WIDTH = B_KV_HEADS * B_HEAD_DIM
IDX_HEADS = 8
IDX_DIM = 64
MAX_KEEP = 256
QUERY_BLOCK = 128
C_WINDOWS = (2, 4, 8, 16)
C_GROUPS = len(C_WINDOWS)
C_GROUP_WIDTH = 128
C_WIDTH = C_GROUPS * C_GROUP_WIDTH
POOL_BUF = max(C_WINDOWS) - 1
N_EXPERTS = 64
TOP_K = 8
N_EXPERT_GROUPS = 8
TOPK_GROUPS = 4
EXPERT_DIM = 256
SHARED_DIM = 256
ROUTED_SCALE = 2.5
EXPERT_BLOCK = 128
DN_ALPHA = (2 * DEPTH) ** 0.25
DN_BETA = (8 * DEPTH) ** -0.25
LN_EPS = 1e-5

IN_WIDTHS = (A_WIDTH, A_WIDTH, A_WIDTH, A_HEADS, A_HEADS, A_WIDTH,
             B_WIDTH, B_KV_WIDTH, B_KV_WIDTH, IDX_HEADS * IDX_DIM, IDX_DIM, IDX_HEADS,
             C_WIDTH, D_MODEL, D_MODEL, D_MODEL)
IN_WIDTH = sum(IN_WIDTHS)

kernel_name = 'hybrid_mlstm_dsa_pool_moe_step'

def layer_norm(x, g, b):
    xf = x.astype(jnp.float32)
    mu = jnp.mean(xf, axis=-1, keepdims=True)
    var = jnp.mean(jnp.square(xf - mu), axis=-1, keepdims=True)
    y = (xf - mu) * lax.rsqrt(var + LN_EPS) * g.astype(jnp.float32) + b.astype(jnp.float32)
    return y.astype(x.dtype)

def split_projection(x, w_in, b_in):
    proj = jnp.einsum('btd,de->bte', x, w_in) + b_in
    points, acc = [], 0
    for w in IN_WIDTHS[:-1]:
        acc += w
        points.append(acc)
    return jnp.split(proj, points, axis=-1)

def mlstm_prepare(a_q, a_k, a_v, a_i, a_f, b_fgate):
    B, T = a_q.shape[:2]
    def heads(a):
        return jnp.moveaxis(a.astype(jnp.float32).reshape(B, T, A_HEADS, A_HEAD_DIM), 2, 1)
    q = heads(a_q)
    k = heads(a_k) * (A_HEAD_DIM ** -0.5)
    v = heads(a_v)
    li = jnp.moveaxis(a_i.astype(jnp.float32), 2, 1)
    lf = jnp.moveaxis(jax.nn.log_sigmoid(a_f.astype(jnp.float32) + b_fgate.astype(jnp.float32)), 2, 1)
    return q, k, v, li, lf

def mlstm_chunk(state, inputs):
    c_prev, n_prev, m_prev = state
    q, k, v, li, lf = inputs
    L = q.shape[2]
    b = jnp.cumsum(lf, axis=-1)
    causal = jnp.tril(jnp.ones((L, L), dtype=bool))
    d_log = jnp.where(causal, b[..., :, None] - b[..., None, :] + li[..., None, :], -jnp.inf)
    inter = b + m_prev[..., None]
    m_t = jnp.maximum(inter, jnp.max(d_log, axis=-1))
    w_inter = jnp.exp(inter - m_t)
    a = jnp.exp(d_log - m_t[..., None]) * jnp.einsum('bhtd,bhsd->bhts', q, k)
    num = w_inter[..., None] * jnp.einsum('bhtd,bhdv->bhtv', q, c_prev) + jnp.einsum('bhts,bhsv->bhtv', a, v)
    den = w_inter * jnp.einsum('bhtd,bhd->bht', q, n_prev) + jnp.sum(a, axis=-1)
    h = num / jnp.maximum(jnp.abs(den), jnp.exp(-m_t))[..., None]
    m_new = m_t[..., -1]
    w_s = jnp.exp(b[..., -1:] - b + li - m_new[..., None])
    decay = jnp.exp(b[..., -1] + m_prev - m_new)
    c_new = decay[..., None, None] * c_prev + jnp.einsum('bhs,bhsk,bhsv->bhkv', w_s, k, v)
    n_new = decay[..., None] * n_prev + jnp.einsum('bhs,bhsk->bhk', w_s, k)
    return (c_new, n_new, m_new), h

def mlstm_scan(q, k, v, li, lf):
    B, H, T, d = q.shape
    nc = T // MLSTM_CHUNK
    def chunks(a):
        return jnp.moveaxis(a.reshape(B, H, nc, MLSTM_CHUNK, *a.shape[3:]), 2, 0)
    init = (jnp.zeros((B, H, d, d), jnp.float32), jnp.zeros((B, H, d), jnp.float32),
            jnp.full((B, H), -jnp.inf, jnp.float32))
    state, h = lax.scan(mlstm_chunk, init, (chunks(q), chunks(k), chunks(v), chunks(li), chunks(lf)))
    return jnp.moveaxis(h, 0, 2).reshape(B, H, T, d), state

def mlstm_output(h, a_o, a_norm_g):
    hb = jnp.moveaxis(h, 1, 2)
    mu = jnp.mean(hb, axis=-1, keepdims=True)
    var = jnp.mean(jnp.square(hb - mu), axis=-1, keepdims=True)
    hn = ((hb - mu) * lax.rsqrt(var + LN_EPS)).reshape(hb.shape[0], hb.shape[1], A_WIDTH)
    out = jax.nn.sigmoid(a_o.astype(jnp.float32)) * hn * a_norm_g.astype(jnp.float32)
    return out.astype(a_o.dtype)

def sparse_attend(q, qi, wi, q_pos, k, v, ki, n_keep):
    L = k.shape[1]
    dots = jnp.einsum('bqhd,bld->bqhl', qi, ki).astype(jnp.float32) * (IDX_DIM ** -0.5)
    score = jnp.einsum('bqhl,bqh->bql', jax.nn.relu(dots), wi.astype(jnp.float32) * (IDX_HEADS ** -0.5))
    visible = jnp.arange(L)[None, :] <= q_pos[:, None]
    score = jnp.where(visible[None], score, -jnp.inf)
    _, sel = lax.top_k(score, n_keep)
    gather = jax.vmap(lambda rows, idx: rows[idx])
    ks = gather(k, sel)
    vs = gather(v, sel)
    Bn, Qn = q.shape[:2]
    qg = q.reshape(Bn, Qn, B_KV_HEADS, B_HEADS // B_KV_HEADS, B_HEAD_DIM)
    logits = jnp.einsum('bqkgd,bqskd->bqkgs', qg, ks).astype(jnp.float32) * (B_HEAD_DIM ** -0.5)
    ok = (sel <= q_pos[None, :, None])[:, :, None, None, :]
    p = jax.nn.softmax(jnp.where(ok, logits, -jnp.inf), axis=-1)
    o = jnp.einsum('bqkgs,bqskd->bqkgd', p.astype(vs.dtype), vs)
    return o.reshape(Bn, Qn, B_WIDTH)

def dsa_prompt(q, qi, wi, k, v, ki):
    B, T = q.shape[:2]
    n_keep = min(MAX_KEEP, T // 4)
    nb = T // QUERY_BLOCK
    def one_block(i):
        t0 = i * QUERY_BLOCK
        def sl(a):
            return lax.dynamic_slice_in_dim(a, t0, QUERY_BLOCK, axis=1)
        return sparse_attend(sl(q), sl(qi), sl(wi), t0 + jnp.arange(QUERY_BLOCK), k, v, ki, n_keep)
    out = lax.map(one_block, jnp.arange(nb))
    return jnp.moveaxis(out, 0, 1).reshape(B, T, B_WIDTH)

def pool_mix(u, pos0, c_map, c_scale):
    B, R, _ = u.shape
    uf = u.astype(jnp.float32)
    wmax = max(C_WINDOWS)
    cs = jnp.concatenate([jnp.zeros((B, wmax, C_WIDTH), jnp.float32), jnp.cumsum(uf, axis=1)], axis=1)
    pos = pos0 + jnp.arange(R)
    means = []
    for g, w in enumerate(C_WINDOWS):
        lo, hi = g * C_GROUP_WIDTH, (g + 1) * C_GROUP_WIDTH
        win = cs[:, wmax:, lo:hi] - cs[:, wmax - w:wmax - w + R, lo:hi]
        cnt = jnp.minimum(w, pos + 1).astype(jnp.float32)
        means.append(win / cnt[None, :, None])
    pooled = jnp.concatenate(means, axis=-1) - uf
    z = jnp.einsum('btgc,gcd->btgd', pooled.reshape(B, R, C_GROUPS, C_GROUP_WIDTH), c_map.astype(jnp.float32))
    return (z.reshape(B, R, C_WIDTH) * c_scale.astype(jnp.float32)).astype(u.dtype)

def moe_ffn(x2, router_w, router_b, exp_gu, exp_down, sh_gu, sh_down):
    n, d = x2.shape
    f32 = jnp.float32
    scores = jax.nn.sigmoid(x2.astype(f32) @ router_w.astype(f32))
    biased = scores + router_b.astype(f32)
    per_group = N_EXPERTS // N_EXPERT_GROUPS
    group_score = jnp.sum(lax.top_k(biased.reshape(n, N_EXPERT_GROUPS, per_group), 2)[0], axis=-1)
    _, top_groups = lax.top_k(group_score, TOPK_GROUPS)
    group_ok = jnp.any(top_groups[:, :, None] == jnp.arange(N_EXPERT_GROUPS), axis=1)
    expert_ok = jnp.repeat(group_ok, per_group, axis=1)
    _, sel = lax.top_k(jnp.where(expert_ok, biased, -jnp.inf), TOP_K)
    s_sel = jnp.take_along_axis(scores, sel, axis=-1)
    gates = ROUTED_SCALE * s_sel / jnp.sum(s_sel, axis=-1, keepdims=True)
    n_assign = n * TOP_K
    n_blocks = -(-(n_assign + N_EXPERTS * (EXPERT_BLOCK - 1)) // EXPERT_BLOCK)
    n_rows = n_blocks * EXPERT_BLOCK
    flat_e = sel.reshape(-1)
    order = jnp.argsort(flat_e)
    e_sorted = flat_e[order]
    counts = jnp.bincount(flat_e, length=N_EXPERTS)
    padded = (counts + EXPERT_BLOCK - 1) // EXPERT_BLOCK * EXPERT_BLOCK
    p_end = jnp.cumsum(padded)
    starts = jnp.cumsum(counts) - counts
    dest = (p_end - padded)[e_sorted] + jnp.arange(n_assign) - starts[e_sorted]
    tok = (jnp.arange(n_assign) // TOP_K)[order].astype(jnp.int32)
    row_tok = jnp.zeros((n_rows,), jnp.int32).at[dest].set(tok)
    row_gate = jnp.zeros((n_rows,), f32).at[dest].set(gates.reshape(-1)[order])
    block_expert = jnp.minimum(jnp.searchsorted(p_end, jnp.arange(n_blocks) * EXPERT_BLOCK, side='right'), N_EXPERTS - 1)

    def expert_block(args):
        tok_b, gate_b, e = args
        g, u = jnp.split(x2[tok_b] @ exp_gu[e], 2, axis=-1)
        return ((jax.nn.silu(g) * u) @ exp_down[e]).astype(f32) * gate_b[:, None]

    rows = lax.map(expert_block, (row_tok.reshape(n_blocks, EXPERT_BLOCK),
                                  row_gate.reshape(n_blocks, EXPERT_BLOCK), block_expert))
    routed = jnp.zeros((n, d), f32).at[row_tok].add(rows.reshape(n_rows, d))
    sg, su = jnp.split(x2 @ sh_gu, 2, axis=-1)
    shared = (jax.nn.silu(sg) * su) @ sh_down
    return (routed + shared.astype(f32)).astype(x2.dtype)

def finish_layer(x, h_a, h_b, h_c, g_a, g_b, g_c, post):
    (p_a, p_b, p_c, w_out, ln1_g, ln1_b, router_w, router_b,
     exp_gu, exp_down, sh_gu, sh_down, ln2_g, ln2_b) = post
    merged = (jax.nn.sigmoid(g_a) * (h_a @ p_a) + jax.nn.sigmoid(g_b) * (h_b @ p_b)
              + jax.nn.sigmoid(g_c) * (h_c @ p_c))
    x = layer_norm(DN_ALPHA * x + merged @ w_out, ln1_g, ln1_b)
    B, T, D = x.shape
    ff = moe_ffn(x.reshape(B * T, D), router_w, router_b, exp_gu, exp_down, sh_gu, sh_down).reshape(B, T, D)
    return layer_norm(DN_ALPHA * x + ff, ln2_g, ln2_b)

def prompt_layer(x, w_in, b_in, b_fgate, a_norm_g, c_map, c_scale, post):
    B, T, _ = x.shape
    (a_q, a_k, a_v, a_i, a_f, a_o, b_q, b_k, b_v, b_iq, b_ik, b_iw,
     c_u, g_a, g_b, g_c) = split_projection(x, w_in, b_in)
    q, k, v, li, lf = mlstm_prepare(a_q, a_k, a_v, a_i, a_f, b_fgate)
    h, (c_fin, n_fin, m_fin) = mlstm_scan(q, k, v, li, lf)
    h_a = mlstm_output(h, a_o, a_norm_g)
    kb = b_k.reshape(B, T, B_KV_HEADS, B_HEAD_DIM)
    vb = b_v.reshape(B, T, B_KV_HEADS, B_HEAD_DIM)
    h_b = dsa_prompt(b_q.reshape(B, T, B_HEADS, B_HEAD_DIM), b_iq.reshape(B, T, IDX_HEADS, IDX_DIM),
                     b_iw, kb, vb, b_ik)
    h_c = pool_mix(c_u, 0, c_map, c_scale)
    y = finish_layer(x, h_a, h_b, h_c, g_a, g_b, g_c, post)
    dt = x.dtype
    return y, (kb, vb, b_ik, c_fin.astype(dt), n_fin.astype(dt), m_fin.astype(dt), c_u[:, T - POOL_BUF:])

def sample_layer(x, cache_k, cache_v, cache_kidx, st_c, st_n, st_m, st_pool, page_table,
                 w_in, b_in, b_fgate, a_norm_g, c_map, c_scale, post):
    Bd, T, _ = x.shape
    f32 = jnp.float32
    (a_q, a_k, a_v, a_i, a_f, a_o, b_q, b_k, b_v, b_iq, b_ik, b_iw,
     c_u, g_a, g_b, g_c) = split_projection(x, w_in, b_in)
    q, k, v, li, lf = mlstm_prepare(a_q, a_k, a_v, a_i, a_f, b_fgate)
    (c_new, n_new, m_new), h = mlstm_chunk((st_c.astype(f32), st_n.astype(f32), st_m.astype(f32)),
                                           (q, k, v, li, lf))
    h_a = mlstm_output(h, a_o, a_norm_g)
    past_len = page_table.shape[1] * cache_k.shape[1]
    def past(cache):
        return cache[page_table].reshape(Bd, past_len, *cache.shape[2:])
    kb = b_k.reshape(Bd, T, B_KV_HEADS, B_HEAD_DIM)
    vb = b_v.reshape(Bd, T, B_KV_HEADS, B_HEAD_DIM)
    k_all = jnp.concatenate([past(cache_k).astype(kb.dtype), kb], axis=1)
    v_all = jnp.concatenate([past(cache_v).astype(vb.dtype), vb], axis=1)
    ki_all = jnp.concatenate([past(cache_kidx).astype(b_ik.dtype), b_ik], axis=1)
    q_pos = past_len + jnp.arange(T)
    h_b = sparse_attend(b_q.reshape(Bd, T, B_HEADS, B_HEAD_DIM), b_iq.reshape(Bd, T, IDX_HEADS, IDX_DIM),
                        b_iw, q_pos, k_all, v_all, ki_all, min(MAX_KEEP, (past_len + T) // 4))
    n_buf = st_pool.shape[1]
    u_full = jnp.concatenate([st_pool.astype(c_u.dtype), c_u], axis=1)
    h_c = pool_mix(u_full, past_len - n_buf, c_map, c_scale)[:, n_buf:]
    y = finish_layer(x, h_a, h_b, h_c, g_a, g_b, g_c, post)
    dt = x.dtype
    return y, (kb, vb, b_ik, c_new.astype(dt), n_new.astype(dt), m_new.astype(dt), u_full[:, -n_buf:])

def setup_inputs(seed: int = 0) -> dict:
    key = jax.random.key(seed)
    keys = iter(jax.random.split(key, 40))
    def normal(shape, scale):
        return scale * jax.random.normal(next(keys), shape, jnp.float32)
    n_pages = PAST_LEN // PAGE_SIZE
    n_pool = (DEC_BATCH * n_pages * 5) // 4
    x_prompt = normal((BATCH, SEQ, D_MODEL), 1.0)
    x_sample = normal((DEC_BATCH, DEC_SEQ, D_MODEL), 1.0)
    cache_k = normal((DEPTH, n_pool, PAGE_SIZE, B_KV_HEADS, B_HEAD_DIM), 1.0)
    cache_v = normal((DEPTH, n_pool, PAGE_SIZE, B_KV_HEADS, B_HEAD_DIM), 1.0)
    cache_kidx = normal((DEPTH, n_pool, PAGE_SIZE, IDX_DIM), 1.0)
    state_C = normal((DEPTH, DEC_BATCH, A_HEADS, A_HEAD_DIM, A_HEAD_DIM), 0.1)
    state_n = normal((DEPTH, DEC_BATCH, A_HEADS, A_HEAD_DIM), 0.3)
    state_m = normal((DEPTH, DEC_BATCH, A_HEADS), 1.0)
    state_pool = normal((DEPTH, DEC_BATCH, POOL_BUF, C_WIDTH), 1.0)
    page_table = jax.random.permutation(next(keys), n_pool)[:DEC_BATCH * n_pages].reshape(
        DEC_BATCH, n_pages).astype(jnp.int32)
    w_in = normal((DEPTH, D_MODEL, IN_WIDTH), D_MODEL ** -0.5)
    b_in = normal((DEPTH, IN_WIDTH), 0.02)
    b_fgate = jnp.linspace(3.0, 6.0, A_HEADS)[None, :] + normal((DEPTH, A_HEADS), 0.1)
    a_norm_g = 1.0 + normal((DEPTH, A_WIDTH), 0.02)
    c_map = normal((DEPTH, C_GROUPS, C_GROUP_WIDTH, C_GROUP_WIDTH), C_GROUP_WIDTH ** -0.5)
    c_scale = 1.0 + normal((DEPTH, C_WIDTH), 0.02)
    p_a = normal((DEPTH, A_WIDTH, D_MODEL), DN_BETA * A_WIDTH ** -0.5)
    p_b = normal((DEPTH, B_WIDTH, D_MODEL), DN_BETA * B_WIDTH ** -0.5)
    p_c = normal((DEPTH, C_WIDTH, D_MODEL), DN_BETA * C_WIDTH ** -0.5)
    w_out = normal((DEPTH, D_MODEL, D_MODEL), DN_BETA * D_MODEL ** -0.5)
    ln1_g = 1.0 + normal((DEPTH, D_MODEL), 0.02)
    ln1_b = normal((DEPTH, D_MODEL), 0.02)
    router_w = normal((DEPTH, D_MODEL, N_EXPERTS), D_MODEL ** -0.5)
    router_b = normal((DEPTH, N_EXPERTS), 0.01)
    exp_gu = normal((DEPTH, N_EXPERTS, D_MODEL, 2 * EXPERT_DIM), D_MODEL ** -0.5)
    exp_down = normal((DEPTH, N_EXPERTS, EXPERT_DIM, D_MODEL), DN_BETA * EXPERT_DIM ** -0.5)
    sh_gu = normal((DEPTH, D_MODEL, 2 * SHARED_DIM), D_MODEL ** -0.5)
    sh_down = normal((DEPTH, SHARED_DIM, D_MODEL), DN_BETA * SHARED_DIM ** -0.5)
    ln2_g = 1.0 + normal((DEPTH, D_MODEL), 0.02)
    ln2_b = normal((DEPTH, D_MODEL), 0.02)
    return {'x_prompt': x_prompt, 'x_sample': x_sample, 'cache_k': cache_k, 'cache_v': cache_v,
            'cache_kidx': cache_kidx, 'state_C': state_C, 'state_n': state_n, 'state_m': state_m,
            'state_pool': state_pool, 'page_table': page_table, 'w_in': w_in, 'b_in': b_in,
            'b_fgate': b_fgate, 'a_norm_g': a_norm_g, 'c_map': c_map, 'c_scale': c_scale,
            'p_a': p_a, 'p_b': p_b, 'p_c': p_c, 'w_out': w_out, 'ln1_g': ln1_g, 'ln1_b': ln1_b,
            'router_w': router_w, 'router_b': router_b, 'exp_gu': exp_gu, 'exp_down': exp_down,
            'sh_gu': sh_gu, 'sh_down': sh_down, 'ln2_g': ln2_g, 'ln2_b': ln2_b}

def reference(x_prompt, x_sample, cache_k, cache_v, cache_kidx, state_C, state_n, state_m, state_pool,
              page_table, w_in, b_in, b_fgate, a_norm_g, c_map, c_scale, p_a, p_b, p_c, w_out,
              ln1_g, ln1_b, router_w, router_b, exp_gu, exp_down, sh_gu, sh_down, ln2_g, ln2_b):
    y_p, y_s = x_prompt, x_sample
    new_p, new_s = [], []
    for l in range(DEPTH):
        post = (p_a[l], p_b[l], p_c[l], w_out[l], ln1_g[l], ln1_b[l], router_w[l], router_b[l],
                exp_gu[l], exp_down[l], sh_gu[l], sh_down[l], ln2_g[l], ln2_b[l])
        y_p, st_p = prompt_layer(y_p, w_in[l], b_in[l], b_fgate[l], a_norm_g[l], c_map[l], c_scale[l], post)
        y_s, st_s = sample_layer(y_s, cache_k[l], cache_v[l], cache_kidx[l], state_C[l], state_n[l],
                                 state_m[l], state_pool[l], page_table, w_in[l], b_in[l], b_fgate[l],
                                 a_norm_g[l], c_map[l], c_scale[l], post)
        new_p.append(st_p)
        new_s.append(st_s)

    def stacked(states, i):
        return jnp.stack([s[i] for s in states])

    return (y_p, y_s,
            stacked(new_p, 0), stacked(new_s, 0),
            stacked(new_p, 1), stacked(new_s, 1),
            stacked(new_p, 2), stacked(new_s, 2),
            stacked(new_p, 3), stacked(new_s, 3),
            stacked(new_p, 4), stacked(new_s, 4),
            stacked(new_p, 5), stacked(new_s, 5),
            stacked(new_p, 6), stacked(new_s, 6))


_drawn_inputs = setup_inputs


def setup_inputs(seed=0):
    import zlib

    import numpy as np

    out = dict(_drawn_inputs(seed))
    spreads = {}
    factors = {'a_norm_g': 3.688, 'c_scale': 3.378, 'ln2_g': 2.731, 'ln2_b': 2.93}
    for name, (base, spread) in spreads.items():
        noise = np.random.default_rng([zlib.crc32(name.encode()), seed]).standard_normal(out[name].shape)
        drawn = base * np.exp(spread * noise) if base else spread * noise
        out[name] = jnp.asarray(drawn.astype(out[name].dtype))
    for name, factor in factors.items():
        out[name] = (out[name] * factor).astype(out[name].dtype)
    return out
```

```python
from contextlib import ExitStack

import numpy as np

import concourse.bass as bass
from concourse import mybir

F32 = mybir.dt.float32
I32 = mybir.dt.int32
U32 = mybir.dt.uint32
ALU = mybir.AluOpType
ACT = mybir.ActivationFunctionType
AX = mybir.AxisListType.X

P = 128
D = 1024
KT = D // P
SEQ = 1024
NB, NS = 8, 8
SM = NB * NS
N = SEQ + SM
NT = -(-N // P)
H, HD = 4, 128
NCH = SEQ // P
BH, BKV, BD = 8, 2, 64
KEEP = 256
PG = 128
NPG = 8
NPOOL = 80
PAST = PG * NPG
NK = PAST + SM
WINDOWS = (2, 4, 8, 16)
POOLB = 15
E, EG, TOPG, TOPK = 64, 8, 4, 8
F = 256
CAP = 192
ROUNDS = -(-N // CAP)
ECAP = ROUNDS * CAP
SHIFT = 11
ALPHA = 2 ** 0.25
EPS = 1e-5
BIG = 1e30
GONE = -3e38

OFF = {}
_at = 0
for _n, _w in (("q", 512), ("k", 512), ("v", 512), ("i", 4), ("f", 4), ("o", 512), ("bq", 512), ("bk", 128),
               ("bv", 128), ("iq", 512), ("ik", 64), ("iw", 8), ("u", 512), ("ga", D), ("gb", D), ("gc", D)):
    OFF[_n] = _at
    _at += _w
IN_W = _at
TOKEN_CHUNKS = ((0, 512), (512, 512), (1024, 64))
BC = {"q": 0, "k": 4, "bq": 8, "bk": 12, "ik": 13, "iq": 14, "u": 18, "g": 22, "i": 46, "f": 47, "ff": 48}
NBC = 49


def rows(t):
    return min(P, N - t * P)


class Core:
    pass


def build(nc, a, upto=99):
    ds = bass.ds
    ctx = ExitStack()
    with ctx:
        ctx.enter_context(nc.allow_non_contiguous_dma(reason="biases, stabilisers: a few KB"))
        live = []

        def sem(name):
            live.append(nc.alloc_semaphore(name))
            return live[-1]

        def renew():
            nc.clear_and_free_semaphores(live)
            nc.all_engine_barrier()
            live.clear()

        def sb(name, shape, dt=F32, c=ctx):
            return c.enter_context(nc.sbuf_tensor(name, shape, dt))

        banks = ctx.enter_context(nc.psum_tensor("banks", [P, 8, 512], F32))
        ps = [banks[:, i, :] for i in range(8)]

        x_p = a["x_prompt"].rearrange("b t d -> (b t) d")
        x_s = a["x_sample"].rearrange("b t d -> (b t) d")
        w_in = a["w_in"][0].rearrange("(k p) n -> p k n", p=P)
        b_in = a["b_in"]

        def token_rows(prompt, sample, t):
            return prompt[t * P:(t + 1) * P] if t < NCH else sample

        mixer = ExitStack()
        ident = sb("ident", [P, P])
        ones = sb("ones", [P, P])
        causalT = sb("causalT", [P, P])
        sampleT = sb("sampleT", [SM, SM])
        sampleQ = sb("sampleQ", [SM, SM])
        own = sb("own", [SM, NB])
        before = sb("before", [P, P])
        pick = sb("pick", [H, H, P])
        neghalf = sb("neghalf", [P, H])
        xT = sb("xT", [P, KT, N])
        hT = sb("hT", [P, 12, N], c=mixer)
        biasc = sb("biasc", [P, NBC], c=mixer)
        biasr = sb("biasr", [1, 512 + 512 + 256 + 72], c=mixer)
        s_const = sem("s_const")
        s_bias = sem("s_bias")

        s_x = [sem(f"s_x{i}") for i in range(3)]
        s_xps = sem("s_xps")
        s_xev_act, s_xev_dve = sem("s_xev_act"), sem("s_xev_dve")
        n_bias_dmas = 17
        with ExitStack() as c0, nc.Block() as block:
            xin = sb("xin", [P, 3, D], c=c0)

            @block.sync
            def _(sp):
                for t in range(NT):
                    if t >= 3:
                        sp.wait_ge(s_xps, 2 * (t - 2))
                    sp.dma_start(xin[0:rows(t), t % 3, :], token_rows(x_p, x_s, t)).then_inc(s_x[t % 3], 16)

            @block.gpsimd
            def _(pool):
                n = 0

                def step(ins):
                    nonlocal n
                    n += 1
                    ins.then_inc(s_const, 1)

                for m, v in ((ident, 0.0), (ones, 1.0), (causalT, 1.0), (sampleT, 1.0), (sampleQ, 1.0), (own, 1.0),
                             (before, 1.0), (pick, 1.0), (neghalf, -0.5)):
                    step(pool.memset(m[:], v))
                pool.wait_ge(s_const, n)
                step(pool.affine_select(out=ident[:], in_=ident[:], compare_op=ALU.not_equal, fill=1.0, base=0,
                                        pattern=[[-1, P]], channel_multiplier=1))
                step(pool.affine_select(out=causalT[:], in_=causalT[:], compare_op=ALU.is_ge, fill=0.0, base=0,
                                        pattern=[[1, P]], channel_multiplier=-1))
                step(pool.affine_select(out=before[:], in_=before[:], compare_op=ALU.is_ge, fill=0.0, base=-1,
                                        pattern=[[1, P]], channel_multiplier=-1))
                step(pool.affine_select(out=pick[:], in_=pick[:], compare_op=ALU.is_equal, fill=0.0, base=0,
                                        pattern=[[-1, H], [0, P]], channel_multiplier=1))
                s3 = sampleT[:].rearrange("s (b j) -> s b j", j=NS)
                step(pool.affine_select(out=s3, in_=s3, compare_op=ALU.is_ge, fill=0.0, base=0,
                                        pattern=[[-NS, NB], [0, NS]], channel_multiplier=1))
                q3 = sampleQ[:].rearrange("t (b j) -> t b j", j=NS)
                step(pool.affine_select(out=q3, in_=q3, compare_op=ALU.is_ge, fill=0.0, base=0,
                                        pattern=[[-NS, NB], [-1, NS]], channel_multiplier=1))
                step(pool.affine_select(out=own[:], in_=own[:], compare_op=ALU.is_ge, fill=0.0, base=0,
                                        pattern=[[-NS, NB]], channel_multiplier=1))
                pool.wait_ge(s_const, n)
                step(pool.affine_select(out=s3, in_=s3, compare_op=ALU.is_ge, fill=0.0, base=0,
                                        pattern=[[NS, NB], [1, NS]], channel_multiplier=-1))
                step(pool.affine_select(out=q3, in_=q3, compare_op=ALU.is_ge, fill=0.0, base=NS - 1,
                                        pattern=[[NS, NB], [0, NS]], channel_multiplier=-1))
                step(pool.affine_select(out=own[:], in_=own[:], compare_op=ALU.is_ge, fill=0.0, base=NS - 1,
                                        pattern=[[NS, NB]], channel_multiplier=-1))

                def column(at, off, count):
                    src = b_in[0, off:off + P * count].rearrange("(c p) -> p c", p=P)
                    pool.dma_start(biasc[:, at:at + count], src).then_inc(s_bias, 16)

                column(BC["q"], OFF["q"], 4)
                column(BC["k"], OFF["k"], 4)
                for g in range(BKV):
                    src = b_in[0, OFF["bq"] + 256 * g:OFF["bq"] + 256 * (g + 1)].rearrange("(c p) -> p c", p=BD)
                    pool.dma_start(biasc[64 * g:64 * g + 64, BC["bq"]:BC["bq"] + 4], src).then_inc(s_bias, 16)
                    src = b_in[0:1, OFF["ik"]:OFF["ik"] + 64].rearrange("a p -> p a")
                    pool.dma_start(biasc[64 * g:64 * g + 64, BC["ik"]:BC["ik"] + 1], src).then_inc(s_bias, 16)
                column(BC["bk"], OFF["bk"], 1)
                column(BC["iq"], OFF["iq"], 4)
                column(BC["u"], OFF["u"], 4)
                column(BC["g"], OFF["ga"], 24)
                for name in "if":
                    src = b_in[0:1, OFF[name]:OFF[name] + H].rearrange("a p -> p a")
                    pool.dma_start(biasc[0:H, BC[name]:BC[name] + 1], src).then_inc(s_bias, 16)
                pool.dma_start(biasc[0:H, BC["ff"]:BC["ff"] + 1], a["b_fgate"].rearrange("a p -> p a")).then_inc(s_bias, 16)
                pool.dma_start(biasr[:, 0:512], b_in[:, OFF["v"]:OFF["v"] + 512]).then_inc(s_bias, 16)
                pool.dma_start(biasr[:, 512:1024], b_in[:, OFF["o"]:OFF["o"] + 512]).then_inc(s_bias, 16)
                pool.dma_start(biasr[:, 1024:1096], b_in[:, OFF["ik"]:OFF["ik"] + 72]).then_inc(s_bias, 16)
                pool.dma_start(biasr[:, 1096:1352], b_in[:, OFF["bk"]:OFF["bk"] + 256]).then_inc(s_bias, 16)
                pool.wait_ge(s_bias, 16 * n_bias_dmas)
                pool.wait_ge(s_const, n)

            @block.tensor
            def _(pe):
                pe.wait_ge(s_const, 10)
                for t in range(NT):
                    pe.wait_ge(s_x[t % 3], 16 * (t // 3 + 1))
                    for h in range(2):
                        j = 2 * t + h
                        if j >= 8:
                            pe.wait_ge((s_xev_act, s_xev_dve)[h], t - 3)
                        for k in range(4):
                            last = pe.transpose(ps[j % 8][:, k * P:k * P + rows(t)],
                                                xin[0:rows(t), t % 3, (4 * h + k) * P:(4 * h + k + 1) * P],
                                                ident[0:rows(t), 0:rows(t)])
                        last.then_inc(s_xps, 1)

            def spread(h, t):
                return (xT[:, 4 * h:4 * h + 4, t * P:t * P + rows(t)],
                        ps[(2 * t + h) % 8].rearrange("p (k n) -> p k n", k=4)[:, :, 0:rows(t)])

            @block.scalar
            def _(act):
                for t in range(NT):
                    act.wait_ge(s_xps, 2 * t + 1)
                    act.copy(*spread(0, t)).then_inc(s_xev_act, 1)

            @block.vector
            def _(dve):
                if "dump" in a:
                    dve.memset(hT[:], 0.0)
                for t in range(NT):
                    dve.wait_ge(s_xps, 2 * t + 2)
                    dve.tensor_copy(*spread(1, t)).then_inc(s_xev_dve, 1)

        k = Core()
        k.banks = banks
        k.ps, k.w_in, k.x_p, k.x_s, k.token_rows, k.sem, k.sb = ps, w_in, x_p, x_s, token_rows, sem, sb
        k.ident, k.ones, k.causalT, k.sampleT, k.sampleQ, k.own = ident, ones, causalT, sampleT, sampleQ, own
        k.before, k.pick, k.neghalf = before, pick, neghalf
        k.xT, k.hT, k.biasc, k.biasr = xT, hT, biasc, biasr
        build_mlstm(nc, a, k)
        renew()
        if upto >= 2:
            build_attention(nc, a, k)
            renew()
        if upto >= 3:
            build_pooling(nc, a, k)
        if upto >= 4:
            build_merge(nc, a, k)
            renew()
            mixer.close()
        else:
            if "dump" in a:
                with nc.Block() as block:
                    s_d = sem("s_dump")
                    @block.sync
                    def _(sp):
                        sp.dma_start(a["dump"], hT[:]).then_inc(s_d, 16)
                        sp.wait_ge(s_d, 16)
            mixer.close()
        if upto >= 5:
            build_moe(nc, a, k)


def product(pe, bank, mt, left, right, count, bias=None):
    n = count + (bias is not None)
    for k in range(count):
        last = pe.matmul(bank, left(k), right(k), start=(k == 0), stop=(k == n - 1))
    if bias is not None:
        last = pe.matmul(bank, bias[0], bias[1], start=(n == 1), stop=True)
    return last


def banks_before(jobs, engine, j):
    return sum(job[-1] == engine for job in jobs[:j])


def build_mlstm(nc, a, k):
    ps, ident, ones, xT, hT, biasc, biasr, sem = k.ps, k.ident, k.ones, k.xT, k.hT, k.biasc, k.biasr, k.sem
    out_c, out_n, out_m = a["C_prompt"], a["n_prompt"], a["m_prompt"]
    outs_c, outs_n, outs_m = a["C_sample"], a["n_sample"], a["m_sample"]
    with ExitStack() as ca:
        def sb(name, shape, dt=F32, c=ca):
            return k.sb(name, shape, dt, c)

        qT = sb("qT", [P, H, N])
        kT = sb("kT", [P, H, N])
        vaug = sb("vaug", [P, NT, H, HD + 1])
        gate_o = sb("gate_o", [P, NT, H * HD])

        groups = ["q", "k", "v", "o"]
        jobs = [("row", name, n0, nn, "act") for name in "if" for n0, nn in TOKEN_CHUNKS]
        for name, eng in (("q", "act"), ("k", "dve")):
            jobs += [(name, ct, n0, nn, eng) for ct in range(4) for n0, nn in TOKEN_CHUNKS]
        jobs += [("v", t, "dve") for t in range(NT)] + [("o", t, "act") for t in range(NT)]
        row = {n: hT[0:H, 4 + i, :] for i, n in enumerate(("li", "f", "t", "g", "gm", "m", "wi", "en"))}
        keep = sb("keep", [H, N])
        mp = sb("mp", [H, NCH + NB])
        decay = sb("decay", [H, NCH + NB])
        mend = sb("mend", [H, NCH + NB])
        s_wg = [sem("s_wg0"), sem("s_wg1")]
        s_wif, s_gfree = sem("s_wif"), sem("s_gfree")
        s_full, s_out_act, s_out_dve = sem("s_full"), sem("s_out_act"), sem("s_out_dve")
        s_gain, s_ones_v, s_og, s_gscale = sem("s_gain"), sem("s_ones_v"), sem("s_og"), sem("s_gscale")
        s_rowd, s_rowa, s_mst, s_mout = sem("s_rowd"), sem("s_rowa"), sem("s_mst"), sem("s_mout")
        with ExitStack() as cw, nc.Block() as block:
            w = sb("w_groups", [P, 2, KT, 512], c=cw)
            wif = sb("w_if", [P, KT, 8], c=cw)
            gain = sb("gain", [P, H * HD], c=cw)

            @block.sync
            def _(sp):
                sp.dma_start(wif[:], k.w_in[:, :, OFF["i"]:OFF["i"] + 8]).then_inc(s_wif, 16)
                for g, name in enumerate(groups):
                    if g >= 2:
                        sp.wait_ge(s_gfree, g - 1)
                    sp.dma_start(w[:, g % 2], k.w_in[:, :, OFF[name]:OFF[name] + 512]).then_inc(s_wg[g % 2], 16)
                    if g == 0:
                        sp.dma_start(gain[:], a["a_norm_g"].broadcast_to([P, H * HD])).then_inc(s_gain, 16)
                        sp.dma_start(mp[:, NCH:], a["state_m"][0].rearrange("b h -> h b")).then_inc(s_mst, 16)
                sp.wait_ge(s_rowd, 16)
                sp.dma_start(out_m[0].rearrange("b h -> h b"), mend[:, NCH - 1:NCH]).then_inc(s_mout, 16)
                sp.dma_start(outs_m[0].rearrange("b h -> h b"), mend[:, NCH:]).then_inc(s_mout, 16)
                sp.wait_ge(s_mout, 32)

            @block.tensor
            def _(pe):
                pe.wait_ge(s_wif, 16)
                for j, job in enumerate(jobs):
                    if j >= 8:
                        eng = jobs[j - 8][-1]
                        pe.wait_ge({"act": s_out_act, "dve": s_out_dve}[eng], banks_before(jobs, eng, j - 7))
                    bank = ps[j % 8]
                    if job[0] == "row":
                        _, name, n0, nn, _ = job
                        c0 = 0 if name == "i" else 4
                        last = product(pe, bank[0:H, 0:nn], H, lambda kt: wif[:, kt, c0:c0 + H],
                                       lambda kt: xT[:, kt, n0:n0 + nn], KT)
                    elif job[0] in ("q", "k"):
                        name, ct, n0, nn, _ = job
                        g = groups.index(name)
                        if ct == 0 and n0 == 0:
                            pe.wait_ge(s_wg[g % 2], 16 * (g // 2 + 1))
                        last = product(pe, bank[:, 0:nn], P, lambda kt: w[:, g % 2, kt, ct * P:(ct + 1) * P],
                                       lambda kt: xT[:, kt, n0:n0 + nn], KT)
                    else:
                        name, t, _ = job
                        g = groups.index(name)
                        if t == 0:
                            pe.wait_ge(s_wg[g % 2], 16 * (g // 2 + 1))
                        r, b0 = rows(t), 0 if name == "v" else 512
                        last = product(pe, bank[0:r, :], r, lambda kt: xT[:, kt, t * P:t * P + r],
                                       lambda kt: w[:, g % 2, kt, :], KT, (ones[0:1, 0:r], biasr[:, b0:b0 + 512]))
                    last.then_inc(s_full, 1)
                    if job[0] in groups and (j + 1 == len(jobs) or jobs[j + 1][0] != job[0]):
                        pe.wait_ge(s_full, j + 1)
                        pe.sem_inc(s_gfree, 1)

            @block.scalar
            def _(act):
                for j, job in enumerate(jobs):
                    if job[-1] != "act":
                        continue
                    act.wait_ge(s_full, j + 1)
                    bank = ps[j % 8]
                    if job[0] == "row":
                        _, name, n0, nn, _ = job
                        act.activation(row["li" if name == "i" else "f"][:, n0:n0 + nn], bank[0:H, 0:nn], ACT.Identity,
                                       bias=biasc[0:H, BC[name]:BC[name] + 1]).then_inc(s_out_act, 1)
                    elif job[0] == "q":
                        _, ct, n0, nn, _ = job
                        act.activation(qT[:, ct, n0:n0 + nn], bank[:, 0:nn], ACT.Identity,
                                       bias=biasc[:, BC["q"] + ct:BC["q"] + ct + 1]).then_inc(s_out_act, 1)
                    else:
                        t = job[1]
                        act.activation(gate_o[0:rows(t), t, :], bank[0:rows(t), :], ACT.Sigmoid).then_inc(s_out_act, 1)
                    if j == 5:
                        act.wait_ge(s_rowd, 2)
                        act.activation(row["t"], row["t"], ACT.Exp, scale=-1.0).then_inc(s_rowa, 1)
                        act.wait_ge(s_rowd, 3)
                        act.activation(row["t"], row["t"], ACT.Ln).then_inc(s_rowa, 1)
                        act.wait_ge(s_rowd, 15)
                        act.activation(row["wi"], row["wi"], ACT.Exp).then_inc(s_rowa, 1)
                        act.activation(row["en"], row["en"], ACT.Exp, scale=-1.0).then_inc(s_rowa, 1)
                        act.activation(row["gm"], row["gm"], ACT.Exp).then_inc(s_rowa, 1)
                        act.activation(decay[:], decay[:], ACT.Exp).then_inc(s_rowa, 1)

            @block.gpsimd
            def _(pool):
                pool.memset(vaug[:, :, :, HD:HD + 1], 1.0).then_inc(s_ones_v, 1)
                pool.wait_ge(s_gain, 16)
                for t in range(NT):
                    j = [i for i, job in enumerate(jobs) if job[0] == "o"][t]
                    pool.wait_ge(s_out_act, banks_before(jobs, "act", j + 1))
                    g = gate_o[0:rows(t), t, :]
                    pool.tensor_tensor(g, g, gain[0:rows(t), :], ALU.mult).then_inc(s_og, 1)
                pool.wait_ge(s_og, NT)
                pool.wait_ge(s_ones_v, 1)

            @block.vector
            def _(dve):
                n = 0

                def step(ins):
                    nonlocal n
                    n += 1
                    ins.then_inc(s_rowd, 1)
                    dve.wait_ge(s_rowd, n)

                R = row
                starts = keep[:, 0:SEQ].rearrange("h (c t) -> h c t", t=P)[:, :, 0:1]
                starts_s = keep[:, SEQ:].rearrange("h (b t) -> h b t", t=NS)[:, :, 0:1]

                def last_of(r):
                    return (r[:, 0:SEQ].rearrange("h (c t) -> h c t", t=P)[:, :, P - 1:P],
                            r[:, SEQ:].rearrange("h (b t) -> h b t", t=NS)[:, :, NS - 1:NS])

                def first_of(r):
                    return (r[:, 0:SEQ].rearrange("h (c t) -> h c t", t=P)[:, :, 0:1],
                            r[:, SEQ:].rearrange("h (b t) -> h b t", t=NS)[:, :, 0:1])

                def cut(r):
                    return (r[:, 0:SEQ].rearrange("h (c t) -> h c t", t=P),
                            r[:, SEQ:].rearrange("h (b t) -> h b t", t=NS))

                def each(r, c0, c1, n_):
                    return r[:, c0:c1].unsqueeze(2).to_broadcast([H, c1 - c0, n_])

                dve.memset(keep[:], 1.0)
                dve.wait_ge(s_out_act, 6)
                dve.wait_ge(s_mst, 16)
                step(dve.tensor_scalar(R["f"], R["f"], biasc[0:H, BC["ff"]:BC["ff"] + 1], None, ALU.add))
                dve.memset(starts, 0.0)
                dve.memset(starts_s, 0.0)
                step(dve.scalar_tensor_tensor(R["t"], R["f"], -1.0, R["f"], ALU.mult, ALU.max))
                dve.wait_ge(s_rowa, 1)
                step(dve.tensor_scalar(R["t"], R["t"], 1.0, None, ALU.add))
                dve.wait_ge(s_rowa, 2)
                step(dve.scalar_tensor_tensor(R["f"], R["f"], 0.0, R["t"], ALU.min, ALU.subtract))
                step(dve.tensor_tensor_scan(R["t"], keep[:], R["f"], 0.0, ALU.mult, ALU.add))
                step(dve.tensor_tensor(R["g"], R["li"], R["t"], ALU.subtract))
                dve.tensor_copy(R["gm"], R["g"])
                step(dve.memset(R["f"], 0.0))
                fp, fs = first_of(R["gm"])
                dve.tensor_tensor(fs, fs, mp[:, NCH:].unsqueeze(2), ALU.max)
                bp, _ = last_of(R["t"])
                dp, dsm = first_of(R["f"])
                dve.tensor_copy(dp[:, 1:NCH], bp[:, 0:NCH - 1])
                step(dve.memset(dsm, -BIG))
                step(dve.tensor_tensor_scan(R["m"], R["f"], R["gm"], -BIG, ALU.add, ALU.max))
                mlp, mls = last_of(R["m"])
                _, bs = last_of(R["t"])
                dve.tensor_tensor(mend[:, 0:NCH].unsqueeze(2), mlp, bp, ALU.add)
                dve.tensor_tensor(mend[:, NCH:].unsqueeze(2), mls, bs, ALU.add)
                dve.memset(mp[:, 0:1], -BIG)
                step(dve.tensor_tensor(R["en"], R["t"], R["m"], ALU.add))
                step(dve.tensor_copy(mp[:, 1:NCH], mend[:, 0:NCH - 1]))
                for c0, c1, n_, m3, w3, g3, s3, l3 in (
                        (0, NCH, P, cut(R["m"])[0], cut(R["wi"])[0], cut(R["g"])[0], cut(R["gm"])[0], mlp),
                        (NCH, NCH + NB, NS, cut(R["m"])[1], cut(R["wi"])[1], cut(R["g"])[1], cut(R["gm"])[1], mls)):
                    dve.tensor_tensor(w3, each(mp, c0, c1, n_), m3, ALU.subtract)
                    dve.tensor_tensor(s3, g3, l3.to_broadcast([H, c1 - c0, n_]), ALU.subtract)
                    step(dve.tensor_tensor(decay[:, c0:c1].unsqueeze(2), mp[:, c0:c1].unsqueeze(2), l3, ALU.subtract))
                step(dve.tensor_scalar(R["m"], R["m"], -1.0, None, ALU.mult))
                step(dve.tensor_copy(R["li"], R["m"]))
                step(dve.tensor_copy(mend[:], mend[:]))
                for j, job in enumerate(jobs):
                    if job[-1] != "dve":
                        continue
                    dve.wait_ge(s_full, j + 1)
                    bank = ps[j % 8]
                    if job[0] == "k":
                        _, ct, n0, nn, _ = job
                        dve.tensor_scalar(kT[:, ct, n0:n0 + nn], bank[:, 0:nn], biasc[:, BC["k"] + ct:BC["k"] + ct + 1],
                                          float(HD) ** -0.5, ALU.add, ALU.mult).then_inc(s_out_dve, 1)
                    else:
                        t = job[1]
                        dve.tensor_copy(vaug[0:rows(t), t, :, 0:HD],
                                        bank[0:rows(t), :].rearrange("p (h d) -> p h d", h=H)).then_inc(s_out_dve, 1)
                dve.wait_ge(s_rowa, 6)

        rows4 = ("g", "wi", "en", "gm")
        dma = sem("s_cst")
        (s_scores, s_cols, s_colsv, s_dlog, s_e, s_em, s_am, s_nums, s_inter, s_cupd, s_numd, s_ve, s_rs, s_ha,
         s_hps, s_hev, s_dec, s_decv, s_kw, s_kv, s_mlst, s_cout, s_c0) = (
            sem("s_" + x) for x in ("scores", "cols", "colsv", "dlog", "e", "em", "am", "nums", "inter", "cupd", "numd",
                                    "ve", "rs", "ha", "hps", "hev", "dec", "decv", "kw", "kv", "mlst", "cout", "c0"))
        s_mst2 = sem("s_chunk_step")
        s_qm, s_nps, s_nev, s_nin = sem("s_qm"), sem("s_nps"), sem("s_nev"), sem("s_nin")
        with ExitStack() as cw, nc.Block() as block:
            cols = sb("cols", [P, NT, 4, H], c=cw)
            dbc = sb("dbc", [P, H, NCH + NB], c=cw)
            C = sb("C", [P, H, HD + 1], c=cw)
            Cs = sb("Cs", [P, NB, H, HD + 1], c=cw)
            nin = sb("nin", [NB * H, HD], c=cw)
            ncol = sb("ncol", [P, NB * H + H], c=cw)
            nout = sb("nout", [NB * H, 2, HD], c=cw)
            dl = sb("dl", [P, H, P], c=cw)
            ex = hT[:, 10, 0:512].rearrange("p (h t) -> p h t", h=H)
            em = hT[:, 10, 512:1024].rearrange("p (h t) -> p h t", h=H)
            am = sb("am", [P, H, P], c=cw)
            kw = sb("kw", [P, H, HD], c=cw)
            wsb = sb("wsb", [SM, H, NB], c=cw)
            kwb = sb("kwb", [SM, 2, H, HD], c=cw)
            qm = hT[:, 8:10, 0:H * NB * SM // 2].rearrange("p a (c b t) -> p a c b t", b=NB, t=SM)
            inter = sb("inter", [P, H, HD + 1], c=cw)
            num = sb("num", [P, H, HD + 1], c=cw)
            hv = sb("hv", [P, H, HD], c=cw)
            hc = hT[:, 11, 512:1024].rearrange("p (h t) -> p h t", h=H)
            sq = hT[:, 11, 0:512].rearrange("p (h t) -> p h t", h=H)
            ha = hT[:, 5, 0:512].rearrange("p (h t) -> p h t", h=H)
            den = sb("den", [P, H], c=cw)
            mu = sb("mu", [P, H], c=cw)
            ve = sb("ve", [P, H], c=cw)
            rs = sb("rs", [P, H], c=cw)

            def three_and_one(i, T):
                return [ps[3 + i][0:T, 129 * h:129 * h + 129] for h in range(3)] + [ps[6][0:T, 129 * i:129 * i + 129]]

            @block.sync
            def _(sp):
                sp.dma_start(nin[:], a["state_n"][0].rearrange("b h d -> (b h) d")).then_inc(s_nin, 16)
                for b in range(NB):
                    sp.dma_start(Cs[:, b, :, 0:HD], a["state_C"][0, b].rearrange("h k v -> k h v")).then_inc(dma, 16)
                sp.wait_ge(s_cupd, NCH)
                sp.dma_start(out_c[0, 0].rearrange("h k v -> k h v"), C[:, :, 0:HD]).then_inc(s_cout, 16)
                for b in range(NB):
                    sp.wait_ge(s_cupd, NCH + b + 1)
                    sp.dma_start(outs_c[0, b].rearrange("h k v -> k h v"), Cs[:, b, :, 0:HD]).then_inc(s_cout, 16)
                sp.wait_ge(s_nev, 2)
                sp.dma_start(outs_n[0].rearrange("b h d -> (b h) d"), nout[:, 0, :]).then_inc(s_cout, 16)
                sp.dma_start(out_n[0, 0], nout[0:H, 1, :]).then_inc(s_cout, 16)
                sp.wait_ge(s_cout, 16 * (NB + 3))

            @block.tensor
            def _(pe):
                for t in range(NT):
                    for i, name in enumerate(rows4):
                        pe.transpose(ps[7][0:rows(t), (t * 4 + i) * H:(t * 4 + i + 1) * H],
                                     row[name][:, t * P:t * P + rows(t)], ident[0:H, 0:H])
                for h in range(H):
                    pe.matmul(ps[0][:, h * 16:h * 16 + 16], k.pick[:, h, :], decay[:], start=True, stop=True)
                pe.wait_ge(s_nin, 16)
                pe.transpose(ps[1][:, 0:NB * H], nin[:], ident[0:NB * H, 0:NB * H]).then_inc(s_cols, 1)
                pe.wait_ge(s_colsv, 1)
                for c in range(NT):
                    T, c0 = rows(c), c * P
                    if c:
                        pe.wait_ge(s_am, c)
                    for h in range(H):
                        pe.matmul(ps[0][0:T, h * T:(h + 1) * T], k.pick[:, h, 0:T], row["li"][:, c0:c0 + T],
                                  start=True, stop=True)
                    for h in range(H):
                        pe.matmul(ps[1][0:T, h * T:(h + 1) * T], kT[:, h, c0:c0 + T], qT[:, h, c0:c0 + T],
                                  start=True, stop=True)
                    for h in range(H):
                        last = pe.transpose(ps[2][0:T, h * HD:(h + 1) * HD], kT[:, h, c0:c0 + T], ident[:])
                    last.then_inc(s_scores, 1)
                    if c:
                        pe.wait_ge(s_numd, c)
                        pe.wait_ge(s_cupd, c)
                    else:
                        pe.wait_ge(s_c0, 1)
                    it, nt_, kv = (three_and_one(i, T) for i in range(3))
                    if c < NCH:
                        for h in range(H):
                            pe.matmul(it[h], qT[:, h, c0:c0 + T], C[:, h, :], start=True, stop=True)
                    else:
                        pe.wait_ge(s_qm, 1)
                        pe.wait_ge(dma, 16 * NB)
                        for h in range(H):
                            for b in range(NB):
                                pe.matmul(it[h], qm[:, h // 2, h % 2, b, :], Cs[:, b, h, :], start=(b == 0), stop=(b == NB - 1))
                    pe.wait_ge(s_am, c + 1)
                    for h in range(H):
                        last = pe.matmul(nt_[h], am[0:T, h, 0:T], vaug[0:T, c, h, :], start=True, stop=True)
                    if c < NCH:
                        kv = three_and_one(2, P)
                        for h in range(H):
                            last = pe.matmul(kv[h], kw[0:T, h, :], vaug[0:T, c, h, :], start=True, stop=True)
                    last.then_inc(s_nums, 1)
                    pe.wait_ge(s_ha, c + 1)
                    if c:
                        pe.wait_ge(s_hev, c)
                    for h in range(H):
                        last = pe.transpose(ps[7][:, h * T:(h + 1) * T], ha[0:T, h, :], ident[0:T, 0:T])
                    last.then_inc(s_hps, 1)
                for b in range(NB):
                    pe.wait_ge(s_kw, b + 1)
                    if b:
                        pe.wait_ge(s_cupd, NCH + b)
                    else:
                        pe.wait_ge(s_am, NT)
                    for h in range(H):
                        last = pe.matmul(ps[h // 3][:, 129 * (h % 3):129 * (h % 3) + 129], kwb[:, b % 2, h, :],
                                         vaug[0:SM, NT - 1, h, :], start=True, stop=True)
                    last.then_inc(s_kv, 1)
                pe.wait_ge(s_mlst, 1)
                pe.transpose(ps[2][0:NB * H, 0:P], ncol[:, 0:NB * H], ident[:])
                pe.transpose(ps[2][0:H, P:2 * P], ncol[:, NB * H:], ident[:]).then_inc(s_nps, 1)

            @block.scalar
            def _(act):
                for c in range(NT):
                    T, c0 = rows(c), c * P
                    act.wait_ge(s_dlog, c + 1)
                    act.activation(ex[0:T, :, 0:T], dl[0:T, :, 0:T], ACT.Exp).then_inc(s_e, 1)
                    act.wait_ge(s_nums, c + 1)
                    it = three_and_one(0, T)
                    for h in range(H):
                        last = act.activation(inter[0:T, h, :], it[h], ACT.Copy, scale=cols[0:T, c, 1, h:h + 1])
                    last.then_inc(s_inter, 1)
                    act.wait_ge(s_hps, c + 1)
                    act.copy(hT[:, 0:H, c0:c0 + T], ps[7][:, 0:H * T].rearrange("p (h t) -> p h t", h=H)).then_inc(s_hev, 1)

            @block.gpsimd
            def _(pool):
                for c in range(NT):
                    T = rows(c)
                    mask = k.causalT[0:T, 0:T] if c < NCH else k.sampleT[:]
                    pool.wait_ge(s_e, c + 1)
                    pool.tensor_tensor(em[0:T, :, 0:T], ex[0:T, :, 0:T], mask.unsqueeze(1).to_broadcast([T, H, T]),
                                       ALU.mult).then_inc(s_em, 1)
                    pool.wait_ge(s_ve, c + 1)
                    pool.tensor_tensor(rs[0:T, :], ve[0:T, :], k.neghalf[0:T, :], ALU.pow).then_inc(s_rs, 1)

            @block.vector
            def _(dve):
                n = 0

                def step(ins):
                    nonlocal n
                    n += 1
                    ins.then_inc(s_mst2, 1)
                    dve.wait_ge(s_mst2, n)

                dve.memset(C[:], 0.0).then_inc(s_c0, 1)
                dve.wait_ge(s_cols, 1)
                dve.memset(hT[:, 8:10, 0:H * NB * SM // 2], 0.0).then_inc(s_c0, 1)
                dve.wait_ge(s_c0, 2)
                dve.tensor_copy(cols[:, 0:NCH], ps[7][:, 0:NCH * 16].rearrange("p (c i h) -> p c i h", c=NCH, i=4))
                dve.tensor_copy(cols[0:SM, NCH], ps[7][0:SM, NCH * 16:NT * 16].rearrange("p (i h) -> p i h", i=4))
                dve.tensor_copy(dbc[:], ps[0][:, 0:64].rearrange("p (h c) -> p h c", h=H))
                for h in range(H):
                    for b in range(NB):
                        dve.tensor_copy(qm[:, h // 2, h % 2, b, NS * b:NS * b + NS], qT[:, h, SEQ + NS * b:SEQ + NS * b + NS])
                step(dve.tensor_copy(Cs[:, :, :, HD:HD + 1],
                                     ps[1][:, 0:NB * H].rearrange("p (b h o) -> p b h o", b=NB, o=1)))
                dve.tensor_tensor(wsb[:], cols[0:SM, NCH, 3, :].unsqueeze(2).to_broadcast([SM, H, NB]),
                                  k.own[:].unsqueeze(1).to_broadcast([SM, H, NB]), ALU.mult).then_inc(s_qm, 1)
                dve.wait_ge(s_qm, 1)
                dve.sem_inc(s_colsv, 1)
                for c in range(NT):
                    T = rows(c)
                    dve.wait_ge(s_scores, c + 1)
                    for h in range(H):
                        last = dve.tensor_scalar(dl[0:T, h, 0:T], ps[0][0:T, h * T:(h + 1) * T],
                                                 cols[0:T, c, 0, h:h + 1], 0.0, ALU.add, ALU.min)
                    last.then_inc(s_dlog, 1)
                    if c < NCH:
                        for h in range(H):
                            dve.tensor_scalar(kw[0:T, h, :], ps[2][0:T, h * HD:(h + 1) * HD], cols[0:T, c, 3, h:h + 1],
                                              None, ALU.mult)
                    else:
                        dve.tensor_copy(kw[0:T], ps[2][0:T, :].rearrange("p (h d) -> p h d", h=H))
                    dve.wait_ge(s_em, c + 1)
                    dve.tensor_tensor(am[0:T, :, 0:T], em[0:T, :, 0:T],
                                      ps[1][0:T, 0:H * T].rearrange("p (h t) -> p h t", h=H), ALU.mult).then_inc(s_am, 1)
                    dve.wait_ge(s_inter, c + 1)
                    if c < NCH:
                        kv = three_and_one(2, P)
                        for h in range(H):
                            last = dve.scalar_tensor_tensor(C[:, h, :], C[:, h, :], dbc[:, h, c:c + 1], kv[h],
                                                            ALU.mult, ALU.add)
                        last.then_inc(s_cupd, 1)
                    dve.tensor_tensor(num[0:T, 0:3, :], inter[0:T, 0:3, :],
                                      ps[4][0:T, 0:387].rearrange("p (h d) -> p h d", h=3), ALU.add)
                    step(dve.tensor_tensor(num[0:T, 3, :], inter[0:T, 3, :], ps[6][0:T, 129:258], ALU.add))
                    dsum = num[0:T, :, HD:HD + 1].rearrange("p h o -> p (h o)")
                    step(dve.scalar_tensor_tensor(den[0:T, :], dsum, -1.0, dsum, ALU.mult, ALU.max))
                    dve.sem_inc(s_numd, 1)
                    step(dve.tensor_tensor(den[0:T, :], den[0:T, :], cols[0:T, c, 2, :], ALU.max))
                    step(dve.reciprocal(den[0:T, :], den[0:T, :]))
                    step(dve.tensor_tensor(hv[0:T], num[0:T, :, 0:HD],
                                           den[0:T, :].unsqueeze(2).to_broadcast([T, H, HD]), ALU.mult))
                    step(dve.tensor_reduce(mu[0:T, :], hv[0:T], AX, ALU.add))
                    step(dve.tensor_scalar(mu[0:T, :], mu[0:T, :], 1.0 / HD, None, ALU.mult))
                    step(dve.tensor_tensor(hc[0:T], hv[0:T], mu[0:T, :].unsqueeze(2).to_broadcast([T, H, HD]),
                                           ALU.subtract))
                    step(dve.tensor_tensor(sq[0:T], hc[0:T], hc[0:T], ALU.mult))
                    step(dve.tensor_reduce(ve[0:T, :], sq[0:T], AX, ALU.add))
                    if c:
                        dve.wait_ge(s_hps, c)
                    dve.tensor_scalar(ve[0:T, :], ve[0:T, :], 1.0 / HD, EPS, ALU.mult, ALU.add).then_inc(s_ve, 1)
                    step(dve.tensor_tensor(hc[0:T], hc[0:T], gate_o[0:T, c, :].rearrange("p (h d) -> p h d", h=H),
                                           ALU.mult))
                    dve.wait_ge(s_rs, c + 1)
                    dve.tensor_tensor(ha[0:T], hc[0:T], rs[0:T, :].unsqueeze(2).to_broadcast([T, H, HD]),
                                      ALU.mult).then_inc(s_ha, 1)
                for b in range(NB):
                    if b >= 2:
                        dve.wait_ge(s_kv, b - 1)
                    for h in range(H):
                        last = dve.tensor_scalar(kwb[:, b % 2, h, :], kw[0:SM, h, :], wsb[:, h, b:b + 1], None, ALU.mult)
                    last.then_inc(s_kw, 1)
                    dve.wait_ge(s_kv, b + 1)
                    for h in range(H):
                        last = dve.scalar_tensor_tensor(Cs[:, b, h, :], Cs[:, b, h, :], dbc[:, h, NCH + b:NCH + b + 1],
                                                        ps[h // 3][:, 129 * (h % 3):129 * (h % 3) + 129],
                                                        ALU.mult, ALU.add)
                    last.then_inc(s_cupd, 1)
                dve.wait_ge(s_cupd, NCH + NB)
                dve.tensor_copy(ncol[:, 0:NB * H].rearrange("p (b h o) -> p b h o", b=NB, o=1), Cs[:, :, :, HD:HD + 1])
                dve.tensor_copy(ncol[:, NB * H:].unsqueeze(2), C[:, :, HD:HD + 1]).then_inc(s_mlst, 1)
                dve.wait_ge(s_nps, 1)
                dve.tensor_copy(nout[:, 0, :], ps[2][0:NB * H, 0:P]).then_inc(s_nev, 1)
                dve.tensor_copy(nout[0:H, 1, :], ps[2][0:H, P:2 * P]).then_inc(s_nev, 1)


TK = {"ik": 0, "iw": 64, "k": 72, "v": 200}
TKW = 328


def build_attention(nc, a, k):
    ps, banks, ident, ones, xT, hT, biasc, biasr, sem = (k.ps, k.banks, k.ident, k.ones, k.xT, k.hT, k.biasc, k.biasr,
                                                        k.sem)
    with ExitStack() as ca:
        def sb(name, shape, dt=F32, c=ca):
            return k.sb(name, shape, dt, c)

        bqT = sb("bqT", [P, 4, N])
        iqT = sb("iqT", [P, 4, N])
        bkT = sb("bkT", [P, N])
        ikT = sb("ikT", [P, N])
        tok = sb("tok", [P, NT, TKW])

        jobs = [("tok", t, ("act", "dve")[t % 2]) for t in range(NT)]
        for name, cts in (("bk", 1), ("ik", 1), ("iq", 4), ("bq", 4)):
            jobs += [(name, ct, n0, nn, ("act", "dve")[(ct + (n0 > 0)) % 2]) for ct in range(cts)
                     for n0, nn in TOKEN_CHUNKS]
        dest = {"bk": lambda ct: bkT, "ik": lambda ct: ikT, "iq": lambda ct: iqT[:, ct], "bq": lambda ct: bqT[:, ct]}
        s_wk, s_wiq, s_wbq = sem("s_wk"), sem("s_wiq"), sem("s_wbq")
        s_full, s_out_act, s_out_dve, s_kvout = (sem("s_keys_" + x) for x in ("full", "out_act", "out_dve", "kvout"))
        with ExitStack() as cw, nc.Block() as block:
            wk = sb("w_keys", [P, KT, 64 + TKW], c=cw)
            wiq = sb("w_iq", [P, KT, 512], c=cw)
            wbq = sb("w_bq", [P, KT, 4, 2, BD], c=cw)

            @block.sync
            def _(sp):
                sp.dma_start(wk[:, :, 0:64], k.w_in[:, :, OFF["ik"]:OFF["ik"] + 64]).then_inc(s_wk, 16)
                sp.dma_start(wk[:, :, 64:136], k.w_in[:, :, OFF["ik"]:OFF["ik"] + 72]).then_inc(s_wk, 16)
                sp.dma_start(wk[:, :, 136:392], k.w_in[:, :, OFF["bk"]:OFF["bk"] + 256]).then_inc(s_wk, 16)
                sp.dma_start(wiq[:], k.w_in[:, :, OFF["iq"]:OFF["iq"] + 512]).then_inc(s_wiq, 16)
                for g in range(BKV):
                    for j in range(4):
                        at = OFF["bq"] + (4 * g + j) * BD
                        sp.dma_start(wbq[:, :, j, g, :], k.w_in[:, :, at:at + BD]).then_inc(s_wbq, 16)
                sp.wait_ge(s_out_act, banks_before(jobs, "act", NT))
                sp.wait_ge(s_out_dve, banks_before(jobs, "dve", NT))
                for out, name, w in (("kidx", "ik", BD), ("k", "k", 128), ("v", "v", 128)):
                    dst = a[out + "_prompt"][0, 0]
                    dst = dst if name == "ik" else dst.rearrange("t h d -> t (h d)")
                    sp.dma_start(dst.rearrange("(t p) c -> p t c", p=P),
                                 tok[:, 0:NCH, TK[name]:TK[name] + w]).then_inc(s_kvout, 16)
                    dst = a[out + "_sample"][0]
                    dst = dst.rearrange("b t c -> (b t) c" if name == "ik" else "b t h d -> (b t) (h d)")
                    sp.dma_start(dst, tok[0:SM, NCH, TK[name]:TK[name] + w]).then_inc(s_kvout, 16)
                sp.wait_ge(s_kvout, 16 * 6)

            @block.tensor
            def _(pe):
                for j, job in enumerate(jobs):
                    if j >= 8:
                        eng = jobs[j - 8][-1]
                        pe.wait_ge({"act": s_out_act, "dve": s_out_dve}[eng], banks_before(jobs, eng, j - 7))
                    if job[0] == "tok":
                        t = job[1]
                        if t == 0:
                            pe.wait_ge(s_wk, 48)
                        last = product(pe, ps[j % 8][0:rows(t), 0:TKW], P,
                                       lambda kt: xT[:, kt, t * P:t * P + rows(t)], lambda kt: wk[:, kt, 64:64 + TKW],
                                       KT, (ones[0:1, 0:rows(t)], biasr[:, 1024:1024 + TKW]))
                    else:
                        name, ct, n0, nn, _ = job
                        if name in ("iq", "bq") and ct == 0 and n0 == 0:
                            pe.wait_ge(s_wiq if name == "iq" else s_wbq, 16 if name == "iq" else 128)
                        left = {"bk": lambda kt: wk[:, kt, 136:264], "ik": lambda kt: wk[:, kt, 0:128],
                                "iq": lambda kt: wiq[:, kt, ct * P:(ct + 1) * P],
                                "bq": lambda kt: wbq[:, kt, ct, :, :].rearrange("p g d -> p (g d)")}[name]
                        last = product(pe, ps[j % 8][:, 0:nn], P, left, lambda kt: xT[:, kt, n0:n0 + nn], KT)
                    last.then_inc(s_full, 1)

            @block.scalar
            def _(act):
                for j, job in enumerate(jobs):
                    if job[-1] == "act":
                        act.wait_ge(s_full, j + 1)
                        if job[0] == "tok":
                            r, t = rows(job[1]), job[1]
                            act.copy(tok[0:r, t, :], ps[j % 8][0:r, 0:TKW]).then_inc(s_out_act, 1)
                        else:
                            name, ct, n0, nn, _ = job
                            act.activation(dest[name](ct)[:, n0:n0 + nn], ps[j % 8][:, 0:nn], ACT.Identity,
                                           bias=biasc[:, BC[name] + ct:BC[name] + ct + 1]).then_inc(s_out_act, 1)

            @block.vector
            def _(dve):
                for j, job in enumerate(jobs):
                    if job[-1] == "dve":
                        dve.wait_ge(s_full, j + 1)
                        if job[0] == "tok":
                            r, t = rows(job[1]), job[1]
                            dve.tensor_copy(tok[0:r, t, :], ps[j % 8][0:r, 0:TKW]).then_inc(s_out_dve, 1)
                        else:
                            name, ct, n0, nn, _ = job
                            dve.tensor_scalar(dest[name](ct)[:, n0:n0 + nn], ps[j % 8][:, 0:nn],
                                              biasc[:, BC[name] + ct:BC[name] + ct + 1], None, ALU.add).then_inc(s_out_dve, 1)

        attend_prompt(nc, a, k, sb, bqT, iqT, bkT, ikT, tok)
        attend_samples(nc, a, k, sb, bqT, iqT, bkT, ikT, tok)


def keep_best(dve, s_best, base, work, best):
    for r in range(KEEP // 8):
        dve.max(best, work).then_inc(s_best, 1)
        dve.wait_ge(s_best, base + 2 * r + 1)
        dve.match_replace(work, best, work, GONE).then_inc(s_best, 1)
        dve.wait_ge(s_best, base + 2 * r + 2)


def attend_prompt(nc, a, k, sb, bqT, iqT, bkT, ikT, tok):
    ps, banks, ident, hT, sem = k.ps, k.banks, k.ident, k.hT, k.sem
    units = [(kind, i, h) for i in range(NCH) for kind in (("dots", "logits") if i >= 2 else ("logits",))
             for h in range(8)]
    taker = {"dots": "act", "logits": "dve"}
    at = {u: n for n, u in enumerate(units)}

    def taken(n, eng):
        return sum(taker[u[0]] == eng for u in units[:n])

    halves = [(i, h, q) for i in range(NCH) for h in range(8) for q in range(-(-(i + 1) // 4))]
    half_at = {x: n for n, x in enumerate(halves)}
    (s_wide, s_wide_act, s_wide_dve, s_acc, s_pen, s_mx, s_ex, s_pn, s_tp, s_pt, s_pv, s_hb, s_best, s_st, s_cst) = (
        sem("s_prompt_" + x) for x in ("wide", "wide_act", "wide_dve", "acc", "pen", "mx", "ex", "pn", "tp", "pt", "pv", "hb",
                                 "best", "st", "cst"))
    with ExitStack() as cw, nc.Block() as block:
        PT = sb("PT", [P, 2, NCH, 4 * P], c=cw)
        rl = sb("rl", [P, 2, SEQ], c=cw)
        lg = sb("lg", [P, 2, SEQ], c=cw)
        score = sb("score", [P, SEQ], c=cw)
        pen = sb("pen", [P, SEQ], c=cw)
        penc = sb("penc", [P, P], c=cw)
        wis = sb("wis", [P, NCH, 8], c=cw)
        best = sb("best", [P, 8], c=cw)
        mx = sb("mx", [P, 2], c=cw)
        nm = sb("nm", [P, 2], c=cw)
        sm = sb("sm", [P, 2], c=cw)
        rc = sb("rc", [P, 2], c=cw)

        def wide(u, L):
            b = 2 * (at[u] % 2)
            return banks[:, b:b + 2, :].rearrange("p b n -> p (b n)")[:, 0:L]

        @block.gpsimd
        def _(pool):
            pool.memset(penc[:], 0.0).then_inc(s_cst, 1)
            pool.wait_ge(s_cst, 1)
            pool.affine_select(out=penc[:], in_=penc[:], compare_op=ALU.is_ge, fill=-BIG, base=0, pattern=[[-1, P]],
                               channel_multiplier=1).then_inc(s_cst, 1)

        @block.tensor
        def _(pe):
            def wide_product(u):
                kind, i, h = u
                n, L = at[u], (i + 1) * P
                if n >= 2:
                    eng = taker[units[n - 2][0]]
                    pe.wait_ge({"act": s_wide_act, "dve": s_wide_dve}[eng], taken(n - 1, eng))
                q, keys = (iqT, ikT) if kind == "dots" else (bqT, bkT)
                g, j = (h % 2, h // 2) if kind == "dots" else (h // 4, h % 4)
                for n0 in range(0, L, 512):
                    nn = min(512, L - n0)
                    last = pe.matmul(banks[:, 2 * (n % 2) + n0 // 512, 0:nn], q[64 * g:64 * g + 64, j, i * P:(i + 1) * P],
                                     keys[64 * g:64 * g + 64, n0:n0 + nn], start=True, stop=True)
                last.then_inc(s_wide, 1)

            def turn(i, h):
                u = 8 * i + h
                pe.wait_ge(s_pn, u + 1)
                for q in range(-(-(i + 1) // 4)):
                    v = half_at[i, h, q]
                    if v >= 2:
                        pe.wait_ge(s_pt, v - 1)
                    for t in range(4 * q, min(4 * q + 4, i + 1)):
                        last = pe.transpose(ps[4 + v % 2][:, (t % 4) * P:(t % 4 + 1) * P],
                                            lg[:, u % 2, t * P:(t + 1) * P], ident[:])
                    last.then_inc(s_tp, 1)

            def mix(i, g):
                n = 2 * i + g
                pe.wait_ge(s_pt, half_at[i, 4 * g + 3, -(-(i + 1) // 4) - 1] + 1)
                if n >= 2:
                    pe.wait_ge(s_hb, n - 1)
                for t in range(i + 1):
                    last = pe.matmul(ps[6 + g], tok[:, t, TK["v"]:TK["v"] + P], PT[:, g, t, :],
                                     start=(t == 0), stop=(t == i))
                last.then_inc(s_pv, 1)

            for i in range(NCH):
                if i >= 2:
                    for h in range(8):
                        wide_product(("dots", i, h))
                wide_product(("logits", i, 0))
                for h in range(8):
                    if h < 7:
                        wide_product(("logits", i, h + 1))
                    turn(i, h)
                    if h == 4:
                        mix(i, 0)
                mix(i, 1)

        @block.scalar
        def _(act):
            def relu(i, h):
                n = 8 * (i - 2) + h
                act.wait_ge(s_wide, at["dots", i, h] + 1)
                if n >= 2:
                    act.wait_ge(s_acc, n - 1)
                act.activation(rl[:, n % 2, 0:(i + 1) * P], wide(("dots", i, h), (i + 1) * P), ACT.Relu,
                               scale=float(BD) ** -0.5).then_inc(s_wide_act, 1)

            def exps(i, h):
                u = 8 * i + h
                act.wait_ge(s_mx, u + 1)
                x = lg[:, u % 2, 0:(i + 1) * P]
                act.activation(x, x, ACT.Exp, bias=nm[:, u % 2:u % 2 + 1], scale=float(BD) ** -0.5,
                               accum_out=sm[:, u % 2:u % 2 + 1]).then_inc(s_ex, 1)

            def spread(i, h):
                for q in range(-(-(i + 1) // 4)):
                    v = half_at[i, h, q]
                    act.wait_ge(s_tp, v + 1)
                    if q == 0 and h % 4 == 0 and i > 0:
                        act.wait_ge(s_pv, 2 * (i - 1) + h // 4 + 1)
                    c = min(4, i + 1 - 4 * q)
                    act.copy(PT[:, h // 4, 4 * q:4 * q + c, (h % 4) * P:(h % 4 + 1) * P],
                             ps[4 + v % 2][:, 0:c * P].rearrange("p (t n) -> p t n", t=c)).then_inc(s_pt, 1)

            def result(i, g):
                act.wait_ge(s_pv, 2 * i + g + 1)
                act.copy(hT[64 * g:64 * g + 64, 4:8, i * P:(i + 1) * P],
                         ps[6 + g][64 * g:64 * g + 64, :].rearrange("p (j q) -> p j q", j=4)).then_inc(s_hb, 1)

            for i in range(NCH):
                if i >= 2:
                    for h in range(8):
                        relu(i, h)
                exps(i, 0)
                for h in range(8):
                    if h < 7:
                        exps(i, h + 1)
                    spread(i, h)
                    if h == 5:
                        result(i, 0)
                result(i, 1)

        @block.vector
        def _(dve):
            n = 0

            def step(ins):
                nonlocal n
                n += 1
                ins.then_inc(s_st, 1)
                dve.wait_ge(s_st, n)

            dve.wait_ge(s_cst, 2)
            step(dve.tensor_scalar(wis[:], tok[:, 0:NCH, TK["iw"]:TK["iw"] + 8], 8.0 ** -0.5, None, ALU.mult))

            def maximum(i, h):
                u, L = 8 * i + h, (i + 1) * P
                dve.wait_ge(s_wide, at["logits", i, h] + 1)
                if u >= 2:
                    i2, h2 = divmod(u - 2, 8)
                    dve.wait_ge(s_tp, half_at[i2, h2, -(-(i2 + 1) // 4) - 1] + 1)
                s = u % 2
                dve.tensor_tensor_reduce(lg[:, s, 0:L], wide(("logits", i, h), L), pen[:, 0:L], 1.0, GONE, ALU.add,
                                         ALU.max, mx[:, s:s + 1]).then_inc(s_wide_dve, 1)
                dve.wait_ge(s_wide_dve, u + 1)
                dve.tensor_scalar(nm[:, s:s + 1], mx[:, s:s + 1], -float(BD) ** -0.5, None, ALU.mult).then_inc(s_mx, 1)

            def scale(i, h):
                u, L = 8 * i + h, (i + 1) * P
                s = u % 2
                dve.wait_ge(s_ex, u + 1)
                step(dve.reciprocal(rc[:, s:s + 1], sm[:, s:s + 1]))
                dve.tensor_scalar(lg[:, s, 0:L], lg[:, s, 0:L], rc[:, s:s + 1], None, ALU.mult).then_inc(s_pn, 1)

            for i in range(NCH):
                L = (i + 1) * P
                if i >= 2:
                    for h in range(8):
                        m = 8 * (i - 2) + h
                        dve.wait_ge(s_wide_act, m + 1)
                        x, w = rl[:, m % 2, 0:L], wis[:, i, h:h + 1]
                        if h == 0:
                            dve.tensor_scalar(score[:, 0:L], x, w, None, ALU.mult).then_inc(s_acc, 1)
                        else:
                            dve.scalar_tensor_tensor(score[:, 0:L], x, w, score[:, 0:L], ALU.mult,
                                                     ALU.add).then_inc(s_acc, 1)
                        dve.wait_ge(s_acc, m + 1)
                    step(dve.tensor_tensor(score[:, i * P:L], score[:, i * P:L], penc[:], ALU.add))
                    keep_best(dve, s_best, (i - 2) * KEEP // 4, score[:, 0:L], best[:])
                    step(dve.tensor_scalar(score[:, 0:L], score[:, 0:L], GONE, 1.0, ALU.is_equal, ALU.subtract))
                    step(dve.tensor_scalar(pen[:, 0:L], score[:, 0:L], BIG, None, ALU.mult))
                else:
                    step(dve.memset(pen[:, 0:L], 0.0))
                    step(dve.tensor_copy(pen[:, i * P:L], penc[:]))
                maximum(i, 0)
                for h in range(8):
                    if h < 7:
                        maximum(i, h + 1)
                    scale(i, h)


def attend_samples(nc, a, k, sb, bqT, iqT, bkT, ikT, tok):
    ps, banks, ident, hT, sem = k.ps, k.banks, k.ident, k.hT, k.sem
    KC = NPG
    (s_pt, s_ixc, s_idx, s_kd, s_vd, s_id, s_dup, s_z, s_zz, s_tr, s_tre, s_dot, s_rel, s_sc, s_best, s_st, s_sel, s_mx,
     s_ex, s_pn, s_tp, s_tpe, s_pv, s_hb, s_wc, s_lgt) = (
        sem("s_sample_" + x) for x in ("pt", "ixc", "idx", "kd", "vd", "id", "dup", "z", "zz", "tr", "tre", "dot", "rel", "sc",
                                 "best", "st", "sel", "mx", "ex", "pn", "tp", "tpe", "pv", "hb", "wc", "lgt"))
    s_idl = [sem(f"s_idl{i}") for i in range(2)]
    s_kdl = [sem(f"s_kdl{i}") for i in range(2)]
    s_vdl = [sem(f"s_vdl{i}") for i in range(2)]
    with ExitStack() as cw, nc.Block() as block:
        page = sb("page", [P, NB], I32, cw)
        lane = sb("lane", [P, 1], I32, cw)
        where = sb("where", [P, NB], I32, cw)
        ic = sb("ic", [P, 2, KC * BD], c=cw)
        icd = hT[:, 8, 0:KC * P].rearrange("p (t g d) -> p t g d", t=KC, g=2)
        kc = sb("kc", [P, 2, KC * P], c=cw)
        vc = hT[:, 10:12, 0:KC * P]
        keysT = sb("keysT", [P, PAST], c=cw)
        dq = sb("dq", [SM, NS], c=cw)
        iqz = sb("iqz", [P, NB, 2, 4, NS], c=cw)
        bqz = sb("bqz", [P, NB, 2, 4, NS], c=cw)
        lw = sb("lw", [SM, 2, 4, NS], c=cw)
        wcol = sb("wcol", [SM, NB], c=cw)
        wsum = sb("wsum", [SM, NB * (SM + NS)], c=cw)
        tell = sb("tell", [SM, NB, 8, NS], c=cw)
        rl = sb("srl", [SM, 2, NK], c=cw)
        sc = sb("ssc", [SM, NK], c=cw)
        pen = sb("spen", [SM, NK], c=cw)
        best = sb("sbest", [SM, 8], c=cw)
        pr = sb("pr", [SM, NK], c=cw)
        prT = hT[:, 9, 0:(KC + 1) * SM].rearrange("p (t n) -> p t n", n=SM)
        mx = sb("smx", [SM, 4], c=cw)

        @block.sync
        def _(sp):
            for g in range(NPG):
                sp.dma_start(page[16 * g:16 * g + 16, :],
                             a["page_table"][:, g:g + 1].rearrange("b o -> o b").broadcast_to([16, NB])).then_inc(s_pt, 16)

        @block.gpsimd
        def _(pool):
            pool.iota(lane[:], pattern=[[0, 1]], base=0, channel_multiplier=1).then_inc(s_ixc, 1)
            pool.wait_ge(s_idx, 1)

            def fetch(dst, src, b, s):
                pool.indirect_dma_start(dst, None, src, bass.IndirectOffsetOnAxis(ap=where[:, b:b + 1], axis=0)).then_inc(s, 16)

            views = [a["cache_kidx"][0].rearrange("n (r e) d -> (n r) (e d)", e=8),
                     a["cache_k"][0].rearrange("n (r e) h d -> (n r) (e h d)", e=8),
                     a["cache_v"][0].rearrange("n (r e) h d -> (n r) (e h d)", e=8)]
            for b in range(NB):
                if b >= 2:
                    pool.wait_ge(s_dup, b - 1)
                fetch(ic[:, b % 2, :], views[0], b, s_idl[b % 2])
            for b in range(NB):
                if b >= 2:
                    pool.wait_ge(s_tr, NB + b - 1)
                fetch(kc[:, b % 2, :], views[1], b, s_kdl[b % 2])
                if b >= 2:
                    pool.wait_ge(s_pv, b - 1)
                fetch(vc[:, b % 2, :], views[2], b, s_vdl[b % 2])
            for s in s_idl + s_kdl + s_vdl:
                pool.wait_ge(s, 16 * NB // 2)

        def new_keys(keys):
            return keys[:, SEQ:N]

        @block.tensor
        def _(pe):
            def turn_keys(n, src):
                if n:
                    pe.wait_ge(s_tre, n)
                for t in range(KC):
                    last = pe.transpose(ps[6 + t // 4][:, (t % 4) * P:(t % 4 + 1) * P], src(t), ident[:])
                last.then_inc(s_tr, 1)

            def against_keys(left, new, first, start, stop):
                for i in range(2):
                    last = pe.matmul(ps[first + i][0:SM, :], left, keysT[:, 512 * i:512 * i + 512], start=start, stop=stop)
                return pe.matmul(ps[first + 2][0:SM, 0:SM], left, new, start=start, stop=stop)

            def columns(b, i):
                return (512 * i, 512) if i < 2 else (PAST, SM)

            pe.wait_ge(s_z, 1)
            pe.matmul(ps[5][0:SM, 0:NB], lw[:].rearrange("p g j q -> p (g j q)"), k.own[:], start=True,
                      stop=True).then_inc(s_wc, 1)
            pe.wait_ge(s_zz, 1)
            for b in range(NB):
                pe.wait_ge(s_dup, b + 1)
                turn_keys(b, lambda t: icd[:, t, :, :].rearrange("p g d -> p (g d)"))
                pe.wait_ge(s_tre, b + 1)
                if b:
                    pe.wait_ge(s_rel, b)
                against_keys(iqz[:, b].rearrange("p g j q -> p (g j q)"), new_keys(ikT), 0, True, True).then_inc(s_dot, 1)
                pe.wait_ge(s_rel, b + 1)
                for i in range(3):
                    c0, cn = columns(b, i)
                    last = pe.matmul(ps[3 + i][0:SM, 0:cn], wsum[:, b * SM:(b + 1) * SM], rl[:, b % 2, c0:c0 + cn],
                                     start=(b == 0), stop=(b == NB - 1))
                last.then_inc(s_sc, 1)
            for b in range(NB):
                pe.wait_ge(s_kdl[b % 2], 16 * (b // 2 + 1))
                turn_keys(NB + b, lambda t: kc[:, b % 2, t * P:(t + 1) * P])
                pe.wait_ge(s_tre, NB + b + 1)
                if b:
                    pe.wait_ge(s_ex, b)
                pe.wait_ge(s_sel, 1)
                left = bqz[:, b].rearrange("p g j q -> p (g j q)")
                against_keys(left, new_keys(bkT), 0, True, False)
                for i in range(3):
                    c0, cn = columns(b, i)
                    last = pe.matmul(ps[i][0:SM, 0:cn], tell[:, b].rearrange("p h q -> p (h q)"), pen[:, c0:c0 + cn],
                                     start=False, stop=True)
                last.then_inc(s_lgt, 1)
                pe.wait_ge(s_pn, b + 1)
                if b:
                    pe.wait_ge(s_tpe, b)
                for t in range(KC):
                    pe.transpose(ps[3][:, t * SM:(t + 1) * SM], pr[:, t * P:(t + 1) * P], ident[0:SM, 0:SM])
                pe.transpose(ps[4][0:SM, 0:SM], pr[:, PAST:NK], ident[0:SM, 0:SM]).then_inc(s_tp, 1)
                pe.wait_ge(s_tpe, b + 1)
                pe.wait_ge(s_vdl[b % 2], 16 * (b // 2 + 1))
                if b:
                    pe.wait_ge(s_hb, b)
                for t in range(KC):
                    pe.matmul(ps[5][:, 0:SM], vc[:, b % 2, t * P:(t + 1) * P], prT[:, t, :], start=(t == 0), stop=False)
                pe.matmul(ps[5][:, 0:SM], tok[0:SM, NCH, TK["v"]:TK["v"] + P], prT[0:SM, KC, :], start=False,
                          stop=True).then_inc(s_pv, 1)

        @block.scalar
        def _(act):
            for b in range(NB):
                act.wait_ge(s_tr, b + 1)
                if b:
                    act.wait_ge(s_dot, b)
                act.copy(keysT[:], banks[:, 6:8, :].rearrange("p b n -> p (b n)")).then_inc(s_tre, 1)
                act.wait_ge(s_dot, b + 1)
                if b >= 2:
                    act.wait_ge(s_sc, b - 1)
                act.activation(rl[:, b % 2, :], banks[0:SM, 0:3, :].rearrange("p b n -> p (b n)")[:, 0:NK], ACT.Relu,
                               scale=float(BD) ** -0.5).then_inc(s_rel, 1)
            for b in range(NB):
                act.wait_ge(s_tr, NB + b + 1)
                act.wait_ge(s_dot, NB)
                if b:
                    act.wait_ge(s_lgt, b)
                act.copy(keysT[:], banks[:, 6:8, :].rearrange("p b n -> p (b n)")).then_inc(s_tre, 1)
                act.wait_ge(s_mx, b + 1)
                if b:
                    act.wait_ge(s_tp, b)
                act.activation(pr[:], banks[0:SM, 0:3, :].rearrange("p b n -> p (b n)")[:, 0:NK], ACT.Exp,
                               bias=mx[:, 1:2], scale=float(BD) ** -0.5, accum_out=mx[:, 2:3]).then_inc(s_ex, 1)

        @block.vector
        def _(dve):
            n = 0

            def step(ins):
                nonlocal n
                n += 1
                ins.then_inc(s_st, 1)
                dve.wait_ge(s_st, n)

            dve.wait_ge(s_ixc, 1)
            dve.wait_ge(s_pt, 16 * NPG)
            dve.tensor_scalar(lane[:], lane[:], 15, None, ALU.bitwise_and)
            step(dve.tensor_scalar(where[:], page[:], 16.0, None, ALU.mult))
            dve.tensor_tensor(where[:], where[:], lane[:].to_broadcast([P, NB]), ALU.add).then_inc(s_idx, 1)
            dve.memset(iqz[:], 0.0)
            dve.memset(wsum[:], 0.0)
            dve.memset(bqz[:], 0.0)
            step(dve.tensor_reduce(dq[:], ident[0:SM, 0:SM].rearrange("p (b q) -> p q b", b=NB), AX, ALU.add))
            dve.tensor_tensor(lw[:], tok[0:SM, NCH, TK["iw"]:TK["iw"] + 8].rearrange("p (j g) -> p g j", g=2)
                              .unsqueeze(3).to_broadcast([SM, 2, 4, NS]),
                              dq[:].unsqueeze(1).unsqueeze(1).to_broadcast([SM, 2, 4, NS]), ALU.mult).then_inc(s_z, 1)
            dve.tensor_tensor(tell[:], k.own[:].unsqueeze(2).unsqueeze(3).to_broadcast([SM, NB, 8, NS]),
                              dq[:].unsqueeze(1).unsqueeze(1).to_broadcast([SM, NB, 8, NS]), ALU.mult)
            for z, q in ((iqz, iqT), (bqz, bqT)):
                for g in range(2):
                    for j in range(4):
                        dve.tensor_copy(z[64 * g:64 * g + 64, :, g, j, :],
                                        q[64 * g:64 * g + 64, j, SEQ:N].rearrange("p (b q) -> p b q", b=NB))
            dve.wait_ge(s_wc, 1)
            step(dve.tensor_scalar(wcol[:], ps[5][0:SM, 0:NB], 8.0 ** -0.5, None, ALU.mult))
            step(dve.tensor_tensor(wsum[:].rearrange("p (b s) -> p b s", s=SM + NS)[:, :, 0:NS],
                                   wcol[:].unsqueeze(2).to_broadcast([SM, NB, NS]),
                                   dq[:].unsqueeze(1).to_broadcast([SM, NB, NS]), ALU.mult))
            step(dve.tensor_scalar(tell[:], tell[:], BIG, None, ALU.mult))
            dve.sem_inc(s_zz, 1)
            for b in range(NB):
                dve.wait_ge(s_idl[b % 2], 16 * (b // 2 + 1))
                if b:
                    dve.wait_ge(s_tr, b)
                for g in range(2):
                    last = dve.tensor_copy(icd[:, :, g, :], ic[:, b % 2, :].rearrange("p (t d) -> p t d", t=KC))
                last.then_inc(s_dup, 1)
            dve.wait_ge(s_sc, NB)
            dve.tensor_copy(sc[:, 0:PAST].rearrange("p (e t) -> p t e", t=KC),
                            banks[0:SM, 3:5, :].rearrange("p b (t e) -> p (b t) e", e=P))
            step(dve.tensor_scalar(pen[:, PAST:NK], k.sampleQ[:], 1.0, BIG, ALU.subtract, ALU.mult))
            step(dve.tensor_tensor(sc[:, PAST:NK], ps[5][0:SM, 0:SM], pen[:, PAST:NK], ALU.add))
            keep_best(dve, s_best, 0, sc[:], best[:])
            dve.tensor_scalar(pen[:, 0:PAST].rearrange("p (t e) -> p t e", e=P),
                              sc[:, 0:PAST].rearrange("p (e t) -> p t e", t=KC), GONE, 1.0, ALU.is_equal, ALU.subtract)
            dve.tensor_scalar(pen[:, PAST:NK], sc[:, PAST:NK], GONE, 1.0, ALU.is_equal, ALU.subtract).then_inc(s_sel, 1)
            for b in range(NB):
                dve.wait_ge(s_lgt, b + 1)
                if b:
                    dve.wait_ge(s_ex, b)
                step(dve.tensor_reduce(mx[:, 0:1], banks[0:SM, 0:3, :].rearrange("p b n -> p (b n)")[:, 0:NK], AX, ALU.max))
                dve.tensor_scalar(mx[:, 1:2], mx[:, 0:1], -float(BD) ** -0.5, None, ALU.mult).then_inc(s_mx, 1)
                dve.wait_ge(s_ex, b + 1)
                step(dve.reciprocal(mx[:, 3:4], mx[:, 2:3]))
                dve.tensor_scalar(pr[:], pr[:], mx[:, 3:4], None, ALU.mult).then_inc(s_pn, 1)
                dve.wait_ge(s_tp, b + 1)
                if b:
                    dve.wait_ge(s_pv, b)
                dve.tensor_copy(prT[:, 0:KC, :], ps[3][:].rearrange("p (t n) -> p t n", t=KC))
                dve.tensor_copy(prT[0:SM, KC, :], ps[4][0:SM, 0:SM]).then_inc(s_tpe, 1)
                dve.wait_ge(s_pv, b + 1)
                for g in range(2):
                    last = dve.tensor_copy(hT[64 * g:64 * g + 64, 4:8, SEQ + NS * b:SEQ + NS * b + NS],
                                           ps[5][64 * g:64 * g + 64, 32 * g:32 * g + 32].rearrange("p (j q) -> p j q", j=4))
                last.then_inc(s_hb, 1)


def build_pooling(nc, a, k):
    ps, ident, ones, xT, hT, biasc, sem = k.ps, k.ident, k.ones, k.xT, k.hT, k.biasc, k.sem
    PAD = max(WINDOWS)
    OLD = NB * POOLB
    jobs = [(g, n0, nn) for g in range(4) for n0, nn in TOKEN_CHUNKS]
    (s_w, s_cm, s_sp, s_full, s_out, s_cst, s_inv, s_sps, s_old, s_st, s_pool, s_z, s_zout, s_rows, s_rowsv, s_dma) = (
        sem("s_pool_" + x) for x in ("w", "cm", "sp", "full", "out", "cst", "inv", "sps", "old", "st", "pool", "z", "zout",
                                 "rows", "rowsv", "dma"))
    with ExitStack() as cw, nc.Block() as block:
        def sb(name, shape, dt=F32):
            return k.sb(name, shape, dt, cw)

        w = sb("w_u", [P, KT, 512])
        cmap = sb("cmap", [P, 4, P])
        cscale = sb("cscale", [P, 4])
        old = sb("old", [OLD, 512])
        up = sb("up", [P, 4, PAD + SEQ])
        us = sb("us", [P, 4, NB, POOLB + NS])
        un = sb("un", [P, 4, SM])
        sums = sb("sums", [P, 2, PAD + SEQ])
        ssums = sb("ssums", [P, 2, NB, POOLB + NS])
        inv = sb("inv", [P, PAD])
        first = sb("first", [P, PAD])
        pooled = sb("pooled", [P, 2, N])
        tail = sb("tail", [POOLB, 512])
        new = sb("new", [SM, 512])

        @block.sync
        def _(sp):
            sp.dma_start(w[:], k.w_in[:, :, OFF["u"]:OFF["u"] + 512]).then_inc(s_w, 16)
            sp.dma_start(old[:], a["state_pool"][0].rearrange("b r c -> (b r) c")).then_inc(s_sp, 16)
            sp.dma_start(cmap[:], a["c_map"][0].rearrange("g c d -> c g d")).then_inc(s_cm, 16)
            sp.dma_start(cscale[:], a["c_scale"][0].rearrange("(g c) -> c g", g=4)).then_inc(s_cm, 16)
            for b in range(NB):
                sp.dma_start(a["pool_sample"][0, b, 0:POOLB - NS], a["state_pool"][0, b, NS:POOLB]).then_inc(s_dma, 16)
            sp.wait_ge(s_rowsv, 2)
            sp.dma_start(a["pool_prompt"][0, 0], tail[:]).then_inc(s_dma, 16)
            for b in range(NB):
                sp.dma_start(a["pool_sample"][0, b, POOLB - NS:], new[NS * b:NS * b + NS, :]).then_inc(s_dma, 16)
            sp.wait_ge(s_dma, 16 * (2 * NB + 1))

        @block.gpsimd
        def _(pool):
            pool.iota(inv[:], pattern=[[1, PAD]], base=1, channel_multiplier=0,
                      allow_small_or_imprecise_dtypes=True).then_inc(s_cst, 1)

        @block.tensor
        def _(pe):
            pe.wait_ge(s_sp, 16)
            for g in range(4):
                last = pe.transpose(ps[7][:, g * OLD:(g + 1) * OLD], old[:, g * P:(g + 1) * P], ident[0:OLD, 0:OLD])
            last.then_inc(s_sps, 1)
            pe.wait_ge(s_w, 16)
            for j, (g, n0, nn) in enumerate(jobs):
                if j >= 4:
                    pe.wait_ge(s_out, j - 3)
                product(pe, ps[j % 4][:, 0:nn], P, lambda kt: w[:, kt, g * P:(g + 1) * P],
                        lambda kt: xT[:, kt, n0:n0 + nn], KT).then_inc(s_full, 1)
            pe.wait_ge(s_out, len(jobs))
            for g in range(4):
                pe.transpose(ps[5][0:POOLB, g * P:(g + 1) * P], up[:, g, PAD + SEQ - POOLB:], ident[:])
            for g in range(4):
                last = pe.transpose(ps[6][0:SM, g * P:(g + 1) * P], un[:, g, :], ident[:])
            last.then_inc(s_rows, 1)
            pe.wait_ge(s_cm, 32)
            for g in range(4):
                pe.wait_ge(s_pool, g + 1)
                for i, (n0, nn) in enumerate(TOKEN_CHUNKS):
                    j = 3 * g + i
                    if j >= 4:
                        pe.wait_ge(s_zout, j - 3)
                    pe.matmul(ps[j % 4][:, 0:nn], cmap[:, g, :], pooled[:, g % 2, n0:n0 + nn], start=True,
                              stop=True).then_inc(s_z, 1)

        @block.scalar
        def _(act):
            for j, (g, n0, nn) in enumerate(jobs):
                act.wait_ge(s_full, j + 1)
                bias = biasc[:, BC["u"] + g:BC["u"] + g + 1]
                if n0 < SEQ:
                    act.activation(up[:, g, PAD + n0:PAD + n0 + nn], ps[j % 4][:, 0:nn], ACT.Identity,
                                   bias=bias).then_inc(s_out, 1)
                else:
                    act.activation(un[:, g, :], ps[j % 4][:, 0:nn], ACT.Identity, bias=bias)
                    act.activation(us[:, g, :, POOLB:], ps[j % 4][:, 0:nn].rearrange("p (b t) -> p b t", b=NB),
                                   ACT.Identity, bias=bias).then_inc(s_out, 1)
            act.wait_ge(s_rows, 1)
            act.copy(tail[:], ps[5][0:POOLB, :]).then_inc(s_rowsv, 1)
            act.copy(new[:], ps[6][0:SM, :]).then_inc(s_rowsv, 1)
            for j in range(12):
                g, (n0, nn) = j // 3, TOKEN_CHUNKS[j % 3]
                act.wait_ge(s_z, j + 1)
                act.activation(hT[:, 8 + g, n0:n0 + nn], ps[j % 4][:, 0:nn], ACT.Copy,
                               scale=cscale[:, g:g + 1]).then_inc(s_zout, 1)

        @block.vector
        def _(dve):
            n = 0

            def step(ins):
                nonlocal n
                n += 1
                ins.then_inc(s_st, 1)
                dve.wait_ge(s_st, n)

            dve.memset(up[:, :, 0:PAD], 0.0)
            dve.memset(sums[:, :, 0:PAD], 0.0)
            dve.memset(ssums[:], 0.0)
            dve.wait_ge(s_cst, 1)
            step(dve.reciprocal(inv[:], inv[:]))
            dve.wait_ge(s_sps, 1)
            step(dve.tensor_copy(us[:, :, :, 0:POOLB], ps[7][:, 0:4 * OLD].rearrange("p (g b r) -> p g b r", g=4, b=NB)))
            for g, w_ in enumerate(WINDOWS):
                dve.wait_ge(s_out, 3 * g + 3)
                src, ssrc, d, i = up[:, g, :], us[:, g], 1, 0
                while d < w_:
                    dst, sdst = sums[:, i % 2, :], ssums[:, i % 2]
                    dve.tensor_tensor(sdst[:, :, d:], ssrc[:, :, d:], ssrc[:, :, :POOLB + NS - d], ALU.add)
                    step(dve.tensor_tensor(dst[:, PAD:], src[:, PAD:], src[:, PAD - d:PAD + SEQ - d], ALU.add))
                    src, ssrc, d, i = dst, sdst, 2 * d, i + 1
                if g >= 2:
                    dve.wait_ge(s_z, 3 * (g - 1))
                dve.scalar_tensor_tensor(pooled[:, g % 2, 0:SEQ], src[:, PAD:], 1.0 / w_, up[:, g, PAD:], ALU.mult,
                                         ALU.subtract)
                dve.scalar_tensor_tensor(pooled[:, g % 2, SEQ:].rearrange("p (b t) -> p b t", b=NB), ssrc[:, :, POOLB:],
                                         1.0 / w_, us[:, g, :, POOLB:], ALU.mult, ALU.subtract)
                step(dve.tensor_tensor(first[:, 0:w_], src[:, PAD:PAD + w_], inv[:, 0:w_], ALU.mult))
                dve.tensor_tensor(pooled[:, g % 2, 0:w_], first[:, 0:w_], up[:, g, PAD:PAD + w_],
                                  ALU.subtract).then_inc(s_pool, 1)


def build_merge(nc, a, k):
    ps, banks, ident, xT, hT, biasc, sem = k.ps, k.banks, k.ident, k.xT, k.hT, k.biasc, k.sem
    units = [(et, c, x) for et in range(KT) for c in range(3) for x in range(3)]
    (s_w, s_full, s_sig, s_prod, s_st, s_wo, s_ln) = (sem("s_merge_" + x) for x in ("w", "full", "sig", "prod", "st", "wo", "ln"))
    s_wt = [sem("s_mwt0"), sem("s_mwt1")]
    with ExitStack() as cm:
        def sb(name, shape, dt=F32):
            return k.sb(name, shape, dt, cm)

        merged = sb("merged", [P, KT, N])
        wo = sb("w_out_t", [P, KT, D])
        with ExitStack() as cw, nc.Block() as block:
            wt = k.sb("w_gates", [P, 2, 3, KT, P], F32, cw)
            pt = k.sb("p_mix", [P, 2, 3, 4, P], F32, cw)
            sg = k.sb("sg", [P, 4, 512], F32, cw)
            pr = k.sb("prod", [P, 512], F32, cw)

            @block.sync
            def _(sp):
                for et in range(KT):
                    if et >= 2:
                        sp.wait_ge(s_full, 9 * (et - 1))
                    s, cols = et % 2, slice(et * P, (et + 1) * P)
                    for x, name in enumerate(("ga", "gb", "gc")):
                        at = OFF[name] + et * P
                        sp.dma_start(wt[:, s, x], k.w_in[:, :, at:at + P]).then_inc(s_wt[s], 16)
                    sp.dma_start(pt[:, s, 0], a["p_a"][0].rearrange("(k p) n -> p k n", p=P)[:, :, cols]).then_inc(s_wt[s], 16)
                    for g in range(BKV):
                        sp.dma_start(pt[64 * g:64 * g + 64, s, 1],
                                     a["p_b"][0][256 * g:256 * g + 256].rearrange("(j d) n -> d j n", d=BD)[:, :, cols]
                                     ).then_inc(s_wt[s], 16)
                    sp.dma_start(pt[:, s, 2], a["p_c"][0].rearrange("(k p) n -> p k n", p=P)[:, :, cols]).then_inc(s_wt[s], 16)
                sp.dma_start(wo[:], a["w_out"][0].rearrange("(k p) n -> p k n", p=P)).then_inc(s_wo, 16)
                sp.wait_ge(s_wo, 16)

            @block.tensor
            def _(pe):
                for n, (et, c, x) in enumerate(units):
                    s, (n0, nn) = et % 2, TOKEN_CHUNKS[c]
                    if c == 0 and x == 0:
                        pe.wait_ge(s_wt[s], 16 * 7 * (et // 2 + 1))
                    if n >= 4:
                        pe.wait_ge(s_prod, n - 3)
                    b = 2 * (n % 4)
                    product(pe, ps[b][:, 0:nn], P, lambda kt: wt[:, s, x, kt, :], lambda kt: xT[:, kt, n0:n0 + nn], KT)
                    product(pe, ps[b + 1][:, 0:nn], P, lambda kt: pt[:, s, x, kt, :],
                            lambda kt: hT[:, 4 * x + kt, n0:n0 + nn], 4).then_inc(s_full, 1)

            @block.scalar
            def _(act):
                for n, (et, c, x) in enumerate(units):
                    nn = TOKEN_CHUNKS[c][1]
                    act.wait_ge(s_full, n + 1)
                    col = BC["g"] + 8 * x + et
                    act.activation(sg[:, n % 4, 0:nn], ps[2 * (n % 4)][:, 0:nn], ACT.Sigmoid,
                                   bias=biasc[:, col:col + 1]).then_inc(s_sig, 1)

            @block.vector
            def _(dve):
                m = 0
                for n, (et, c, x) in enumerate(units):
                    n0, nn = TOKEN_CHUNKS[c]
                    dve.wait_ge(s_sig, n + 1)
                    out = merged[:, et, n0:n0 + nn]
                    if x and m:
                        dve.wait_ge(s_st, m)
                    dve.tensor_tensor(pr[:, 0:nn] if x else out, sg[:, n % 4, 0:nn], ps[2 * (n % 4) + 1][:, 0:nn],
                                      ALU.mult).then_inc(s_prod, 1)
                    if x:
                        dve.wait_ge(s_prod, n + 1)
                        dve.tensor_tensor(out, out, pr[:, 0:nn], ALU.add).then_inc(s_st, 1)
                        m += 1

        k.x1 = nc.dram_tensor("x1", (N, D), F32, kind="Internal").ap()
        (s_y, s_yst, s_ve, s_rs, s_nb, s_z, s_x1, s_tp, s_tpe, s_ys) = (
            sem("s_norm_" + x) for x in ("y", "yst", "ve", "rs", "nb", "z", "x1", "tp", "tpe", "ys"))
        s_x1d = [sem("s_x1_stored0"), sem("s_x1_stored1")]
        s_full2 = sem("s_lfull")
        s_xr = [sem("s_lxr0"), sem("s_lxr1")]
        with ExitStack() as cw, nc.Block() as block:
            lng = k.sb("ln1g", [P, D], F32, cw)
            lnb = k.sb("ln1b", [P, D], F32, cw)
            xr = k.sb("xr", [P, 2, D], F32, cw)
            y = k.sb("y", [P, 2, D], F32, cw)
            st = k.sb("st", [P, 2, 6], F32, cw)
            mv = k.sb("mv", [P, 2, 4], F32, cw)

            @block.sync
            def _(sp):
                sp.dma_start(lng[:], a["ln1_g"].broadcast_to([P, D])).then_inc(s_ln, 16)
                sp.dma_start(lnb[:], a["ln1_b"].broadcast_to([P, D])).then_inc(s_ln, 16)
                for t in range(NT):
                    if t >= 2:
                        sp.wait_ge(s_y, t - 1)
                    sp.dma_start(xr[0:rows(t), t % 2, :], k.token_rows(k.x_p, k.x_s, t)).then_inc(s_xr[t % 2], 16)
                    if t:
                        sp.wait_ge(s_x1, t)
                        sp.dma_start(k.x1[(t - 1) * P:t * P, :], y[:, (t - 1) % 2, :]).then_inc(s_x1d[(t - 1) % 2], 16)
                sp.wait_ge(s_x1, NT)
                sp.dma_start(k.x1[SEQ:N, :], y[0:SM, (NT - 1) % 2, :]).then_inc(s_x1d[(NT - 1) % 2], 16)
                for s in range(2):
                    sp.wait_ge(s_x1d[s], 16 * ((NT + 1 - s) // 2))

            @block.tensor
            def _(pe):
                def turn(t):
                    pe.wait_ge(s_x1, t + 1)
                    if t:
                        pe.wait_ge(s_tpe, t)
                    for i in range(KT):
                        last = pe.transpose(ps[4 + i // 4][:, (i % 4) * P:(i % 4) * P + rows(t)],
                                            y[0:rows(t), t % 2, i * P:(i + 1) * P], ident[0:rows(t), 0:rows(t)])
                    last.then_inc(s_tp, 1)

                for t in range(NT):
                    if t >= 2:
                        pe.wait_ge(s_y, t - 1)
                    for i in range(2):
                        last = product(pe, ps[2 * (t % 2) + i][0:rows(t), :], P,
                                       lambda kt: merged[:, kt, t * P:t * P + rows(t)],
                                       lambda kt: wo[:, kt, 512 * i:512 * i + 512], KT)
                    last.then_inc(s_full2, 1)
                    if t:
                        turn(t - 1)
                turn(NT - 1)

            @block.scalar
            def _(act):
                def spread(t):
                    act.wait_ge(s_tp, t + 1)
                    act.copy(xT[:, :, t * P:t * P + rows(t)],
                             banks[:, 4:6, :].rearrange("p b (k n) -> p (b k) n", n=P)[:, :, 0:rows(t)]).then_inc(s_tpe, 1)

                for t in range(NT):
                    act.wait_ge(s_nb, t + 1)
                    r = rows(t)
                    act.activation(y[0:r, t % 2, :], y[0:r, t % 2, :], ACT.Identity, bias=mv[0:r, t % 2, 3:4],
                                   scale=mv[0:r, t % 2, 2:3]).then_inc(s_z, 1)
                    if t:
                        spread(t - 1)
                spread(NT - 1)

            @block.gpsimd
            def _(pool):
                for t in range(NT):
                    r = rows(t)
                    pool.wait_ge(s_ve, t + 1)
                    pool.tensor_tensor(mv[0:r, t % 2, 2:3], mv[0:r, t % 2, 1:2], k.neghalf[0:r, 0:1],
                                       ALU.pow).then_inc(s_rs, 1)

            @block.vector
            def _(dve):
                n = 0

                def step(ins):
                    nonlocal n
                    n += 1
                    ins.then_inc(s_yst, 1)
                    dve.wait_ge(s_yst, n)

                dve.wait_ge(s_ln, 32)
                for t in range(NT):
                    r, s = rows(t), t % 2
                    v = y[0:r, s, :]
                    dve.wait_ge(s_xr[s], 16 * (t // 2 + 1))
                    dve.wait_ge(s_full2, t + 1)
                    if t >= 2:
                        dve.wait_ge(s_x1d[s], 16 * (t // 2))
                        dve.wait_ge(s_tp, t - 1)
                    dve.scalar_tensor_tensor(v, xr[0:r, s, :], ALPHA,
                                             banks[0:r, 2 * s:2 * s + 2, :].rearrange("p b n -> p (b n)"), ALU.mult,
                                             ALU.add).then_inc(s_y, 1)
                    dve.wait_ge(s_y, t + 1)
                    for i in range(2):
                        last = dve.bn_stats(st[0:r, i, :], y[0:r, s, 512 * i:512 * i + 512])
                    step(last)
                    step(dve.bn_aggr(mv[0:r, s, 0:2], st[0:r]))
                    dve.tensor_scalar(mv[0:r, s, 1:2], mv[0:r, s, 1:2], EPS, None, ALU.add).then_inc(s_ve, 1)
                    dve.wait_ge(s_rs, t + 1)
                    dve.scalar_tensor_tensor(mv[0:r, s, 3:4], mv[0:r, s, 0:1], -1.0, mv[0:r, s, 2:3], ALU.mult,
                                             ALU.mult).then_inc(s_nb, 1)
                    dve.wait_ge(s_z, t + 1)
                    step(dve.tensor_tensor(v, v, lng[0:r, :], ALU.mult))
                    dve.tensor_tensor(v, v, lnb[0:r, :], ALU.add).then_inc(s_x1, 1)


def build_moe(nc, a, k):
    ps, banks, ident, ones, xT, sem = k.ps, k.banks, k.ident, k.ones, k.xT, k.sem
    ds = bass.ds
    table = nc.dram_tensor("token_of_slot", (E * ECAP, 1), F32, kind="Internal").ap()
    rows_out = nc.dram_tensor("expert_rows", (E * CAP, D), F32, kind="Internal").ap()
    with ExitStack() as cm:
        def sb(name, shape, dt=F32, c=cm):
            return k.sb(name, shape, dt, c)

        acc = sb("acc", [P, NT, D])
        gate8 = sb("gate8", [P, NT, TOPK])
        exp8 = sb("exp8", [P, NT, TOPK])
        rel8 = sb("rel8", [P, NT, TOPK])
        longest = sb("longest", [P, 1], I32)

        s9 = {x: sem("s_route_" + x) for x in ("w", "wsh", "wdn", "zero", "tab", "lg", "sig", "st", "iota", "sel", "pos",
                                               "slot", "scat", "sh", "shs", "shh", "dn", "acc", "xr", "xrm")}
        s_xr = [sem("s_route_xr0"), sem("s_route_xr1")]
        shared = [(m, n0, nn) for n0, nn in TOKEN_CHUNKS for m in range(2)]
        with ExitStack() as cw, nc.Block() as block:
            rw = sb("rw", [P, KT, E], c=cw)
            rb = sb("rb", [P, E], c=cw)
            zero = sb("zero", [E, ECAP], c=cw)
            sgu = sb("sgu", [P, KT, 512], c=cw)
            sdn = sb("sdn", [P, 2, D], c=cw)
            shT = sb("shT", [P, 2, N], c=cw)
            ssg = sb("ssg", [P, 2, 512], c=cw)
            xr = sb("xr9", [P, 2, D], c=cw)
            sc = sb("sc9", [P, NT, E], c=cw)
            bi = sb("bi", [P, NT, E], c=cw)
            sel = sb("sel", [P, NT, E], c=cw)
            t1 = sb("t1", [P, NT, E], c=cw)
            gates = sb("gates", [P, NT, E], c=cw)
            val = sb("val", [P, NT, E], c=cw)
            cum = sb("cum", [P, NT, E], c=cw)
            m8 = sb("m8", [P, NT * EG, 8], c=cw)
            gs = sb("gs", [P, NT * EG], c=cw)
            rank = sb("rank", [P, NT * EG], c=cw)
            lower = sb("lower", [P, EG, EG], c=cw)
            slot0 = sb("slot0", [P, E], c=cw)
            den = sb("den9", [P, NT], c=cw)
            v8 = sb("v8", [P, NT, TOPK], c=cw)
            i8 = sb("i8", [P, NT, TOPK], I32, cw)
            j8 = sb("j8", [P, NT, TOPK], I32, cw)
            slot8 = sb("slot8", [P, NT, TOPK], I32, cw)
            token = sb("token", [P, NT], c=cw)
            lmax = sb("lmax", [P, 1], c=cw)

            @block.sync
            def _(sp):
                sp.dma_start(rw[:], a["router_w"][0].rearrange("(k p) e -> p k e", p=P)).then_inc(s9["w"], 16)
                sp.dma_start(rb[:], a["router_b"].broadcast_to([P, E])).then_inc(s9["w"], 16)
                sp.dma_start(sgu[:], a["sh_gu"][0].rearrange("(k p) n -> p k n", p=P)).then_inc(s9["wsh"], 16)
                sp.dma_start(sdn[:], a["sh_down"][0].rearrange("(k p) n -> p k n", p=P)).then_inc(s9["wdn"], 16)
                sp.wait_ge(s9["zero"], 1)
                sp.dma_start(table.rearrange("(e c) o -> e (c o)", e=E), zero[:]).then_inc(s9["tab"], 16)
                for t in range(NT):
                    if t >= 2:
                        sp.wait_ge(s9["acc"], t - 1)
                    sp.dma_start(xr[0:rows(t), t % 2, :], k.x1[t * P:t * P + rows(t), :]).then_inc(s_xr[t % 2], 16)

            @block.gpsimd
            def _(pool):
                pool.memset(zero[:], 0.0).then_inc(s9["zero"], 1)
                pool.memset(lower[:], 1.0).then_inc(s9["zero"], 1)
                pool.iota(slot0[:], pattern=[[1 << SHIFT, E]], base=1, channel_multiplier=0,
                          allow_small_or_imprecise_dtypes=True).then_inc(s9["iota"], 1)
                pool.iota(token[:], pattern=[[P, NT]], base=0, channel_multiplier=1,
                          allow_small_or_imprecise_dtypes=True).then_inc(s9["iota"], 1)
                pool.wait_ge(s9["zero"], 2)
                pool.affine_select(out=lower[:], in_=lower[:], compare_op=ALU.is_ge, fill=0.0, base=-1,
                                   pattern=[[1, EG], [-1, EG]], channel_multiplier=0).then_inc(s9["iota"], 1)
                pool.wait_ge(s9["tab"], 16)
                pool.wait_ge(s9["slot"], 1)
                pool.wait_ge(s9["iota"], 3)
                for t in range(NT):
                    for i in range(TOPK):
                        pool.indirect_dma_start(table, bass.IndirectOffsetOnAxis(ap=slot8[0:rows(t), t, i:i + 1], axis=0),
                                                token[0:rows(t), t:t + 1], None).then_inc(s9["scat"], 16)
                pool.wait_ge(s9["scat"], 16 * NT * TOPK)

            @block.tensor
            def _(pe):
                pe.wait_ge(s9["w"], 32)
                for t in range(NT):
                    last = product(pe, ps[t // 8][0:rows(t), (t % 8) * E:(t % 8 + 1) * E], P,
                                   lambda kt: xT[:, kt, t * P:t * P + rows(t)], lambda kt: rw[:, kt, :], KT)
                last.then_inc(s9["lg"], 1)
                pe.wait_ge(s9["wsh"], 16)
                for j, (m, n0, nn) in enumerate(shared):
                    if j >= 2:
                        pe.wait_ge(s9["shh"], j - 1)
                    b = 4 + 2 * (j % 2)
                    product(pe, ps[b][:, 0:nn], P, lambda kt: sgu[:, kt, m * P:(m + 1) * P],
                            lambda kt: xT[:, kt, n0:n0 + nn], KT)
                    product(pe, ps[b + 1][:, 0:nn], P, lambda kt: sgu[:, kt, F + m * P:F + (m + 1) * P],
                            lambda kt: xT[:, kt, n0:n0 + nn], KT).then_inc(s9["sh"], 1)
                pe.wait_ge(s9["wdn"], 16)
                pe.wait_ge(s9["shh"], len(shared))

                def down(t):
                    if t >= 2:
                        pe.wait_ge(s9["acc"], t - 1)
                    for i in range(2):
                        last = product(pe, ps[4 + 2 * (t % 2) + i][0:rows(t), :], P,
                                       lambda kt: shT[:, kt, t * P:t * P + rows(t)],
                                       lambda kt: sdn[:, kt, 512 * i:512 * i + 512], 2)
                    last.then_inc(s9["dn"], 1)

                down(0)
                down(1)
                pe.wait_ge(s9["sel"], 1)
                for t in range(NT):
                    out = ps[2 + t // 8][:, (t % 8) * E:(t % 8 + 1) * E]
                    pe.matmul(out, k.before[:], sel[:, t, :], start=True, stop=(t == 0))
                    if t:
                        pe.matmul(out, ones[:], cum[:, t - 1, :], start=False, stop=True)
                pe.matmul(ps[3][:, E:2 * E], ones[:], cum[:, NT - 1, :], start=True, stop=True).then_inc(s9["pos"], 1)
                for t in range(2, NT):
                    down(t)

            @block.scalar
            def _(act):
                act.wait_ge(s9["lg"], 1)
                act.activation(sc[:, 0:8, :], ps[0].rearrange("p (t e) -> p t e", t=8), ACT.Sigmoid)
                act.activation(sc[0:SM, 8, :], ps[1][0:SM, 0:E], ACT.Sigmoid).then_inc(s9["sig"], 1)
                for j, (m, n0, nn) in enumerate(shared):
                    b = 4 + 2 * (j % 2)
                    act.wait_ge(s9["sh"], j + 1)
                    act.activation(ssg[:, j % 2, 0:nn], ps[b][:, 0:nn], ACT.Silu).then_inc(s9["shs"], 1)
                for t in range(NT):
                    r = rows(t)
                    act.wait_ge(s_xr[t % 2], 16 * (t // 2 + 1))
                    act.activation(acc[0:r, t, :], xr[0:r, t % 2, :], ACT.Copy, scale=ALPHA).then_inc(s9["xrm"], 1)
                    act.wait_ge(s9["acc"], t + 1)

            @block.vector
            def _(dve):
                n = 0

                def step(ins):
                    nonlocal n
                    n += 1
                    ins.then_inc(s9["st"], 1)
                    dve.wait_ge(s9["st"], n)

                def by_group(x):
                    return x[:].rearrange("p t (g e) -> p (t g) e", e=E // EG)

                def pairs(x, at):
                    return x[:].rearrange("p (t g) -> p t g", g=EG).unsqueeze(at).to_broadcast([P, NT, EG, EG])

                step(dve.memset(sc[SM:P, 8, :], 0.5))
                dve.wait_ge(s9["w"], 32)
                dve.wait_ge(s9["sig"], 1)
                step(dve.tensor_tensor(bi[:], sc[:], rb[:].unsqueeze(1).to_broadcast([P, NT, E]), ALU.add))
                for i in range(NT * EG):
                    last = dve.max(m8[:, i, :], by_group(bi)[:, i, :])
                step(last)
                step(dve.tensor_tensor(gs[:].unsqueeze(2), m8[:, :, 0:1], m8[:, :, 1:2], ALU.add))
                dve.wait_ge(s9["iota"], 3)
                p1 = t1[:].rearrange("p t (i j) -> p t i j", i=EG)
                p2 = sel[:].rearrange("p t (i j) -> p t i j", i=EG)
                dve.tensor_tensor(p1, pairs(gs, 2), pairs(gs, 3), ALU.is_gt)
                step(dve.tensor_tensor(p2, pairs(gs, 2), pairs(gs, 3), ALU.is_equal))
                step(dve.tensor_tensor(p2, p2, lower[:].unsqueeze(1).to_broadcast([P, NT, EG, EG]), ALU.mult))
                step(dve.tensor_tensor(p1, p1, p2, ALU.add))
                step(dve.tensor_reduce(rank[:].rearrange("p (t g) -> p t g", g=EG), p1, AX, ALU.add))
                step(dve.tensor_scalar(rank[:], rank[:], float(TOPG), 1.0, ALU.is_lt, ALU.subtract))
                step(dve.tensor_scalar(rank[:], rank[:], BIG, None, ALU.mult))
                step(dve.tensor_tensor(by_group(bi), by_group(bi), rank[:].unsqueeze(2).to_broadcast([P, NT * EG, E // EG]),
                                       ALU.add))
                for t in range(NT):
                    last = dve.max(v8[:, t, :], bi[:, t, :])
                step(last)
                for t in range(NT):
                    last = dve.match_replace(t1[:, t, :], v8[:, t, :], bi[:, t, :], GONE)
                step(last)
                step(dve.tensor_scalar(sel[:], t1[:], GONE, None, ALU.is_equal))
                step(dve.memset(sel[SM:P, 8, :], 0.0))
                step(dve.tensor_copy(cum[:, 0, :], sel[:, 0, :]))
                for t in range(1, NT):
                    step(dve.tensor_tensor(cum[:, t, :], cum[:, t - 1, :], sel[:, t, :], ALU.add))
                dve.sem_inc(s9["sel"], 1)
                step(dve.tensor_tensor(gates[:], sc[:], sel[:], ALU.mult))
                step(dve.tensor_reduce(den[:], gates[:], AX, ALU.add))
                step(dve.memset(den[SM:P, 8:9], 1.0))
                step(dve.reciprocal(den[:], den[:]))
                step(dve.tensor_scalar(den[:], den[:], 2.5, None, ALU.mult))
                step(dve.tensor_tensor(gates[:], gates[:], den[:].unsqueeze(2).to_broadcast([P, NT, E]), ALU.mult))
                for j, (m, n0, nn) in enumerate(shared):
                    b = 4 + 2 * (j % 2)
                    dve.wait_ge(s9["shs"], j + 1)
                    dve.tensor_tensor(shT[:, m, n0:n0 + nn], ssg[:, j % 2, 0:nn], ps[b + 1][:, 0:nn],
                                      ALU.mult).then_inc(s9["shh"], 1)
                dve.wait_ge(s9["pos"], 1)
                dve.tensor_tensor(val[:, 0:8, :], ps[2].rearrange("p (t e) -> p t e", t=8),
                                  slot0[:].unsqueeze(1).to_broadcast([P, 8, E]), ALU.add)
                step(dve.tensor_tensor(val[:, 8, :], ps[3][:, 0:E], slot0[:], ALU.add))
                step(dve.tensor_tensor(val[:], val[:], sel[:], ALU.mult))
                step(dve.tensor_scalar(val[:], val[:], 1.0, None, ALU.subtract))
                dve.tensor_reduce(lmax[:], ps[3][:, E:2 * E], AX, ALU.max)
                for t in range(NT):
                    last = dve.max(v8[:, t, :], val[:, t, :])
                step(last)
                dve.tensor_copy(longest[:], lmax[:])
                step(dve.tensor_copy(i8[:], v8[:]))
                dve.tensor_scalar(j8[:], i8[:], SHIFT, None, ALU.arith_shift_right)
                step(dve.tensor_scalar(i8[:], i8[:], (1 << SHIFT) - 1, None, ALU.bitwise_and))
                dve.tensor_copy(rel8[:], i8[:])
                step(dve.tensor_copy(exp8[:], j8[:]))
                step(dve.scalar_tensor_tensor(slot8[:], exp8[:], float(ECAP), rel8[:], ALU.mult, ALU.add))
                dve.sem_inc(s9["slot"], 1)
                step(dve.tensor_scalar(exp8[:], exp8[:], float(CAP), None, ALU.mult))
                for i in range(TOPK):
                    step(dve.tensor_tensor(t1[:], val[:], v8[:, :, i:i + 1].to_broadcast([P, NT, E]), ALU.is_equal))
                    step(dve.tensor_tensor(t1[:], t1[:], gates[:], ALU.mult))
                    step(dve.tensor_reduce(gate8[:, :, i:i + 1].rearrange("p t o -> p (t o)"), t1[:], AX, ALU.add))
                for t in range(NT):
                    r, b = rows(t), 4 + 2 * (t % 2)
                    dve.wait_ge(s9["dn"], t + 1)
                    dve.wait_ge(s9["xrm"], t + 1)
                    dve.tensor_tensor(acc[0:r, t, :], acc[0:r, t, :],
                                      banks[0:r, b:b + 2, :].rearrange("p b n -> p (b n)"), ALU.add).then_inc(s9["acc"], 1)

        s_r = {x: sem("s_round_" + x) for x in ("tab", "turn", "ids", "step", "tp", "xev", "gu", "silu", "h", "dn",
                                                "yev", "idx", "comb", "seen", "wfree", "gfree")}
        s_w = [[sem(f"s_round_wgu{i}"), sem(f"s_round_wdn{i}")] for i in range(2)]
        s_xg = [sem(f"s_round_xg{i}") for i in range(2)]
        s_ys = [sem(f"s_round_stored{i}") for i in range(2)]
        s_yb = [sem(f"s_round_back{i}") for i in range(4)]
        everything = list(s_r.values()) + s_w[0] + s_w[1] + s_xg + s_ys + s_yb
        count = nc.values_load(longest[0:1, 0:1], min_val=1, max_val=N)
        SLOTS = ((0, P), (P, CAP - P))
        TURNS = ((0, P, 0, 4), (1, CAP - P, 0, KT), (0, P, 4, 4))
        with nc.Fori(0, ROUNDS) as r, nc.If(count > r * CAP):
            with ExitStack() as cw, nc.Block() as block:
                wgu = sb("wgu", [P, 2, KT, 2 * F], c=cw)
                wdn = sb("wdn", [P, 2, 2, D], c=cw)
                tab = sb("tab", [E, CAP], c=cw)
                ids = sb("ids", [P, 2, E], I32, cw)
                xg = sb("xg", [P, 2, 2, D], c=cw)
                xgT = sb("xgT", [P, 2, KT, CAP], c=cw)
                sg = sb("sgr", [P, 2, 2 * CAP], c=cw)
                hh = sb("hh", [P, 2, 2, CAP], c=cw)
                y = sb("yr", [P, 2, 2, D], c=cw)
                gu_view = a["exp_gu"][0].rearrange("e (k p) n -> p e k n", p=P)
                dn_view = a["exp_down"][0].rearrange("e (k p) n -> p e k n", p=P)
                last_pair = E // 2 - 1

                @block.sync
                def _(sp):
                    sp.dma_start(tab[:], table.rearrange("(e c) o -> e (c o)", e=E)[:, ds(r * CAP, CAP)]
                                 ).then_inc(s_r["tab"], 16)

                    def load(e, u):
                        sp.dma_start(wgu[:, u], gu_view[:, ds(e, 1)].rearrange("p o k n -> p (o k) n")).then_inc(s_w[u][0], 16)
                        sp.dma_start(wdn[:, u], dn_view[:, ds(e, 1)].rearrange("p o k n -> p (o k) n")).then_inc(s_w[u][1], 16)

                    def store(e, u, n):
                        sp.wait_ge(s_r["yev"], n)
                        for i, (at, c) in enumerate(SLOTS):
                            sp.dma_start(rows_out[ds(e * CAP + at, c), :], y[0:c, u, i, :]).then_inc(s_ys[u], 16)

                    load(0, 0)
                    load(1, 1)
                    with sp.Fori(0, last_pair) as i:
                        for u in range(2):
                            sp.wait_ge(s_r["dn"], i * 2 + (u + 1))
                            load(i * 2 + (u + 2), u)
                            store(i * 2 + u, u, i * 8 + (4 * u + 4))
                    for u in range(2):
                        store(2 * last_pair + u, u, 8 * last_pair + 4 * u + 4)
                    for u in range(2):
                        sp.wait_ge(s_ys[u], 32 * (last_pair + 1))

                @block.gpsimd
                def _(pool):
                    pool.wait_ge(s_r["ids"], 1)
                    for e in range(E):
                        u, n = e % 2, e // 2
                        if n:
                            pool.wait_ge(s_xg[u], 32 * n)
                            pool.wait_ge(s_r["tp"], 3 * (e - 1))
                        for i, (at, c) in enumerate(SLOTS):
                            pool.indirect_dma_start(xg[0:c, u, i, :], None, k.x1,
                                                    bass.IndirectOffsetOnAxis(ap=ids[0:c, i, e:e + 1], axis=0)
                                                    ).then_inc(s_xg[u], 16)
                    for u in range(2):
                        pool.wait_ge(s_xg[u], 32 * (last_pair + 1))

                @block.tensor
                def _(pe):
                    pe.wait_ge(s_r["tab"], 16)
                    pe.transpose(ps[0][:, 0:E], tab[:, 0:P], ident[0:E, 0:E])
                    pe.transpose(ps[0][0:CAP - P, E:2 * E], tab[:, P:CAP], ident[0:E, 0:E]).then_inc(s_r["turn"], 1)
                    pe.wait_ge(s_r["ids"], 1)

                    def turn(u, n, first):
                        if not first or u:
                            pe.wait_ge(s_r["xev"], n * 6 + 3 * u)
                        pe.wait_ge(s_xg[u], n * 32 + 32)
                        for q in range(3):
                            at = 3 * u + q
                            if q == 2:
                                pe.wait_ge(s_r["xev"], n * 6 + (at - 1))
                            i, c, k0, kn = TURNS[q]
                            for kt in range(kn):
                                last = pe.transpose(ps[at % 2][:, kt * c:(kt + 1) * c],
                                                    xg[0:c, u, i, (k0 + kt) * P:(k0 + kt + 1) * P], ident[0:c, 0:c])
                            last.then_inc(s_r["tp"], 1)

                    def gate_up(u, n, first):
                        pe.wait_ge(s_w[u][0], n * 16 + 16)
                        pe.wait_ge(s_r["xev"], n * 6 + (3 * u + 3))
                        if not (first and u == 0):
                            pe.wait_ge(s_r["h"], n * 2 + u)
                        for m in range(4):
                            last = product(pe, ps[2 + m // 2][:, (m % 2) * CAP:(m % 2 + 1) * CAP], P,
                                           lambda kt: wgu[:, u, kt, m * P:(m + 1) * P], lambda kt: xgT[:, u, kt, :], KT)
                        last.then_inc(s_r["gu"], 1)

                    def down(u, n, first):
                        pe.wait_ge(s_w[u][1], n * 16 + 16)
                        pe.wait_ge(s_r["h"], n * 2 + (u + 1))
                        for q in range(4):
                            (at, c), i = SLOTS[q // 2], q % 2
                            if not (first and u == 0):
                                pe.wait_ge(s_r["yev"], n * 8 + (4 * u + q - 3))
                            last = product(pe, ps[4 + q][0:c, :], P, lambda kt: hh[:, u, kt, at:at + c],
                                           lambda kt: wdn[:, u, kt, 512 * i:512 * i + 512], 2)
                            last.then_inc(s_r["gfree"], 1)
                        pe.wait_ge(s_r["gfree"], n * 8 + (4 * u + 4))
                        pe.sem_inc(s_r["dn"], 1)

                    turn(0, 0, True)
                    gate_up(0, 0, True)
                    turn(1, 0, True)
                    down(0, 0, True)
                    gate_up(1, 0, False)
                    turn(0, 1, False)
                    down(1, 0, False)
                    with pe.Fori(1, last_pair) as i:
                        gate_up(0, i, False)
                        turn(1, i, False)
                        down(0, i, False)
                        gate_up(1, i, False)
                        turn(0, i + 1, False)
                        down(1, i, False)
                    gate_up(0, last_pair, False)
                    turn(1, last_pair, False)
                    down(0, last_pair, False)
                    gate_up(1, last_pair, False)
                    down(1, last_pair, False)

                @block.scalar
                def _(act):
                    def spread(u, n, first):
                        for q in range(3):
                            at = 3 * u + q
                            act.wait_ge(s_r["tp"], n * 6 + (at + 1))
                            if q == 0 and not first:
                                act.wait_ge(s_r["gu"], n * 2 + (u - 1))
                            if q != 1:
                                act.copy(xgT[:, u, 2 * q:2 * q + 4, 0:P],
                                         ps[at % 2].rearrange("p (k c) -> p k c", k=4)).then_inc(s_r["xev"], 1)
                            else:
                                act.copy(xgT[:, u, :, P:CAP],
                                         ps[at % 2].rearrange("p (k c) -> p k c", k=KT)).then_inc(s_r["xev"], 1)

                    def silu(u, n, first):
                        act.wait_ge(s_r["gu"], n * 2 + (u + 1))
                        act.activation(sg[:, u, :], ps[2][:, 0:2 * CAP], ACT.Silu).then_inc(s_r["silu"], 1)

                    spread(0, 0, True)
                    silu(0, 0, True)
                    spread(1, 0, True)
                    silu(1, 0, True)
                    spread(0, 1, False)
                    with act.Fori(1, last_pair) as i:
                        silu(0, i, False)
                        spread(1, i, False)
                        silu(1, i, False)
                        spread(0, i + 1, False)
                    silu(0, last_pair, False)
                    spread(1, last_pair, False)
                    silu(1, last_pair, False)

                @block.vector
                def _(dve):
                    dve.memset(ids[CAP - P:P, 1, :], 0)
                    dve.wait_ge(s_r["turn"], 1)
                    dve.tensor_copy(ids[:, 0, :], ps[0][:, 0:E]).then_inc(s_r["step"], 1)
                    dve.wait_ge(s_r["step"], 1)
                    dve.tensor_copy(ids[0:CAP - P, 1, :], ps[0][0:CAP - P, E:2 * E]).then_inc(s_r["ids"], 1)

                    def expert(u, n, first):
                        dve.wait_ge(s_r["silu"], n * 2 + (u + 1))
                        if not first:
                            dve.wait_ge(s_r["dn"], n * 2 + (u - 1))
                        dve.tensor_tensor(hh[:, u].rearrange("p k c -> p (k c)"), sg[:, u, :], ps[3][:, 0:2 * CAP],
                                          ALU.mult).then_inc(s_r["h"], 1)
                        if not first:
                            dve.wait_ge(s_ys[u], n * 32)
                        for q in range(4):
                            (at, c), i = SLOTS[q // 2], q % 2
                            dve.wait_ge(s_r["gfree"], n * 8 + (4 * u + q + 1))
                            dve.tensor_copy(y[0:c, u, q // 2, 512 * i:512 * i + 512], ps[4 + q][0:c, :]
                                            ).then_inc(s_r["yev"], 1)

                    expert(0, 0, True)
                    expert(1, 0, True)
                    with dve.Fori(1, last_pair + 1) as i:
                        expert(0, i, False)
                        expert(1, i, False)

            with ExitStack() as cw, nc.Block() as block:
                lo = sb("lo", [P, NT, TOPK], c=cw)
                gw = sb("gw", [P, NT, TOPK], c=cw)
                at8 = sb("at8", [P, NT, TOPK], I32, cw)
                back = sb("back", [P, 4, D], c=cw)
                rounds = [(t, i) for t in range(NT) for i in range(TOPK)]

                @block.gpsimd
                def _(pool):
                    pool.wait_ge(s_r["idx"], 1)
                    for n, (t, i) in enumerate(rounds):
                        if n >= 4:
                            pool.wait_ge(s_r["comb"], n - 3)
                        pool.indirect_dma_start(back[0:rows(t), n % 4, :], None, rows_out,
                                                bass.IndirectOffsetOnAxis(ap=at8[0:rows(t), t, i:i + 1], axis=0)
                                                ).then_inc(s_yb[n % 4], 16)

                @block.vector
                def _(dve):
                    dve.tensor_scalar(lo[:], rel8[:], 0.0, None, ALU.is_ge)
                    dve.tensor_scalar(gw[:], rel8[:], float(CAP), None, ALU.is_lt).then_inc(s_r["seen"], 1)
                    dve.wait_ge(s_r["seen"], 1)
                    dve.tensor_tensor(gw[:], gw[:], lo[:], ALU.mult).then_inc(s_r["seen"], 1)
                    dve.wait_ge(s_r["seen"], 2)
                    dve.tensor_scalar(lo[:], rel8[:], 0.0, float(CAP - 1), ALU.max, ALU.min)
                    dve.tensor_tensor(gw[:], gw[:], gate8[:], ALU.mult).then_inc(s_r["seen"], 1)
                    dve.wait_ge(s_r["seen"], 3)
                    dve.tensor_tensor(at8[:], lo[:], exp8[:], ALU.add).then_inc(s_r["idx"], 1)
                    dve.tensor_scalar(rel8[:], rel8[:], float(CAP), None, ALU.subtract).then_inc(s_r["seen"], 1)
                    for n, (t, i) in enumerate(rounds):
                        dve.wait_ge(s_yb[n % 4], 16 * (n // 4 + 1))
                        if n:
                            dve.wait_ge(s_r["comb"], n)
                        rr = rows(t)
                        dve.scalar_tensor_tensor(acc[0:rr, t, :], back[0:rr, n % 4, :], gw[0:rr, t, i:i + 1],
                                                 acc[0:rr, t, :], ALU.mult, ALU.add).then_inc(s_r["comb"], 1)
                    dve.wait_ge(s_r["comb"], len(rounds))

            with nc.Block() as block:
                @block.sync
                def _(sp):
                    for s in everything:
                        sp.sem_clear(s)
            nc.all_engine_barrier()

        s_f = {x: sem("s_last_" + x) for x in ("ln", "st", "ve", "rs", "nb", "z", "y", "out")}
        with ExitStack() as cw, nc.Block() as block:
            lng = sb("ln2g", [P, D], c=cw)
            lnb = sb("ln2b", [P, D], c=cw)
            st = sb("st2", [P, 2, 6], c=cw)
            mv = sb("mv2", [P, NT, 4], c=cw)

            @block.sync
            def _(sp):
                sp.dma_start(lng[:], a["ln2_g"].broadcast_to([P, D])).then_inc(s_f["ln"], 16)
                sp.dma_start(lnb[:], a["ln2_b"].broadcast_to([P, D])).then_inc(s_f["ln"], 16)
                y_p = a["y_prompt"].rearrange("b t d -> (b t) d")
                y_s = a["y_sample"].rearrange("b t d -> (b t) d")
                for t in range(NT):
                    sp.wait_ge(s_f["y"], t + 1)
                    sp.dma_start(k.token_rows(y_p, y_s, t), acc[0:rows(t), t, :]).then_inc(s_f["out"], 16)
                sp.wait_ge(s_f["out"], 16 * NT)

            @block.gpsimd
            def _(pool):
                for t in range(NT):
                    pool.wait_ge(s_f["ve"], t + 1)
                    pool.tensor_tensor(mv[0:rows(t), t, 2:3], mv[0:rows(t), t, 1:2], k.neghalf[0:rows(t), 0:1],
                                       ALU.pow).then_inc(s_f["rs"], 1)

            @block.scalar
            def _(act):
                for t in range(NT):
                    act.wait_ge(s_f["nb"], t + 1)
                    r = rows(t)
                    act.activation(acc[0:r, t, :], acc[0:r, t, :], ACT.Identity, bias=mv[0:r, t, 3:4],
                                   scale=mv[0:r, t, 2:3]).then_inc(s_f["z"], 1)

            @block.vector
            def _(dve):
                n = 0

                def step(ins):
                    nonlocal n
                    n += 1
                    ins.then_inc(s_f["st"], 1)
                    dve.wait_ge(s_f["st"], n)

                def gain(t):
                    v, r = acc[0:rows(t), t, :], rows(t)
                    dve.wait_ge(s_f["z"], t + 1)
                    step(dve.tensor_tensor(v, v, lng[0:r, :], ALU.mult))
                    dve.tensor_tensor(v, v, lnb[0:r, :], ALU.add).then_inc(s_f["y"], 1)

                for t in range(NT):
                    v, r = acc[0:rows(t), t, :], rows(t)
                    for i in range(2):
                        last = dve.bn_stats(st[0:r, i, :], acc[0:r, t, 512 * i:512 * i + 512])
                    step(last)
                    step(dve.bn_aggr(mv[0:r, t, 0:2], st[0:r]))
                    dve.tensor_scalar(mv[0:r, t, 1:2], mv[0:r, t, 1:2], EPS, None, ALU.add).then_inc(s_f["ve"], 1)
                    if t == 0:
                        dve.wait_ge(s_f["ln"], 32)
                    else:
                        gain(t - 1)
                    dve.wait_ge(s_f["rs"], t + 1)
                    dve.scalar_tensor_tensor(mv[0:r, t, 3:4], mv[0:r, t, 0:1], -1.0, mv[0:r, t, 2:3], ALU.mult,
                                             ALU.mult).then_inc(s_f["nb"], 1)
                gain(NT - 1)


OUTS = (("y_prompt", (1, SEQ, D)), ("y_sample", (NB, NS, D)),
        ("k_prompt", (1, 1, SEQ, BKV, BD)), ("k_sample", (1, NB, NS, BKV, BD)),
        ("v_prompt", (1, 1, SEQ, BKV, BD)), ("v_sample", (1, NB, NS, BKV, BD)),
        ("kidx_prompt", (1, 1, SEQ, BD)), ("kidx_sample", (1, NB, NS, BD)),
        ("C_prompt", (1, 1, H, HD, HD)), ("C_sample", (1, NB, H, HD, HD)),
        ("n_prompt", (1, 1, H, HD)), ("n_sample", (1, NB, H, HD)),
        ("m_prompt", (1, 1, H)), ("m_sample", (1, NB, H)),
        ("pool_prompt", (1, 1, POOLB, 512)), ("pool_sample", (1, NB, POOLB, 512)))


def kernel(**inputs):
    import concourse.bacc as bacc
    from concourse.bass_utils import run_bass_kernel_spmd

    nc = bacc.Bacc("TRN2", target_bir_lowering=False, num_devices=1)
    arrays, io = {}, {}
    for name, value in inputs.items():
        arrays[f"in_{name}"] = np.ascontiguousarray(value)
        io[name] = nc.dram_tensor(f"in_{name}", arrays[f"in_{name}"].shape,
                                  mybir.dt.from_np(arrays[f"in_{name}"].dtype), kind="ExternalInput").ap()
    for name, shape in OUTS:
        io[name] = nc.dram_tensor(f"out_{name}", shape, F32, kind="ExternalOutput").ap()
    build(nc, io)
    r = run_bass_kernel_spmd(nc, [arrays], core_ids=[0])
    return tuple(r.results[0][f"out_{name}"] for name, _ in OUTS)
```

```python
from contextlib import ExitStack

import numpy as np

import concourse.bass as bass
from concourse import mybir

F32 = mybir.dt.float32
I32 = mybir.dt.int32
U32 = mybir.dt.uint32
F32R = mybir.dt.float32r
ALU = mybir.AluOpType
ACT = mybir.ActivationFunctionType
AX = mybir.AxisListType.X

P = 128
D = 1024
KT = D // P
SEQ = 1024
NB, NS = 8, 8
SM = NB * NS
N = SEQ + SM
NT = -(-N // P)
H, HD = 4, 128
NCH = SEQ // P
BH, BKV, BD = 8, 2, 64
KEEP = 256
PG = 128
NPG = 8
NPOOL = 80
PAST = PG * NPG
NK = PAST + SM
WINDOWS = (2, 4, 8, 16)
POOLB = 15
E, EG, TOPG, TOPK = 64, 8, 4, 8
F = 256
CAP = 176
ROUNDS = -(-N // CAP)
ECAP = ROUNDS * CAP
SHIFT = 11
ALPHA = 2 ** 0.25
EPS = 1e-5
BIG = 1e30
GONE = -3e38

OFF = {}
_at = 0
for _n, _w in (("q", 512), ("k", 512), ("v", 512), ("i", 4), ("f", 4), ("o", 512), ("bq", 512), ("bk", 128),
               ("bv", 128), ("iq", 512), ("ik", 64), ("iw", 8), ("u", 512), ("ga", D), ("gb", D), ("gc", D)):
    OFF[_n] = _at
    _at += _w
IN_W = _at
TOKEN_CHUNKS = ((0, 512), (512, 512), (1024, 64))
BC = {"q": 0, "k": 4, "bq": 8, "bk": 12, "ik": 13, "iq": 14, "u": 18, "g": 22, "i": 46, "f": 47, "ff": 48}
NBC = 49
ASIDE = 4 + 3 * D // P
EARLY, LATE = 3, 5


def rows(t):
    return min(P, N - t * P)


class Core:
    pass


def build(nc, a):
    ds = bass.ds
    ctx = ExitStack()
    with ctx:
        ctx.enter_context(nc.allow_non_contiguous_dma(reason="biases, stabilisers: a few KB"))
        live = []

        def sem(name):
            live.append(nc.alloc_semaphore(name))
            return live[-1]

        def renew():
            nc.clear_and_free_semaphores(live)
            nc.all_engine_barrier()
            live.clear()

        def sb(name, shape, dt=F32, c=ctx):
            return c.enter_context(nc.sbuf_tensor(name, shape, dt))

        banks = ctx.enter_context(nc.psum_tensor("banks", [P, 8, 512], F32))
        ps = [banks[:, i, :] for i in range(8)]

        x_p = a["x_prompt"].rearrange("b t d -> (b t) d")
        x_s = a["x_sample"].rearrange("b t d -> (b t) d")
        w_in = a["w_in"][0].rearrange("(k p) n -> p k n", p=P)
        b_in = a["b_in"]

        def token_rows(prompt, sample, t):
            return prompt[t * P:(t + 1) * P] if t < NCH else sample

        mixer = ExitStack()
        ident = sb("ident", [P, P])
        ones = sb("ones", [P, P])
        causalT = sb("causalT", [P, P])
        sampleT = sb("sampleT", [SM, SM])
        sampleQ = sb("sampleQ", [SM, SM])
        own = sb("own", [SM, NB])
        before = sb("before", [P, P])
        pick = sb("pick", [H, H, P])
        neghalf = sb("neghalf", [P, H])
        xT = sb("xT", [P, KT, N])
        hT = sb("hT", [P, 12, N], c=mixer)
        biasc = sb("biasc", [P, NBC], c=mixer)
        biasr = sb("biasr", [1, 512 + 512 + 256 + 72], c=mixer)
        s_const = sem("s_const")
        s_bias = sem("s_bias")

        s_x = [sem(f"s_x{i}") for i in range(3)]
        first_w = hT[:, 0:4, :].rearrange("p a n -> p (a n)")
        w_q = first_w[:, 0:KT * 512].rearrange("p (k c) -> p k c", k=KT)
        w_if = first_w[:, KT * 512:KT * 520].rearrange("p (k c) -> p k c", k=KT)
        s_wq, s_wif = sem("s_wq"), sem("s_wif")
        s_xps = sem("s_xps")
        s_xev_act, s_xev_dve = sem("s_xev_act"), sem("s_xev_dve")
        n_bias_dmas = 17
        with ExitStack() as c0, nc.Block() as block:
            xin = sb("xin", [P, 3, D], c=c0)

            @block.sync
            def _(sp):
                def biases():
                    def column(at, off, count):
                        src = b_in[0, off:off + P * count].rearrange("(c p) -> p c", p=P)
                        sp.dma_start(biasc[:, at:at + count], src).then_inc(s_bias, 16)

                    column(BC["q"], OFF["q"], 4)
                    column(BC["k"], OFF["k"], 4)
                    for g in range(BKV):
                        src = b_in[0, OFF["bq"] + 256 * g:OFF["bq"] + 256 * (g + 1)].rearrange("(c p) -> p c", p=BD)
                        sp.dma_start(biasc[64 * g:64 * g + 64, BC["bq"]:BC["bq"] + 4], src).then_inc(s_bias, 16)
                        src = b_in[0:1, OFF["ik"]:OFF["ik"] + 64].rearrange("a p -> p a")
                        sp.dma_start(biasc[64 * g:64 * g + 64, BC["ik"]:BC["ik"] + 1], src).then_inc(s_bias, 16)
                    column(BC["bk"], OFF["bk"], 1)
                    column(BC["iq"], OFF["iq"], 4)
                    column(BC["u"], OFF["u"], 4)
                    column(BC["g"], OFF["ga"], 24)
                    for name in "if":
                        src = b_in[0:1, OFF[name]:OFF[name] + H].rearrange("a p -> p a")
                        sp.dma_start(biasc[0:H, BC[name]:BC[name] + 1], src).then_inc(s_bias, 16)
                    sp.dma_start(biasc[0:H, BC["ff"]:BC["ff"] + 1], a["b_fgate"].rearrange("a p -> p a")).then_inc(s_bias, 16)
                    sp.dma_start(biasr[:, 0:512], b_in[:, OFF["v"]:OFF["v"] + 512]).then_inc(s_bias, 16)
                    sp.dma_start(biasr[:, 512:1024], b_in[:, OFF["o"]:OFF["o"] + 512]).then_inc(s_bias, 16)
                    sp.dma_start(biasr[:, 1024:1096], b_in[:, OFF["ik"]:OFF["ik"] + 72]).then_inc(s_bias, 16)
                    sp.dma_start(biasr[:, 1096:1352], b_in[:, OFF["bk"]:OFF["bk"] + 256]).then_inc(s_bias, 16)

                for t in range(NT):
                    if t == 3:
                        biases()
                    if t >= 3:
                        sp.wait_ge(s_xps, 2 * (t - 2))
                    sp.dma_start(xin[0:rows(t), t % 3, :], token_rows(x_p, x_s, t)).then_inc(s_x[t % 3], 16)
                sp.dma_start(w_if, w_in[:, :, OFF["i"]:OFF["i"] + 8]).then_inc(s_wif, 16)
                sp.dma_start(w_q, w_in[:, :, OFF["q"]:OFF["q"] + 512]).then_inc(s_wq, 16)
                sp.wait_ge(s_bias, 16 * n_bias_dmas)

            @block.gpsimd
            def _(pool):
                n = 0

                def step(ins):
                    nonlocal n
                    n += 1
                    ins.then_inc(s_const, 1)

                for m, v in ((ident, 0.0), (ones, 1.0), (causalT, 1.0), (sampleT, 1.0), (sampleQ, 1.0), (own, 1.0),
                             (before, 1.0), (pick, 1.0), (neghalf, -0.5)):
                    step(pool.memset(m[:], v))
                pool.wait_ge(s_const, n)
                step(pool.affine_select(out=ident[:], in_=ident[:], compare_op=ALU.not_equal, fill=1.0, base=0,
                                        pattern=[[-1, P]], channel_multiplier=1))
                step(pool.affine_select(out=causalT[:], in_=causalT[:], compare_op=ALU.is_ge, fill=0.0, base=0,
                                        pattern=[[1, P]], channel_multiplier=-1))
                step(pool.affine_select(out=before[:], in_=before[:], compare_op=ALU.is_ge, fill=0.0, base=-1,
                                        pattern=[[1, P]], channel_multiplier=-1))
                step(pool.affine_select(out=pick[:], in_=pick[:], compare_op=ALU.is_equal, fill=0.0, base=0,
                                        pattern=[[-1, H], [0, P]], channel_multiplier=1))
                s3 = sampleT[:].rearrange("s (b j) -> s b j", j=NS)
                step(pool.affine_select(out=s3, in_=s3, compare_op=ALU.is_ge, fill=0.0, base=0,
                                        pattern=[[-NS, NB], [0, NS]], channel_multiplier=1))
                q3 = sampleQ[:].rearrange("t (b j) -> t b j", j=NS)
                step(pool.affine_select(out=q3, in_=q3, compare_op=ALU.is_ge, fill=0.0, base=0,
                                        pattern=[[-NS, NB], [-1, NS]], channel_multiplier=1))
                step(pool.affine_select(out=own[:], in_=own[:], compare_op=ALU.is_ge, fill=0.0, base=0,
                                        pattern=[[-NS, NB]], channel_multiplier=1))
                pool.wait_ge(s_const, n)
                step(pool.affine_select(out=s3, in_=s3, compare_op=ALU.is_ge, fill=0.0, base=0,
                                        pattern=[[NS, NB], [1, NS]], channel_multiplier=-1))
                step(pool.affine_select(out=q3, in_=q3, compare_op=ALU.is_ge, fill=0.0, base=NS - 1,
                                        pattern=[[NS, NB], [0, NS]], channel_multiplier=-1))
                step(pool.affine_select(out=own[:], in_=own[:], compare_op=ALU.is_ge, fill=0.0, base=NS - 1,
                                        pattern=[[NS, NB]], channel_multiplier=-1))

                pool.wait_ge(s_const, n)

            @block.tensor
            def _(pe):
                pe.wait_ge(s_const, 10)
                for t in range(NT):
                    pe.wait_ge(s_x[t % 3], 16 * (t // 3 + 1))
                    for h in range(2):
                        j = 2 * t + h
                        if j >= 8:
                            pe.wait_ge((s_xev_act, s_xev_dve)[h], t - 3)
                        for k in range(4):
                            last = pe.transpose(ps[j % 8][:, k * P:k * P + rows(t)],
                                                xin[0:rows(t), t % 3, (4 * h + k) * P:(4 * h + k + 1) * P],
                                                ident[0:rows(t), 0:rows(t)])
                        last.then_inc(s_xps, 1)

            def spread(h, t):
                return (xT[:, 4 * h:4 * h + 4, t * P:t * P + rows(t)],
                        ps[(2 * t + h) % 8].rearrange("p (k n) -> p k n", k=4)[:, :, 0:rows(t)])

            @block.scalar
            def _(act):
                for t in range(NT):
                    act.wait_ge(s_xps, 2 * t + 1)
                    act.copy(*spread(0, t)).then_inc(s_xev_act, 1)

            @block.vector
            def _(dve):
                for t in range(NT):
                    dve.wait_ge(s_xps, 2 * t + 2)
                    dve.tensor_copy(*spread(1, t)).then_inc(s_xev_dve, 1)

        k = Core()
        k.banks = banks
        k.ps, k.w_in, k.x_p, k.x_s, k.token_rows, k.sem, k.sb = ps, w_in, x_p, x_s, token_rows, sem, sb
        k.ident, k.ones, k.causalT, k.sampleT, k.sampleQ, k.own = ident, ones, causalT, sampleT, sampleQ, own
        k.before, k.pick, k.neghalf = before, pick, neghalf
        k.xT, k.hT, k.biasc, k.biasr = xT, hT, biasc, biasr
        k.w_q, k.w_if, k.s_wq, k.s_wif = w_q, w_if, s_wq, s_wif
        k.aside = nc.dram_tensor("u_and_gates", (ASIDE, P, N), F32, kind="Internal").ap()
        build_mlstm(nc, a, k)
        renew()
        build_attention(nc, a, k)
        renew()
        build_pooling(nc, a, k)
        build_merge(nc, a, k)
        renew()
        mixer.close()
        build_moe(nc, a, k)


def product(pe, bank, mt, left, right, count, bias=None):
    n = count + (bias is not None)
    for k in range(count):
        last = pe.matmul(bank, left(k), right(k), start=(k == 0), stop=(k == n - 1))
    if bias is not None:
        last = pe.matmul(bank, bias[0], bias[1], start=(n == 1), stop=True)
    return last


def split_product(pe, bank, left, right, count):
    for k in range(count):
        (lh, ll), (rh, rl) = left(k), right(k)
        pe.matmul(bank, lh, rh, start=(k == 0), stop=False)
        pe.matmul(bank, lh, rl, start=False, stop=False)
        last = pe.matmul(bank, ll, rh, start=False, stop=(k == count - 1))
    return last


def banks_before(jobs, engine, j):
    return sum(job[-1] == engine for job in jobs[:j])


def build_mlstm(nc, a, k):
    ps, ident, ones, xT, hT, biasc, biasr, sem = k.ps, k.ident, k.ones, k.xT, k.hT, k.biasc, k.biasr, k.sem
    out_c, out_n, out_m = a["C_prompt"], a["n_prompt"], a["m_prompt"]
    outs_c, outs_n, outs_m = a["C_sample"], a["n_sample"], a["m_sample"]
    with ExitStack() as ca:
        def sb(name, shape, dt=F32, c=ca):
            return k.sb(name, shape, dt, c)

        qT = sb("qT", [P, H, N])
        kT = sb("kT", [P, H, N])
        vaug = sb("vaug", [P, NT, H, HD + 1])
        gate_o = sb("gate_o", [P, NT, H * HD])

        groups = ["q", "k", "v", "o"]
        jobs = [("row", name, n0, nn, "act") for name in "if" for n0, nn in TOKEN_CHUNKS]
        for name, eng in (("q", "act"), ("k", "dve")):
            jobs += [(name, ct, n0, nn, eng) for ct in range(4) for n0, nn in TOKEN_CHUNKS]
        jobs += [("v", t, "dve") for t in range(NT)] + [("o", t, "act") for t in range(NT)]
        row = {n: hT[0:H, 4 + i, :] for i, n in enumerate(("li", "f", "t", "g", "gm", "m", "wi", "en"))}
        keep = sb("keep", [H, N])
        mp = sb("mp", [H, NCH + NB])
        decay = sb("decay", [H, NCH + NB])
        mend = sb("mend", [H, NCH + NB])
        s_wg = [k.s_wq] + [sem("s_project_w" + x) for x in "kvo"]
        s_gfree = sem("s_gfree")
        s_full, s_out_act, s_out_dve = sem("s_full"), sem("s_out_act"), sem("s_out_dve")
        s_gain, s_ones_v, s_og, s_gscale = sem("s_gain"), sem("s_ones_v"), sem("s_og"), sem("s_gscale")
        s_rowd, s_rowa, s_mst, s_mout = sem("s_rowd"), sem("s_rowa"), sem("s_mst"), sem("s_mout")
        with ExitStack() as cw, nc.Block() as block:
            w = sb("w_groups", [P, 2, KT, 512], c=cw)
            w_of = [k.w_q, w[:, 0], w[:, 1], w[:, 0]]
            wif = k.w_if
            gain = sb("gain", [P, H * HD], c=cw)

            @block.sync
            def _(sp):
                for g in (1, 2, 3):
                    if g == 3:
                        sp.wait_ge(s_gfree, 2)
                    at = OFF[groups[g]]
                    sp.dma_start(w_of[g], k.w_in[:, :, at:at + 512]).then_inc(s_wg[g], 16)
                    if g == 2:
                        sp.dma_start(gain[:], a["a_norm_g"].broadcast_to([P, H * HD])).then_inc(s_gain, 16)
                        sp.dma_start(mp[:, NCH:], a["state_m"][0].rearrange("b h -> h b")).then_inc(s_mst, 16)
                sp.wait_ge(s_rowd, 16)
                sp.dma_start(out_m[0].rearrange("b h -> h b"), mend[:, NCH - 1:NCH]).then_inc(s_mout, 16)
                sp.dma_start(outs_m[0].rearrange("b h -> h b"), mend[:, NCH:]).then_inc(s_mout, 16)
                sp.wait_ge(s_mout, 32)

            @block.tensor
            def _(pe):
                pe.wait_ge(k.s_wif, 16)
                for j, job in enumerate(jobs):
                    if j >= 8:
                        eng = jobs[j - 8][-1]
                        pe.wait_ge({"act": s_out_act, "dve": s_out_dve}[eng], banks_before(jobs, eng, j - 7))
                    bank = ps[j % 8]
                    if job[0] == "row":
                        _, name, n0, nn, _ = job
                        c0 = 0 if name == "i" else 4
                        last = product(pe, bank[0:H, 0:nn], H, lambda kt: wif[:, kt, c0:c0 + H],
                                       lambda kt: xT[:, kt, n0:n0 + nn], KT)
                    elif job[0] in ("q", "k"):
                        name, ct, n0, nn, _ = job
                        g = groups.index(name)
                        if ct == 0 and n0 == 0:
                            pe.wait_ge(s_wg[g], 16)
                        last = product(pe, bank[:, 0:nn], P, lambda kt: w_of[g][:, kt, ct * P:(ct + 1) * P],
                                       lambda kt: xT[:, kt, n0:n0 + nn], KT)
                    else:
                        name, t, _ = job
                        g = groups.index(name)
                        if t == 0:
                            pe.wait_ge(s_wg[g], 16)
                        r, b0 = rows(t), 0 if name == "v" else 512
                        last = product(pe, bank[0:r, :], r, lambda kt: xT[:, kt, t * P:t * P + r],
                                       lambda kt: w_of[g][:, kt, :], KT, (ones[0:1, 0:r], biasr[:, b0:b0 + 512]))
                    last.then_inc(s_full, 1)
                    if job[0] in groups and (j + 1 == len(jobs) or jobs[j + 1][0] != job[0]):
                        pe.wait_ge(s_full, j + 1)
                        pe.sem_inc(s_gfree, 1)

            @block.scalar
            def _(act):
                for j, job in enumerate(jobs):
                    if job[-1] != "act":
                        continue
                    act.wait_ge(s_full, j + 1)
                    bank = ps[j % 8]
                    if job[0] == "row":
                        _, name, n0, nn, _ = job
                        act.activation(row["li" if name == "i" else "f"][:, n0:n0 + nn], bank[0:H, 0:nn], ACT.Identity,
                                       bias=biasc[0:H, BC[name]:BC[name] + 1]).then_inc(s_out_act, 1)
                    elif job[0] == "q":
                        _, ct, n0, nn, _ = job
                        act.activation(qT[:, ct, n0:n0 + nn], bank[:, 0:nn], ACT.Identity,
                                       bias=biasc[:, BC["q"] + ct:BC["q"] + ct + 1]).then_inc(s_out_act, 1)
                    else:
                        t = job[1]
                        act.activation(gate_o[0:rows(t), t, :], bank[0:rows(t), :], ACT.Sigmoid).then_inc(s_out_act, 1)
                    if j == 5:
                        act.wait_ge(s_rowd, 2)
                        act.activation(row["t"], row["t"], ACT.Exp, scale=-1.0).then_inc(s_rowa, 1)
                        act.wait_ge(s_rowd, 3)
                        act.activation(row["t"], row["t"], ACT.Ln).then_inc(s_rowa, 1)
                        act.wait_ge(s_rowd, 15)
                        act.activation(row["wi"], row["wi"], ACT.Exp).then_inc(s_rowa, 1)
                        act.activation(row["en"], row["en"], ACT.Exp, scale=-1.0).then_inc(s_rowa, 1)
                        act.activation(row["gm"], row["gm"], ACT.Exp).then_inc(s_rowa, 1)
                        act.activation(decay[:], decay[:], ACT.Exp).then_inc(s_rowa, 1)

            @block.gpsimd
            def _(pool):
                pool.memset(vaug[:, :, :, HD:HD + 1], 1.0).then_inc(s_ones_v, 1)
                pool.wait_ge(s_gain, 16)
                for t in range(NT):
                    j = [i for i, job in enumerate(jobs) if job[0] == "o"][t]
                    pool.wait_ge(s_out_act, banks_before(jobs, "act", j + 1))
                    g = gate_o[0:rows(t), t, :]
                    pool.tensor_tensor(g, g, gain[0:rows(t), :], ALU.mult).then_inc(s_og, 1)
                pool.wait_ge(s_og, NT)
                pool.wait_ge(s_ones_v, 1)

            @block.vector
            def _(dve):
                n = 0

                def step(ins):
                    nonlocal n
                    n += 1
                    ins.then_inc(s_rowd, 1)
                    dve.wait_ge(s_rowd, n)

                R = row
                starts = keep[:, 0:SEQ].rearrange("h (c t) -> h c t", t=P)[:, :, 0:1]
                starts_s = keep[:, SEQ:].rearrange("h (b t) -> h b t", t=NS)[:, :, 0:1]

                def last_of(r):
                    return (r[:, 0:SEQ].rearrange("h (c t) -> h c t", t=P)[:, :, P - 1:P],
                            r[:, SEQ:].rearrange("h (b t) -> h b t", t=NS)[:, :, NS - 1:NS])

                def first_of(r):
                    return (r[:, 0:SEQ].rearrange("h (c t) -> h c t", t=P)[:, :, 0:1],
                            r[:, SEQ:].rearrange("h (b t) -> h b t", t=NS)[:, :, 0:1])

                def cut(r):
                    return (r[:, 0:SEQ].rearrange("h (c t) -> h c t", t=P),
                            r[:, SEQ:].rearrange("h (b t) -> h b t", t=NS))

                def each(r, c0, c1, n_):
                    return r[:, c0:c1].unsqueeze(2).to_broadcast([H, c1 - c0, n_])

                dve.memset(keep[:], 1.0)
                dve.wait_ge(s_out_act, 6)
                dve.wait_ge(s_mst, 16)
                step(dve.tensor_scalar(R["f"], R["f"], biasc[0:H, BC["ff"]:BC["ff"] + 1], None, ALU.add))
                dve.memset(starts, 0.0)
                dve.memset(starts_s, 0.0)
                step(dve.scalar_tensor_tensor(R["t"], R["f"], -1.0, R["f"], ALU.mult, ALU.max))
                dve.wait_ge(s_rowa, 1)
                step(dve.tensor_scalar(R["t"], R["t"], 1.0, None, ALU.add))
                dve.wait_ge(s_rowa, 2)
                step(dve.scalar_tensor_tensor(R["f"], R["f"], 0.0, R["t"], ALU.min, ALU.subtract))
                step(dve.tensor_tensor_scan(R["t"], keep[:], R["f"], 0.0, ALU.mult, ALU.add))
                step(dve.tensor_tensor(R["g"], R["li"], R["t"], ALU.subtract))
                dve.tensor_copy(R["gm"], R["g"])
                step(dve.memset(R["f"], 0.0))
                fp, fs = first_of(R["gm"])
                dve.tensor_tensor(fs, fs, mp[:, NCH:].unsqueeze(2), ALU.max)
                bp, _ = last_of(R["t"])
                dp, dsm = first_of(R["f"])
                dve.tensor_copy(dp[:, 1:NCH], bp[:, 0:NCH - 1])
                step(dve.memset(dsm, -BIG))
                step(dve.tensor_tensor_scan(R["m"], R["f"], R["gm"], -BIG, ALU.add, ALU.max))
                mlp, mls = last_of(R["m"])
                _, bs = last_of(R["t"])
                dve.tensor_tensor(mend[:, 0:NCH].unsqueeze(2), mlp, bp, ALU.add)
                dve.tensor_tensor(mend[:, NCH:].unsqueeze(2), mls, bs, ALU.add)
                dve.memset(mp[:, 0:1], -BIG)
                step(dve.tensor_tensor(R["en"], R["t"], R["m"], ALU.add))
                step(dve.tensor_copy(mp[:, 1:NCH], mend[:, 0:NCH - 1]))
                for c0, c1, n_, m3, w3, g3, s3, l3 in (
                        (0, NCH, P, cut(R["m"])[0], cut(R["wi"])[0], cut(R["g"])[0], cut(R["gm"])[0], mlp),
                        (NCH, NCH + NB, NS, cut(R["m"])[1], cut(R["wi"])[1], cut(R["g"])[1], cut(R["gm"])[1], mls)):
                    dve.tensor_tensor(w3, each(mp, c0, c1, n_), m3, ALU.subtract)
                    dve.tensor_tensor(s3, g3, l3.to_broadcast([H, c1 - c0, n_]), ALU.subtract)
                    step(dve.tensor_tensor(decay[:, c0:c1].unsqueeze(2), mp[:, c0:c1].unsqueeze(2), l3, ALU.subtract))
                step(dve.tensor_scalar(R["m"], R["m"], -1.0, None, ALU.mult))
                step(dve.tensor_copy(R["li"], R["m"]))
                step(dve.tensor_copy(mend[:], mend[:]))
                for j, job in enumerate(jobs):
                    if job[-1] != "dve":
                        continue
                    dve.wait_ge(s_full, j + 1)
                    bank = ps[j % 8]
                    if job[0] == "k":
                        _, ct, n0, nn, _ = job
                        dve.tensor_scalar(kT[:, ct, n0:n0 + nn], bank[:, 0:nn], biasc[:, BC["k"] + ct:BC["k"] + ct + 1],
                                          float(HD) ** -0.5, ALU.add, ALU.mult).then_inc(s_out_dve, 1)
                    else:
                        t = job[1]
                        dve.tensor_copy(vaug[0:rows(t), t, :, 0:HD],
                                        bank[0:rows(t), :].rearrange("p (h d) -> p h d", h=H)).then_inc(s_out_dve, 1)
                dve.wait_ge(s_rowa, 6)

        rows4 = ("g", "wi", "en", "gm")
        dma = sem("s_cst")
        (s_scores, s_cols, s_colsv, s_dlog, s_e, s_em, s_am, s_nums, s_inter, s_cupd, s_numd, s_ve, s_rs, s_ha,
         s_hps, s_hev, s_dec, s_decv, s_kw, s_kv, s_mlst, s_cout, s_c0) = (
            sem("s_" + x) for x in ("scores", "cols", "colsv", "dlog", "e", "em", "am", "nums", "inter", "cupd", "numd",
                                    "ve", "rs", "ha", "hps", "hev", "dec", "decv", "kw", "kv", "mlst", "cout", "c0"))
        s_mst2 = sem("s_chunk_step")
        side = [(ft, n0, nn) for ft in range(EARLY) for n0, nn in TOKEN_CHUNKS]
        s_ew, s_est = sem("s_early_w"), [sem("s_early_stored0"), sem("s_early_stored1")]
        s_efull, s_eout = sem("s_early_full"), sem("s_early_out")
        s_qm, s_nps, s_nev, s_nin = sem("s_qm"), sem("s_nps"), sem("s_nev"), sem("s_nin")
        with ExitStack() as cw, nc.Block() as block:
            cols = sb("cols", [P, NT, 4, H], c=cw)
            dbc = sb("dbc", [P, H, NCH + NB], c=cw)
            C = sb("C", [P, H, HD + 1], c=cw)
            Cs = sb("Cs", [P, NB, H, HD + 1], c=cw)
            nin = sb("nin", [NB * H, HD], c=cw)
            ncol = sb("ncol", [P, NB * H + H], c=cw)
            nout = sb("nout", [NB * H, 2, HD], c=cw)
            dl = sb("dl", [P, H, P], c=cw)
            ex = hT[:, 10, 0:512].rearrange("p (h t) -> p h t", h=H)
            em = hT[:, 10, 512:1024].rearrange("p (h t) -> p h t", h=H)
            am = sb("am", [P, H, P], c=cw)
            kw = sb("kw", [P, H, HD], c=cw)
            wsb = sb("wsb", [SM, H, NB], c=cw)
            kwb = sb("kwb", [SM, 2, H, HD], c=cw)
            qm = hT[:, 8:10, 0:H * NB * SM // 2].rearrange("p a (c b t) -> p a c b t", b=NB, t=SM)
            inter = sb("inter", [P, H, HD + 1], c=cw)
            num = sb("num", [P, H, HD + 1], c=cw)
            hv = sb("hv", [P, H, HD], c=cw)
            hc = hT[:, 11, 512:1024].rearrange("p (h t) -> p h t", h=H)
            sq = hT[:, 11, 0:512].rearrange("p (h t) -> p h t", h=H)
            ha = hT[:, 5, 0:512].rearrange("p (h t) -> p h t", h=H)
            side_w = hT[:, 7, 0:D].rearrange("p (k c) -> p k c", k=KT)
            side_y = hT[:, 6, 0:1024].rearrange("p (s c) -> p s c", s=2)
            den = sb("den", [P, H], c=cw)
            mu = sb("mu", [P, H], c=cw)
            ve = sb("ve", [P, H], c=cw)
            rs = sb("rs", [P, H], c=cw)

            def three_and_one(i, T):
                return [ps[3 + i][0:T, 129 * h:129 * h + 129] for h in range(3)] + [ps[6][0:T, 129 * i:129 * i + 129]]

            @block.sync
            def _(sp):
                sp.dma_start(nin[:], a["state_n"][0].rearrange("b h d -> (b h) d")).then_inc(s_nin, 16)
                for b in range(NB):
                    sp.dma_start(Cs[:, b, :, 0:HD], a["state_C"][0, b].rearrange("h k v -> k h v")).then_inc(dma, 16)

                def load(f):
                    at = OFF["u"] + f * P
                    sp.dma_start(side_w, k.w_in[:, :, at:at + P]).then_inc(s_ew, 16)

                def put_aside(u):
                    ft, n0, nn = side[u]
                    sp.wait_ge(s_eout, u + 1)
                    sp.dma_start(k.aside[ft, :, n0:n0 + nn], side_y[:, u % 2, 0:nn]).then_inc(s_est[u % 2], 16)
                    if u % 3 == 2 and u // 3 + 1 < EARLY:
                        load(u // 3 + 1)

                sp.wait_ge(s_cols, 1)
                load(0)
                for u in range(NT):
                    put_aside(u)
                sp.wait_ge(s_cupd, NCH)
                sp.dma_start(out_c[0, 0].rearrange("h k v -> k h v"), C[:, :, 0:HD]).then_inc(s_cout, 16)
                for b in range(NB):
                    if NT + b < len(side):
                        put_aside(NT + b)
                    sp.wait_ge(s_cupd, NCH + b + 1)
                    sp.dma_start(outs_c[0, b].rearrange("h k v -> k h v"), Cs[:, b, :, 0:HD]).then_inc(s_cout, 16)
                sp.wait_ge(s_nev, 2)
                sp.dma_start(outs_n[0].rearrange("b h d -> (b h) d"), nout[:, 0, :]).then_inc(s_cout, 16)
                sp.dma_start(out_n[0, 0], nout[0:H, 1, :]).then_inc(s_cout, 16)
                sp.wait_ge(s_cout, 16 * (NB + 3))
                for i, s in enumerate(s_est):
                    sp.wait_ge(s, 16 * ((len(side) + 1 - i) // 2))

            @block.tensor
            def _(pe):
                for t in range(NT):
                    for i, name in enumerate(rows4):
                        pe.transpose(ps[7][0:rows(t), (t * 4 + i) * H:(t * 4 + i + 1) * H],
                                     row[name][:, t * P:t * P + rows(t)], ident[0:H, 0:H])
                for h in range(H):
                    pe.matmul(ps[0][:, h * 16:h * 16 + 16], k.pick[:, h, :], decay[:], start=True, stop=True)
                pe.wait_ge(s_nin, 16)
                pe.transpose(ps[1][:, 0:NB * H], nin[:], ident[0:NB * H, 0:NB * H]).then_inc(s_cols, 1)
                pe.wait_ge(s_colsv, 1)

                def side_product(u):
                    (ft, n0, nn), f = side[u], u // 3
                    if n0 == 0:
                        pe.wait_ge(s_ew, 16 * (f + 1))
                    if u:
                        pe.wait_ge(s_eout, u)
                    product(pe, ps[7][:, 0:nn], P, lambda kt: side_w[:, kt, :],
                            lambda kt: xT[:, kt, n0:n0 + nn], KT).then_inc(s_efull, 1)

                def scores(c):
                    T, c0 = rows(c), c * P
                    if c:
                        pe.wait_ge(s_am, c)
                    if c >= 2:
                        pe.wait_ge(s_hev, c - 1)
                    for h in range(H):
                        pe.matmul(ps[0][0:T, h * T:(h + 1) * T], k.pick[:, h, 0:T], row["li"][:, c0:c0 + T],
                                  start=True, stop=True)
                    for h in range(H):
                        pe.matmul(ps[1][0:T, h * T:(h + 1) * T], kT[:, h, c0:c0 + T], qT[:, h, c0:c0 + T],
                                  start=True, stop=True)
                    for h in range(H):
                        last = pe.transpose(ps[2][0:T, h * HD:(h + 1) * HD], kT[:, h, c0:c0 + T], ident[:])
                    last.then_inc(s_scores, 1)

                scores(0)
                for c in range(NT):
                    T, c0 = rows(c), c * P
                    if c:
                        pe.wait_ge(s_numd, c)
                        pe.wait_ge(s_cupd, c)
                    else:
                        pe.wait_ge(s_c0, 1)
                    it, nt_, kv = (three_and_one(i, T) for i in range(3))
                    if c < NCH:
                        for h in range(H):
                            pe.matmul(it[h], qT[:, h, c0:c0 + T], C[:, h, :], start=True, stop=True)
                    else:
                        pe.wait_ge(s_qm, 1)
                        pe.wait_ge(dma, 16 * NB)
                        for h in range(H):
                            for b in range(NB):
                                pe.matmul(it[h], qm[:, h // 2, h % 2, b, :], Cs[:, b, h, :], start=(b == 0), stop=(b == NB - 1))
                    pe.wait_ge(s_am, c + 1)
                    for h in range(H):
                        last = pe.matmul(nt_[h], am[0:T, h, 0:T], vaug[0:T, c, h, :], start=True, stop=True)
                    if c < NCH:
                        kv = three_and_one(2, P)
                        for h in range(H):
                            last = pe.matmul(kv[h], kw[0:T, h, :], vaug[0:T, c, h, :], start=True, stop=True)
                    last.then_inc(s_nums, 1)
                    if c + 1 < NT:
                        scores(c + 1)
                    side_product(c)
                    pe.wait_ge(s_ha, c + 1)
                    for h in range(H):
                        last = pe.transpose(ps[2][:, h * T:(h + 1) * T], ha[0:T, h, :], ident[0:T, 0:T])
                    last.then_inc(s_hps, 1)
                for b in range(NB):
                    if NT + b < len(side):
                        side_product(NT + b)
                    pe.wait_ge(s_kw, b + 1)
                    if b:
                        pe.wait_ge(s_cupd, NCH + b)
                    else:
                        pe.wait_ge(s_am, NT)
                    for h in range(H):
                        last = pe.matmul(ps[h // 3][:, 129 * (h % 3):129 * (h % 3) + 129], kwb[:, b % 2, h, :],
                                         vaug[0:SM, NT - 1, h, :], start=True, stop=True)
                    last.then_inc(s_kv, 1)
                pe.wait_ge(s_mlst, 1)
                pe.wait_ge(s_hev, NT)
                pe.transpose(ps[2][0:NB * H, 0:P], ncol[:, 0:NB * H], ident[:])
                pe.transpose(ps[2][0:H, P:2 * P], ncol[:, NB * H:], ident[:]).then_inc(s_nps, 1)

            @block.scalar
            def _(act):
                def side_out(u):
                    ft, n0, nn = side[u]
                    act.wait_ge(s_efull, u + 1)
                    if u >= 2:
                        act.wait_ge(s_est[u % 2], 16 * (u // 2))
                    col = BC["u"] + ft
                    act.activation(side_y[:, u % 2, 0:nn], ps[7][:, 0:nn], ACT.Identity,
                                   bias=biasc[:, col:col + 1]).then_inc(s_eout, 1)

                def exps(c):
                    T = rows(c)
                    act.wait_ge(s_dlog, c + 1)
                    act.activation(ex[0:T, :, 0:T], dl[0:T, :, 0:T], ACT.Exp).then_inc(s_e, 1)

                exps(0)
                for c in range(NT):
                    T, c0 = rows(c), c * P
                    act.wait_ge(s_nums, c + 1)
                    it = three_and_one(0, T)
                    for h in range(H):
                        last = act.activation(inter[0:T, h, :], it[h], ACT.Copy, scale=cols[0:T, c, 1, h:h + 1])
                    last.then_inc(s_inter, 1)
                    if c + 1 < NT:
                        exps(c + 1)
                    side_out(c)
                    act.wait_ge(s_hps, c + 1)
                    act.copy(hT[:, 0:H, c0:c0 + T], ps[2][:, 0:H * T].rearrange("p (h t) -> p h t", h=H)).then_inc(s_hev, 1)
                for u in range(NT, len(side)):
                    side_out(u)

            @block.gpsimd
            def _(pool):
                def masked(c):
                    T = rows(c)
                    mask = k.causalT[0:T, 0:T] if c < NCH else k.sampleT[:]
                    pool.wait_ge(s_e, c + 1)
                    pool.tensor_tensor(em[0:T, :, 0:T], ex[0:T, :, 0:T], mask.unsqueeze(1).to_broadcast([T, H, T]),
                                       ALU.mult).then_inc(s_em, 1)

                masked(0)
                for c in range(NT):
                    T = rows(c)
                    if c + 1 < NT:
                        masked(c + 1)
                    pool.wait_ge(s_ve, c + 1)
                    pool.tensor_tensor(rs[0:T, :], ve[0:T, :], k.neghalf[0:T, :], ALU.pow).then_inc(s_rs, 1)

            @block.vector
            def _(dve):
                n = 0

                def step(ins):
                    nonlocal n
                    n += 1
                    ins.then_inc(s_mst2, 1)
                    dve.wait_ge(s_mst2, n)

                dve.memset(C[:], 0.0).then_inc(s_c0, 1)
                dve.wait_ge(s_cols, 1)
                dve.memset(hT[:, 8:10, 0:H * NB * SM // 2], 0.0).then_inc(s_c0, 1)
                dve.wait_ge(s_c0, 2)
                dve.tensor_copy(cols[:, 0:NCH], ps[7][:, 0:NCH * 16].rearrange("p (c i h) -> p c i h", c=NCH, i=4))
                dve.tensor_copy(cols[0:SM, NCH], ps[7][0:SM, NCH * 16:NT * 16].rearrange("p (i h) -> p i h", i=4))
                dve.tensor_copy(dbc[:], ps[0][:, 0:64].rearrange("p (h c) -> p h c", h=H))
                for h in range(H):
                    for b in range(NB):
                        dve.tensor_copy(qm[:, h // 2, h % 2, b, NS * b:NS * b + NS], qT[:, h, SEQ + NS * b:SEQ + NS * b + NS])
                step(dve.tensor_copy(Cs[:, :, :, HD:HD + 1],
                                     ps[1][:, 0:NB * H].rearrange("p (b h o) -> p b h o", b=NB, o=1)))
                dve.tensor_tensor(wsb[:], cols[0:SM, NCH, 3, :].unsqueeze(2).to_broadcast([SM, H, NB]),
                                  k.own[:].unsqueeze(1).to_broadcast([SM, H, NB]), ALU.mult).then_inc(s_qm, 1)
                dve.wait_ge(s_qm, 1)
                dve.sem_inc(s_colsv, 1)

                def weigh(c):
                    T = rows(c)
                    dve.wait_ge(s_scores, c + 1)
                    for h in range(H):
                        last = dve.tensor_scalar(dl[0:T, h, 0:T], ps[0][0:T, h * T:(h + 1) * T],
                                                 cols[0:T, c, 0, h:h + 1], 0.0, ALU.add, ALU.min)
                    last.then_inc(s_dlog, 1)
                    if c < NCH:
                        for h in range(H):
                            dve.tensor_scalar(kw[0:T, h, :], ps[2][0:T, h * HD:(h + 1) * HD], cols[0:T, c, 3, h:h + 1],
                                              None, ALU.mult)
                    else:
                        dve.tensor_copy(kw[0:T], ps[2][0:T, :].rearrange("p (h d) -> p h d", h=H))

                weigh(0)
                for c in range(NT):
                    T = rows(c)
                    dve.wait_ge(s_em, c + 1)
                    dve.tensor_tensor(am[0:T, :, 0:T], em[0:T, :, 0:T],
                                      ps[1][0:T, 0:H * T].rearrange("p (h t) -> p h t", h=H), ALU.mult).then_inc(s_am, 1)
                    dve.wait_ge(s_inter, c + 1)
                    if c < NCH:
                        kv = three_and_one(2, P)
                        for h in range(H):
                            last = dve.scalar_tensor_tensor(C[:, h, :], C[:, h, :], dbc[:, h, c:c + 1], kv[h],
                                                            ALU.mult, ALU.add)
                        last.then_inc(s_cupd, 1)
                    dve.tensor_tensor(num[0:T, 0:3, :], inter[0:T, 0:3, :],
                                      ps[4][0:T, 0:387].rearrange("p (h d) -> p h d", h=3), ALU.add)
                    step(dve.tensor_tensor(num[0:T, 3, :], inter[0:T, 3, :], ps[6][0:T, 129:258], ALU.add))
                    dsum = num[0:T, :, HD:HD + 1].rearrange("p h o -> p (h o)")
                    step(dve.scalar_tensor_tensor(den[0:T, :], dsum, -1.0, dsum, ALU.mult, ALU.max))
                    dve.sem_inc(s_numd, 1)
                    step(dve.tensor_tensor(den[0:T, :], den[0:T, :], cols[0:T, c, 2, :], ALU.max))
                    step(dve.reciprocal(den[0:T, :], den[0:T, :]))
                    step(dve.tensor_tensor(hv[0:T], num[0:T, :, 0:HD],
                                           den[0:T, :].unsqueeze(2).to_broadcast([T, H, HD]), ALU.mult))
                    if c + 1 < NT:
                        weigh(c + 1)
                    step(dve.tensor_reduce(mu[0:T, :], hv[0:T], AX, ALU.add))
                    step(dve.tensor_scalar(mu[0:T, :], mu[0:T, :], 1.0 / HD, None, ALU.mult))
                    step(dve.tensor_tensor(hc[0:T], hv[0:T], mu[0:T, :].unsqueeze(2).to_broadcast([T, H, HD]),
                                           ALU.subtract))
                    step(dve.tensor_tensor(sq[0:T], hc[0:T], hc[0:T], ALU.mult))
                    step(dve.tensor_reduce(ve[0:T, :], sq[0:T], AX, ALU.add))
                    if c:
                        dve.wait_ge(s_hps, c)
                    dve.tensor_scalar(ve[0:T, :], ve[0:T, :], 1.0 / HD, EPS, ALU.mult, ALU.add).then_inc(s_ve, 1)
                    step(dve.tensor_tensor(hc[0:T], hc[0:T], gate_o[0:T, c, :].rearrange("p (h d) -> p h d", h=H),
                                           ALU.mult))
                    dve.wait_ge(s_rs, c + 1)
                    dve.tensor_tensor(ha[0:T], hc[0:T], rs[0:T, :].unsqueeze(2).to_broadcast([T, H, HD]),
                                      ALU.mult).then_inc(s_ha, 1)
                for b in range(NB):
                    if b >= 2:
                        dve.wait_ge(s_kv, b - 1)
                    for h in range(H):
                        last = dve.tensor_scalar(kwb[:, b % 2, h, :], kw[0:SM, h, :], wsb[:, h, b:b + 1], None, ALU.mult)
                    last.then_inc(s_kw, 1)
                    dve.wait_ge(s_kv, b + 1)
                    for h in range(H):
                        last = dve.scalar_tensor_tensor(Cs[:, b, h, :], Cs[:, b, h, :], dbc[:, h, NCH + b:NCH + b + 1],
                                                        ps[h // 3][:, 129 * (h % 3):129 * (h % 3) + 129],
                                                        ALU.mult, ALU.add)
                    last.then_inc(s_cupd, 1)
                dve.wait_ge(s_cupd, NCH + NB)
                dve.tensor_copy(ncol[:, 0:NB * H].rearrange("p (b h o) -> p b h o", b=NB, o=1), Cs[:, :, :, HD:HD + 1])
                dve.tensor_copy(ncol[:, NB * H:].unsqueeze(2), C[:, :, HD:HD + 1]).then_inc(s_mlst, 1)
                dve.wait_ge(s_nps, 1)
                dve.tensor_copy(nout[:, 0, :], ps[2][0:NB * H, 0:P]).then_inc(s_nev, 1)
                dve.tensor_copy(nout[0:H, 1, :], ps[2][0:H, P:2 * P]).then_inc(s_nev, 1)


TK = {"ik": 0, "iw": 64, "k": 72, "v": 200}
TKW = 328


def build_attention(nc, a, k):
    ps, banks, ident, ones, xT, hT, biasc, biasr, sem = (k.ps, k.banks, k.ident, k.ones, k.xT, k.hT, k.biasc, k.biasr,
                                                        k.sem)
    with ExitStack() as ca:
        def sb(name, shape, dt=F32, c=ca):
            return k.sb(name, shape, dt, c)

        bqT = sb("bqT", [P, 4, N])
        iqT = sb("iqT", [P, 4, N])
        bkT = sb("bkT", [P, N])
        ikT = sb("ikT", [P, N])
        tok = sb("tok", [P, NT, TKW])

        jobs = [("tok", t, ("act", "dve")[t % 2]) for t in range(NT)]
        for name, cts in (("bk", 1), ("ik", 1), ("iq", 4), ("bq", 4)):
            jobs += [(name, ct, n0, nn, ("act", "dve")[(ct + (n0 > 0)) % 2]) for ct in range(cts)
                     for n0, nn in TOKEN_CHUNKS]
        dest = {"bk": lambda ct: bkT, "ik": lambda ct: ikT, "iq": lambda ct: iqT[:, ct], "bq": lambda ct: bqT[:, ct]}
        s_wk, s_wiq, s_wbq = sem("s_wk"), sem("s_wiq"), sem("s_wbq")
        s_full, s_out_act, s_out_dve, s_kvout = (sem("s_keys_" + x) for x in ("full", "out_act", "out_dve", "kvout"))
        with ExitStack() as cw, nc.Block() as block:
            wk = sb("w_keys", [P, KT, 64 + TKW], c=cw)
            wiq = sb("w_iq", [P, KT, 512], c=cw)
            wbq = sb("w_bq", [P, KT, 4, 2, BD], c=cw)

            @block.sync
            def _(sp):
                sp.dma_start(wk[:, :, 0:64], k.w_in[:, :, OFF["ik"]:OFF["ik"] + 64]).then_inc(s_wk, 16)
                sp.dma_start(wk[:, :, 64:136], k.w_in[:, :, OFF["ik"]:OFF["ik"] + 72]).then_inc(s_wk, 16)
                sp.dma_start(wk[:, :, 136:392], k.w_in[:, :, OFF["bk"]:OFF["bk"] + 256]).then_inc(s_wk, 16)
                sp.dma_start(wiq[:], k.w_in[:, :, OFF["iq"]:OFF["iq"] + 512]).then_inc(s_wiq, 16)
                for g in range(BKV):
                    for j in range(4):
                        at = OFF["bq"] + (4 * g + j) * BD
                        sp.dma_start(wbq[:, :, j, g, :], k.w_in[:, :, at:at + BD]).then_inc(s_wbq, 16)
                sp.wait_ge(s_out_act, banks_before(jobs, "act", NT))
                sp.wait_ge(s_out_dve, banks_before(jobs, "dve", NT))
                for out, name, w in (("kidx", "ik", BD), ("k", "k", 128), ("v", "v", 128)):
                    dst = a[out + "_prompt"][0, 0]
                    dst = dst if name == "ik" else dst.rearrange("t h d -> t (h d)")
                    sp.dma_start(dst.rearrange("(t p) c -> p t c", p=P),
                                 tok[:, 0:NCH, TK[name]:TK[name] + w]).then_inc(s_kvout, 16)
                    dst = a[out + "_sample"][0]
                    dst = dst.rearrange("b t c -> (b t) c" if name == "ik" else "b t h d -> (b t) (h d)")
                    sp.dma_start(dst, tok[0:SM, NCH, TK[name]:TK[name] + w]).then_inc(s_kvout, 16)
                sp.wait_ge(s_kvout, 16 * 6)

            @block.tensor
            def _(pe):
                for j, job in enumerate(jobs):
                    if j >= 8:
                        eng = jobs[j - 8][-1]
                        pe.wait_ge({"act": s_out_act, "dve": s_out_dve}[eng], banks_before(jobs, eng, j - 7))
                    if job[0] == "tok":
                        t = job[1]
                        if t == 0:
                            pe.wait_ge(s_wk, 48)
                        last = product(pe, ps[j % 8][0:rows(t), 0:TKW], P,
                                       lambda kt: xT[:, kt, t * P:t * P + rows(t)], lambda kt: wk[:, kt, 64:64 + TKW],
                                       KT, (ones[0:1, 0:rows(t)], biasr[:, 1024:1024 + TKW]))
                    else:
                        name, ct, n0, nn, _ = job
                        if name in ("iq", "bq") and ct == 0 and n0 == 0:
                            pe.wait_ge(s_wiq if name == "iq" else s_wbq, 16 if name == "iq" else 128)
                        left = {"bk": lambda kt: wk[:, kt, 136:264], "ik": lambda kt: wk[:, kt, 0:128],
                                "iq": lambda kt: wiq[:, kt, ct * P:(ct + 1) * P],
                                "bq": lambda kt: wbq[:, kt, ct, :, :].rearrange("p g d -> p (g d)")}[name]
                        last = product(pe, ps[j % 8][:, 0:nn], P, left, lambda kt: xT[:, kt, n0:n0 + nn], KT)
                    last.then_inc(s_full, 1)

            @block.scalar
            def _(act):
                for j, job in enumerate(jobs):
                    if job[-1] == "act":
                        act.wait_ge(s_full, j + 1)
                        if job[0] == "tok":
                            r, t = rows(job[1]), job[1]
                            act.copy(tok[0:r, t, :], ps[j % 8][0:r, 0:TKW]).then_inc(s_out_act, 1)
                        else:
                            name, ct, n0, nn, _ = job
                            act.activation(dest[name](ct)[:, n0:n0 + nn], ps[j % 8][:, 0:nn], ACT.Identity,
                                           bias=biasc[:, BC[name] + ct:BC[name] + ct + 1]).then_inc(s_out_act, 1)

            @block.vector
            def _(dve):
                for j, job in enumerate(jobs):
                    if job[-1] == "dve":
                        dve.wait_ge(s_full, j + 1)
                        if job[0] == "tok":
                            r, t = rows(job[1]), job[1]
                            dve.tensor_copy(tok[0:r, t, :], ps[j % 8][0:r, 0:TKW]).then_inc(s_out_dve, 1)
                        else:
                            name, ct, n0, nn, _ = job
                            dve.tensor_scalar(dest[name](ct)[:, n0:n0 + nn], ps[j % 8][:, 0:nn],
                                              biasc[:, BC[name] + ct:BC[name] + ct + 1], None, ALU.add).then_inc(s_out_dve, 1)

        attend_prompt(nc, a, k, sb, bqT, iqT, bkT, ikT, tok)
        attend_samples(nc, a, k, sb, bqT, iqT, bkT, ikT, tok)


def keep_best(dve, s_best, base, work, best, first=0, end=KEEP // 8):
    for r in range(first, end):
        dve.max(best, work).then_inc(s_best, 1)
        dve.wait_ge(s_best, base + 2 * r + 1)
        dve.match_replace(work, best, work, GONE).then_inc(s_best, 1)
        dve.wait_ge(s_best, base + 2 * r + 2)


def attend_prompt(nc, a, k, sb, bqT, iqT, bkT, ikT, tok):
    ps, banks, ident, hT, xT, biasc, sem = k.ps, k.banks, k.ident, k.hT, k.xT, k.biasc, k.sem
    units = []
    for i in range(NCH):
        if 2 <= i + 1 < NCH:
            units += [("dots", i + 1, h) for h in range(8)]
        units += [("logits", i, h) for h in range(8)]
    taker = {"dots": "act", "logits": "dve"}
    at = {u: n for n, u in enumerate(units)}

    def taken(n, eng):
        return sum(taker[u[0]] == eng for u in units[:n])

    side = [(ft, n0, nn) for ft in range(EARLY, ASIDE - LATE) for n0, nn in TOKEN_CHUNKS]
    side_count = (6, 6, 7, 8, 9, 10, 10, 4)
    assert sum(side_count) == len(side)

    def side_of(i, h):
        at = sum(side_count[:i])
        return range(at + side_count[i] * h // 8, at + side_count[i] * (h + 1) // 8)

    s_sw = [sem(f"s_side_w{i}") for i in range(3)]
    s_sst = [sem("s_side_stored0"), sem("s_side_stored1")]
    s_sfull, s_sout = sem("s_side_full"), sem("s_side_out")
    halves = [(i, h, q) for i in range(NCH) for h in range(8) for q in range(-(-(i + 1) // 4))]
    half_at = {x: n for n, x in enumerate(halves)}
    (s_wide, s_wide_act, s_wide_dve, s_acc, s_pen, s_mx, s_ex, s_pn, s_tp, s_pt, s_pv, s_hb, s_best, s_st, s_cst) = (
        sem("s_prompt_" + x) for x in ("wide", "wide_act", "wide_dve", "acc", "pen", "mx", "ex", "pn", "tp", "pt", "pv", "hb",
                                 "best", "st", "cst"))
    with ExitStack() as cw, nc.Block() as block:
        PT = sb("PT", [P, 2, NCH, 4 * P], c=cw)
        rl = sb("rl", [P, 2, SEQ], c=cw)
        lg = sb("lg", [P, 2, SEQ], c=cw)
        score = sb("score", [P, SEQ], c=cw)
        pen = sb("pen", [P, SEQ], c=cw)
        penc = sb("penc", [P, P], c=cw)
        wis = sb("wis", [P, NCH, 8], c=cw)
        best = sb("best", [P, 8], c=cw)
        mx = sb("mx", [P, 2], c=cw)
        nm = sb("nm", [P, 2], c=cw)
        sm = sb("sm", [P, 2], c=cw)
        rc = sb("rc", [P, 2], c=cw)

        spare = hT[:, 8:12, :].rearrange("p a n -> p (a n)")
        side_w = spare[:, 0:3 * D].rearrange("p (s k c) -> p s k c", s=3, k=KT)
        side_y = spare[:, 3 * D:4 * D].rearrange("p (s c) -> p s c", s=2)

        def wide(u, L):
            b = 2 * (at[u] % 2)
            return banks[:, b:b + 2, :].rearrange("p b n -> p (b n)")[:, 0:L]

        @block.sync
        def _(sp):
            for u, (ft, n0, nn) in enumerate(side):
                if n0 == 0:
                    for f in ([0, 1, 2] if u == 0 else [u // 3 + 2] if u // 3 + 2 < len(side) // 3 else []):
                        if f >= 3:
                            sp.wait_ge(s_sfull, 3 * (f - 2))
                        at = OFF["u"] + (EARLY + f) * P
                        sp.dma_start(side_w[:, f % 3], k.w_in[:, :, at:at + P]
                                     ).then_inc(s_sw[f % 3], 16)
                sp.wait_ge(s_sout, u + 1)
                sp.dma_start(k.aside[ft, :, n0:n0 + nn], side_y[:, u % 2, 0:nn]).then_inc(s_sst[u % 2], 16)
            for i, s in enumerate(s_sst):
                sp.wait_ge(s, 16 * ((len(side) + 1 - i) // 2))

        @block.gpsimd
        def _(pool):
            pool.memset(penc[:], 0.0).then_inc(s_cst, 1)
            pool.wait_ge(s_cst, 1)
            pool.affine_select(out=penc[:], in_=penc[:], compare_op=ALU.is_ge, fill=-BIG, base=0, pattern=[[-1, P]],
                               channel_multiplier=1).then_inc(s_cst, 1)

        @block.tensor
        def _(pe):
            def wide_product(u):
                kind, i, h = u
                n, L = at[u], (i + 1) * P
                if n >= 2:
                    eng = taker[units[n - 2][0]]
                    pe.wait_ge({"act": s_wide_act, "dve": s_wide_dve}[eng], taken(n - 1, eng))
                q, keys = (iqT, ikT) if kind == "dots" else (bqT, bkT)
                g, j = (h % 2, h // 2) if kind == "dots" else (h // 4, h % 4)
                for n0 in range(0, L, 512):
                    nn = min(512, L - n0)
                    last = pe.matmul(banks[:, 2 * (n % 2) + n0 // 512, 0:nn], q[64 * g:64 * g + 64, j, i * P:(i + 1) * P],
                                     keys[64 * g:64 * g + 64, n0:n0 + nn], start=True, stop=True)
                last.then_inc(s_wide, 1)

            def turn(i, h):
                u = 8 * i + h
                pe.wait_ge(s_pn, u + 1)
                for q in range(-(-(i + 1) // 4)):
                    v = half_at[i, h, q]
                    if v >= 2:
                        pe.wait_ge(s_pt, v - 1)
                    for t in range(4 * q, min(4 * q + 4, i + 1)):
                        last = pe.transpose(ps[4 + v % 2][:, (t % 4) * P:(t % 4 + 1) * P],
                                            lg[:, u % 2, t * P:(t + 1) * P], ident[:])
                    last.then_inc(s_tp, 1)

            def mix(i, g):
                n = 2 * i + g
                pe.wait_ge(s_pt, half_at[i, 4 * g + 3, -(-(i + 1) // 4) - 1] + 1)
                if n:
                    pe.wait_ge(s_hb, n)
                for t in range(i + 1):
                    last = pe.matmul(ps[6], tok[:, t, TK["v"]:TK["v"] + P], PT[:, g, t, :],
                                     start=(t == 0), stop=(t == i))
                last.then_inc(s_pv, 1)

            def side_product(u):
                (ft, n0, nn), f = side[u], u // 3
                if n0 == 0:
                    pe.wait_ge(s_sw[f % 3], 16 * (f // 3 + 1))
                if u:
                    pe.wait_ge(s_sout, u)
                product(pe, ps[7][:, 0:nn], P, lambda kt: side_w[:, f % 3, kt, :], lambda kt: xT[:, kt, n0:n0 + nn],
                        KT).then_inc(s_sfull, 1)

            for i in range(NCH):
                if 2 <= i + 1 < NCH:
                    for h in range(8):
                        wide_product(("dots", i + 1, h))
                wide_product(("logits", i, 0))
                for h in range(8):
                    if h < 7:
                        wide_product(("logits", i, h + 1))
                    for u in side_of(i, h):
                        side_product(u)
                    turn(i, h)
                    if h == 4:
                        mix(i, 0)
                mix(i, 1)

        @block.scalar
        def _(act):
            def relu(i, h):
                n = 8 * (i - 2) + h
                act.wait_ge(s_wide, at["dots", i, h] + 1)
                if n >= 2:
                    act.wait_ge(s_acc, n - 1)
                act.activation(rl[:, n % 2, 0:(i + 1) * P], wide(("dots", i, h), (i + 1) * P), ACT.Relu,
                               scale=float(BD) ** -0.5).then_inc(s_wide_act, 1)

            def exps(i, h):
                u = 8 * i + h
                act.wait_ge(s_mx, u + 1)
                x = lg[:, u % 2, 0:(i + 1) * P]
                act.activation(x, x, ACT.Exp, bias=nm[:, u % 2:u % 2 + 1], scale=float(BD) ** -0.5,
                               accum_out=sm[:, u % 2:u % 2 + 1]).then_inc(s_ex, 1)

            def spread(i, h):
                for q in range(-(-(i + 1) // 4)):
                    v = half_at[i, h, q]
                    act.wait_ge(s_tp, v + 1)
                    if q == 0 and h % 4 == 0 and i > 0:
                        act.wait_ge(s_pv, 2 * (i - 1) + h // 4 + 1)
                    c = min(4, i + 1 - 4 * q)
                    act.copy(PT[:, h // 4, 4 * q:4 * q + c, (h % 4) * P:(h % 4 + 1) * P],
                             ps[4 + v % 2][:, 0:c * P].rearrange("p (t n) -> p t n", t=c)).then_inc(s_pt, 1)

            def result(i, g):
                act.wait_ge(s_pv, 2 * i + g + 1)
                act.copy(hT[64 * g:64 * g + 64, 4:8, i * P:(i + 1) * P],
                         ps[6][64 * g:64 * g + 64, :].rearrange("p (j q) -> p j q", j=4)).then_inc(s_hb, 1)

            def side_out(u):
                ft, n0, nn = side[u]
                act.wait_ge(s_sfull, u + 1)
                if u >= 2:
                    act.wait_ge(s_sst[u % 2], 16 * (u // 2))
                col = BC["u"] + ft
                act.activation(side_y[:, u % 2, 0:nn], ps[7][:, 0:nn], ACT.Identity,
                               bias=biasc[:, col:col + 1]).then_inc(s_sout, 1)

            for i in range(NCH):
                if 2 <= i + 1 < NCH:
                    for h in range(8):
                        relu(i + 1, h)
                exps(i, 0)
                for h in range(8):
                    if h < 7:
                        exps(i, h + 1)
                    for u in side_of(i, h):
                        side_out(u)
                    spread(i, h)
                    if h == 5:
                        result(i, 0)
                result(i, 1)

        @block.vector
        def _(dve):
            n = 0

            def step(ins):
                nonlocal n
                n += 1
                ins.then_inc(s_st, 1)
                dve.wait_ge(s_st, n)

            dve.wait_ge(s_cst, 2)
            step(dve.tensor_scalar(wis[:], tok[:, 0:NCH, TK["iw"]:TK["iw"] + 8], 8.0 ** -0.5, None, ALU.mult))

            def maximum(i, h):
                u, L = 8 * i + h, (i + 1) * P
                dve.wait_ge(s_wide, at["logits", i, h] + 1)
                if u >= 2:
                    i2, h2 = divmod(u - 2, 8)
                    dve.wait_ge(s_tp, half_at[i2, h2, -(-(i2 + 1) // 4) - 1] + 1)
                s = u % 2
                dve.tensor_tensor_reduce(lg[:, s, 0:L], wide(("logits", i, h), L), pen[:, 0:L], 1.0, GONE, ALU.add,
                                         ALU.max, mx[:, s:s + 1]).then_inc(s_wide_dve, 1)
                dve.wait_ge(s_wide_dve, u + 1)
                dve.tensor_scalar(nm[:, s:s + 1], mx[:, s:s + 1], -float(BD) ** -0.5, None, ALU.mult).then_inc(s_mx, 1)

            def scale(i, h):
                u, L = 8 * i + h, (i + 1) * P
                s = u % 2
                dve.wait_ge(s_ex, u + 1)
                step(dve.reciprocal(rc[:, s:s + 1], sm[:, s:s + 1]))
                dve.tensor_scalar(lg[:, s, 0:L], lg[:, s, 0:L], rc[:, s:s + 1], None, ALU.mult).then_inc(s_pn, 1)

            def sum_scores(i):
                L = (i + 1) * P
                for h in range(8):
                    m = 8 * (i - 2) + h
                    dve.wait_ge(s_wide_act, m + 1)
                    x, w = rl[:, m % 2, 0:L], wis[:, i, h:h + 1]
                    if h == 0:
                        dve.tensor_scalar(score[:, 0:L], x, w, None, ALU.mult).then_inc(s_acc, 1)
                    else:
                        dve.scalar_tensor_tensor(score[:, 0:L], x, w, score[:, 0:L], ALU.mult,
                                                 ALU.add).then_inc(s_acc, 1)
                    dve.wait_ge(s_acc, m + 1)
                step(dve.tensor_tensor(score[:, i * P:L], score[:, i * P:L], penc[:], ALU.add))

            for i in range(NCH):
                L, ahead = (i + 1) * P, 2 <= i + 1 < NCH
                if i >= 2:
                    step(dve.tensor_scalar(score[:, 0:L], score[:, 0:L], GONE, 1.0, ALU.is_equal, ALU.subtract))
                    step(dve.tensor_scalar(pen[:, 0:L], score[:, 0:L], BIG, None, ALU.mult))
                else:
                    step(dve.memset(pen[:, 0:L], 0.0))
                    step(dve.tensor_copy(pen[:, i * P:L], penc[:]))
                if ahead:
                    sum_scores(i + 1)
                maximum(i, 0)
                for h in range(8):
                    if ahead:
                        keep_best(dve, s_best, (i - 1) * KEEP // 4, score[:, 0:L + P], best[:], 4 * h, 4 * h + 4)
                    if h < 7:
                        maximum(i, h + 1)
                    scale(i, h)


def attend_samples(nc, a, k, sb, bqT, iqT, bkT, ikT, tok):
    ps, banks, ident, hT, sem = k.ps, k.banks, k.ident, k.hT, k.sem
    KC = NPG
    (s_pt, s_ixc, s_idx, s_kd, s_vd, s_id, s_dup, s_z, s_zz, s_tr, s_tre, s_dot, s_rel, s_sc, s_best, s_st, s_sel, s_mx,
     s_ex, s_pn, s_tp, s_tpe, s_pv, s_hb, s_wc, s_lgt) = (
        sem("s_sample_" + x) for x in ("pt", "ixc", "idx", "kd", "vd", "id", "dup", "z", "zz", "tr", "tre", "dot", "rel", "sc",
                                 "best", "st", "sel", "mx", "ex", "pn", "tp", "tpe", "pv", "hb", "wc", "lgt"))
    side = [(ft, n0, nn) for ft in range(ASIDE - LATE, ASIDE) for n0, nn in TOKEN_CHUNKS]
    s_sw = [sem(f"s_late_w{i}") for i in range(2)]
    s_sst = [sem(f"s_late_stored{i}") for i in range(2)]
    s_sfull, s_sout = sem("s_late_full"), sem("s_late_out")
    s_idl = [sem(f"s_idl{i}") for i in range(2)]
    s_kdl = [sem(f"s_kdl{i}") for i in range(2)]
    s_vdl = [sem(f"s_vdl{i}") for i in range(2)]
    with ExitStack() as cw, nc.Block() as block:
        page = sb("page", [P, NB], I32, cw)
        lane = sb("lane", [P, 1], I32, cw)
        where = sb("where", [P, NB], I32, cw)
        ic = sb("ic", [P, 2, KC * BD], c=cw)
        icd = hT[:, 8, 0:KC * P].rearrange("p (t g d) -> p t g d", t=KC, g=2)
        kc = sb("kc", [P, 2, KC * P], c=cw)
        vc = hT[:, 10:12, 0:KC * P]
        keysT = sb("keysT", [P, PAST], c=cw)
        dq = sb("dq", [SM, NS], c=cw)
        iqz = sb("iqz", [P, NB, 2, 4, NS], c=cw)
        bqz = sb("bqz", [P, NB, 2, 4, NS], c=cw)
        lw = sb("lw", [SM, 2, 4, NS], c=cw)
        wcol = sb("wcol", [SM, NB], c=cw)
        wsum = sb("wsum", [SM, NB * (SM + NS)], c=cw)
        tell = sb("tell", [SM, NB, 8, NS], c=cw)
        rl_all = sb("srl", [P, 2, NK], c=cw)
        rl = rl_all[0:SM]
        sc = sb("ssc", [SM, NK], c=cw)
        pen = sb("spen", [SM, NK], c=cw)
        best = sb("sbest", [SM, 8], c=cw)
        pr = sb("pr", [SM, NK], c=cw)
        side_w = [rl_all[:, i, 0:D].rearrange("p (k c) -> p k c", k=KT) for i in range(2)]
        side_y = hT[:, 8, 0:2 * 512].rearrange("p (s c) -> p s c", s=2)
        prT = hT[:, 9, 0:(KC + 1) * SM].rearrange("p (t n) -> p t n", n=SM)
        mx = sb("smx", [SM, 4], c=cw)

        @block.sync
        def _(sp):
            for g in range(NPG):
                sp.dma_start(page[16 * g:16 * g + 16, :],
                             a["page_table"][:, g:g + 1].rearrange("b o -> o b").broadcast_to([16, NB])).then_inc(s_pt, 16)

            def load(i):
                at = OFF["u"] + (ASIDE - LATE + i) * P
                sp.dma_start(side_w[i % 2], k.w_in[:, :, at:at + P]).then_inc(s_sw[i % 2], 16)

            sp.wait_ge(s_sc, NB)
            load(0)
            load(1)
            for u, (ft, n0, nn) in enumerate(side):
                sp.wait_ge(s_sout, u + 1)
                sp.dma_start(k.aside[ft, :, n0:n0 + nn], side_y[:, u % 2, 0:nn]).then_inc(s_sst[u % 2], 16)
                if u % 3 == 2 and u // 3 + 2 < LATE:
                    load(u // 3 + 2)
            for i, s in enumerate(s_sst):
                sp.wait_ge(s, 16 * ((len(side) + 1 - i) // 2))

        @block.gpsimd
        def _(pool):
            pool.iota(lane[:], pattern=[[0, 1]], base=0, channel_multiplier=1).then_inc(s_ixc, 1)
            pool.wait_ge(s_idx, 1)

            def fetch(dst, src, b, s):
                pool.indirect_dma_start(dst, None, src, bass.IndirectOffsetOnAxis(ap=where[:, b:b + 1], axis=0)).then_inc(s, 16)

            views = [a["cache_kidx"][0].rearrange("n (r e) d -> (n r) (e d)", e=8),
                     a["cache_k"][0].rearrange("n (r e) h d -> (n r) (e h d)", e=8),
                     a["cache_v"][0].rearrange("n (r e) h d -> (n r) (e h d)", e=8)]
            for b in range(NB):
                if b >= 2:
                    pool.wait_ge(s_dup, b - 1)
                fetch(ic[:, b % 2, :], views[0], b, s_idl[b % 2])
            for b in range(NB):
                if b >= 2:
                    pool.wait_ge(s_tr, NB + b - 1)
                fetch(kc[:, b % 2, :], views[1], b, s_kdl[b % 2])
                if b >= 2:
                    pool.wait_ge(s_pv, b - 1)
                fetch(vc[:, b % 2, :], views[2], b, s_vdl[b % 2])
            for s in s_idl + s_kdl + s_vdl:
                pool.wait_ge(s, 16 * NB // 2)

        def new_keys(keys):
            return keys[:, SEQ:N]

        @block.tensor
        def _(pe):
            def turn_keys(n, src):
                if n:
                    pe.wait_ge(s_tre, n)
                for t in range(KC):
                    last = pe.transpose(ps[6 + t // 4][:, (t % 4) * P:(t % 4 + 1) * P], src(t), ident[:])
                last.then_inc(s_tr, 1)

            def against_keys(left, new, first, start, stop):
                for i in range(2):
                    last = pe.matmul(ps[first + i][0:SM, :], left, keysT[:, 512 * i:512 * i + 512], start=start, stop=stop)
                return pe.matmul(ps[first + 2][0:SM, 0:SM], left, new, start=start, stop=stop)

            def columns(b, i):
                return (512 * i, 512) if i < 2 else (PAST, SM)

            pe.wait_ge(s_z, 1)
            pe.matmul(ps[5][0:SM, 0:NB], lw[:].rearrange("p g j q -> p (g j q)"), k.own[:], start=True,
                      stop=True).then_inc(s_wc, 1)
            pe.wait_ge(s_zz, 1)
            def turn_index_keys(b):
                pe.wait_ge(s_dup, b + 1)
                turn_keys(b, lambda t: icd[:, t, :, :].rearrange("p g d -> p (g d)"))

            turn_index_keys(0)
            for b in range(NB):
                pe.wait_ge(s_tre, b + 1)
                if b:
                    pe.wait_ge(s_rel, b)
                against_keys(iqz[:, b].rearrange("p g j q -> p (g j q)"), new_keys(ikT), 0, True, True).then_inc(s_dot, 1)
                if b + 1 < NB:
                    turn_index_keys(b + 1)
                pe.wait_ge(s_rel, b + 1)
                for i in range(3):
                    c0, cn = columns(b, i)
                    last = pe.matmul(ps[3 + i][0:SM, 0:cn], wsum[:, b * SM:(b + 1) * SM], rl[:, b % 2, c0:c0 + cn],
                                     start=(b == 0), stop=(b == NB - 1))
                last.then_inc(s_sc, 1)
            def turn_cached_keys(b):
                pe.wait_ge(s_kdl[b % 2], 16 * (b // 2 + 1))
                turn_keys(NB + b, lambda t: kc[:, b % 2, t * P:(t + 1) * P])

            def logits(b):
                pe.wait_ge(s_tre, NB + b + 1)
                if b:
                    pe.wait_ge(s_ex, b)
                pe.wait_ge(s_sel, 1)
                left = bqz[:, b].rearrange("p g j q -> p (g j q)")
                against_keys(left, new_keys(bkT), 0, True, False)
                for i in range(3):
                    c0, cn = columns(b, i)
                    last = pe.matmul(ps[i][0:SM, 0:cn], tell[:, b].rearrange("p h q -> p (h q)"), pen[:, c0:c0 + cn],
                                     start=False, stop=True)
                last.then_inc(s_lgt, 1)

            def turn_probs(b):
                pe.wait_ge(s_pn, b + 1)
                if b:
                    pe.wait_ge(s_tpe, b)
                for t in range(KC):
                    pe.transpose(ps[3][:, t * SM:(t + 1) * SM], pr[:, t * P:(t + 1) * P], ident[0:SM, 0:SM])
                pe.transpose(ps[4][0:SM, 0:SM], pr[:, PAST:NK], ident[0:SM, 0:SM]).then_inc(s_tp, 1)

            def mix(b):
                pe.wait_ge(s_tpe, b + 1)
                pe.wait_ge(s_vdl[b % 2], 16 * (b // 2 + 1))
                if b:
                    pe.wait_ge(s_hb, b)
                for t in range(KC):
                    pe.matmul(ps[5][:, 0:SM], vc[:, b % 2, t * P:(t + 1) * P], prT[:, t, :], start=(t == 0), stop=False)
                pe.matmul(ps[5][:, 0:SM], tok[0:SM, NCH, TK["v"]:TK["v"] + P], prT[0:SM, KC, :], start=False,
                          stop=True).then_inc(s_pv, 1)

            turn_cached_keys(0)
            for u, (ft, n0, nn) in enumerate(side):
                if n0 == 0:
                    i = u // 3
                    pe.wait_ge(s_sw[i % 2], 16 * (i // 2 + 1))
                if u >= 2:
                    pe.wait_ge(s_sout, u - 1)
                product(pe, ps[u % 2][:, 0:nn], P, lambda kt: side_w[u // 3 % 2][:, kt, :],
                        lambda kt: k.xT[:, kt, n0:n0 + nn], KT).then_inc(s_sfull, 1)
            pe.wait_ge(s_sout, len(side))
            logits(0)
            for b in range(NB):
                if b + 1 < NB:
                    turn_cached_keys(b + 1)
                turn_probs(b)
                if b + 1 < NB:
                    logits(b + 1)
                mix(b)

        @block.scalar
        def _(act):
            def keep_keys(n, s, used):
                act.wait_ge(s_tr, n + 1)
                if used:
                    act.wait_ge(s, used)
                act.copy(keysT[:], banks[:, 6:8, :].rearrange("p b n -> p (b n)")).then_inc(s_tre, 1)

            keep_keys(0, s_dot, 0)
            for b in range(NB):
                act.wait_ge(s_dot, b + 1)
                if b >= 2:
                    act.wait_ge(s_sc, b - 1)
                act.activation(rl[:, b % 2, :], banks[0:SM, 0:3, :].rearrange("p b n -> p (b n)")[:, 0:NK], ACT.Relu,
                               scale=float(BD) ** -0.5).then_inc(s_rel, 1)
                if b + 1 < NB:
                    keep_keys(b + 1, s_dot, b + 1)
            keep_keys(NB, s_dot, NB)
            act.wait_ge(s_sc, NB)
            for u, (ft, n0, nn) in enumerate(side):
                act.wait_ge(s_sfull, u + 1)
                if u >= 2:
                    act.wait_ge(s_sst[u % 2], 16 * (u // 2))
                col = BC["u"] + ft
                act.activation(side_y[:, u % 2, 0:nn], ps[u % 2][:, 0:nn], ACT.Identity,
                               bias=k.biasc[:, col:col + 1]).then_inc(s_sout, 1)
            for b in range(NB):
                if b + 1 < NB:
                    keep_keys(NB + b + 1, s_lgt, b + 1)
                act.wait_ge(s_mx, b + 1)
                if b:
                    act.wait_ge(s_tp, b)
                act.activation(pr[:], banks[0:SM, 0:3, :].rearrange("p b n -> p (b n)")[:, 0:NK], ACT.Exp,
                               bias=mx[:, 1:2], scale=float(BD) ** -0.5, accum_out=mx[:, 2:3]).then_inc(s_ex, 1)

        @block.vector
        def _(dve):
            n = 0

            def step(ins):
                nonlocal n
                n += 1
                ins.then_inc(s_st, 1)
                dve.wait_ge(s_st, n)

            dve.wait_ge(s_ixc, 1)
            dve.wait_ge(s_pt, 16 * NPG)
            dve.tensor_scalar(lane[:], lane[:], 15, None, ALU.bitwise_and)
            step(dve.tensor_scalar(where[:], page[:], 16.0, None, ALU.mult))
            dve.tensor_tensor(where[:], where[:], lane[:].to_broadcast([P, NB]), ALU.add).then_inc(s_idx, 1)
            dve.memset(iqz[:], 0.0)
            dve.memset(wsum[:], 0.0)
            dve.memset(bqz[:], 0.0)
            step(dve.tensor_reduce(dq[:], ident[0:SM, 0:SM].rearrange("p (b q) -> p q b", b=NB), AX, ALU.add))
            dve.tensor_tensor(lw[:], tok[0:SM, NCH, TK["iw"]:TK["iw"] + 8].rearrange("p (j g) -> p g j", g=2)
                              .unsqueeze(3).to_broadcast([SM, 2, 4, NS]),
                              dq[:].unsqueeze(1).unsqueeze(1).to_broadcast([SM, 2, 4, NS]), ALU.mult).then_inc(s_z, 1)
            dve.tensor_tensor(tell[:], k.own[:].unsqueeze(2).unsqueeze(3).to_broadcast([SM, NB, 8, NS]),
                              dq[:].unsqueeze(1).unsqueeze(1).to_broadcast([SM, NB, 8, NS]), ALU.mult)
            for z, q in ((iqz, iqT), (bqz, bqT)):
                for g in range(2):
                    for j in range(4):
                        dve.tensor_copy(z[64 * g:64 * g + 64, :, g, j, :],
                                        q[64 * g:64 * g + 64, j, SEQ:N].rearrange("p (b q) -> p b q", b=NB))
            dve.wait_ge(s_wc, 1)
            step(dve.tensor_scalar(wcol[:], ps[5][0:SM, 0:NB], 8.0 ** -0.5, None, ALU.mult))
            step(dve.tensor_tensor(wsum[:].rearrange("p (b s) -> p b s", s=SM + NS)[:, :, 0:NS],
                                   wcol[:].unsqueeze(2).to_broadcast([SM, NB, NS]),
                                   dq[:].unsqueeze(1).to_broadcast([SM, NB, NS]), ALU.mult))
            step(dve.tensor_scalar(tell[:], tell[:], BIG, None, ALU.mult))
            dve.sem_inc(s_zz, 1)
            for b in range(NB):
                dve.wait_ge(s_idl[b % 2], 16 * (b // 2 + 1))
                if b:
                    dve.wait_ge(s_tr, b)
                for g in range(2):
                    last = dve.tensor_copy(icd[:, :, g, :], ic[:, b % 2, :].rearrange("p (t d) -> p t d", t=KC))
                last.then_inc(s_dup, 1)
            dve.wait_ge(s_sc, NB)
            dve.tensor_copy(sc[:, 0:PAST].rearrange("p (e t) -> p t e", t=KC),
                            banks[0:SM, 3:5, :].rearrange("p b (t e) -> p (b t) e", e=P))
            step(dve.tensor_scalar(pen[:, PAST:NK], k.sampleQ[:], 1.0, BIG, ALU.subtract, ALU.mult))
            step(dve.tensor_tensor(sc[:, PAST:NK], ps[5][0:SM, 0:SM], pen[:, PAST:NK], ALU.add))
            keep_best(dve, s_best, 0, sc[:], best[:])
            dve.tensor_scalar(pen[:, 0:PAST].rearrange("p (t e) -> p t e", e=P),
                              sc[:, 0:PAST].rearrange("p (e t) -> p t e", t=KC), GONE, 1.0, ALU.is_equal, ALU.subtract)
            dve.tensor_scalar(pen[:, PAST:NK], sc[:, PAST:NK], GONE, 1.0, ALU.is_equal, ALU.subtract).then_inc(s_sel, 1)
            for b in range(NB):
                dve.wait_ge(s_lgt, b + 1)
                if b:
                    dve.wait_ge(s_ex, b)
                step(dve.tensor_reduce(mx[:, 0:1], banks[0:SM, 0:3, :].rearrange("p b n -> p (b n)")[:, 0:NK], AX, ALU.max))
                dve.tensor_scalar(mx[:, 1:2], mx[:, 0:1], -float(BD) ** -0.5, None, ALU.mult).then_inc(s_mx, 1)
                dve.wait_ge(s_ex, b + 1)
                step(dve.reciprocal(mx[:, 3:4], mx[:, 2:3]))
                dve.tensor_scalar(pr[:], pr[:], mx[:, 3:4], None, ALU.mult).then_inc(s_pn, 1)
                dve.wait_ge(s_tp, b + 1)
                if b:
                    dve.wait_ge(s_pv, b)
                dve.tensor_copy(prT[:, 0:KC, :], ps[3][:].rearrange("p (t n) -> p t n", t=KC))
                dve.tensor_copy(prT[0:SM, KC, :], ps[4][0:SM, 0:SM]).then_inc(s_tpe, 1)
                dve.wait_ge(s_pv, b + 1)
                for g in range(2):
                    last = dve.tensor_copy(hT[64 * g:64 * g + 64, 4:8, SEQ + NS * b:SEQ + NS * b + NS],
                                           ps[5][64 * g:64 * g + 64, 32 * g:32 * g + 32].rearrange("p (j q) -> p j q", j=4))
                last.then_inc(s_hb, 1)


def build_pooling(nc, a, k):
    ps, ident, ones, xT, hT, biasc, sem = k.ps, k.ident, k.ones, k.xT, k.hT, k.biasc, k.sem
    PAD = max(WINDOWS)
    OLD = NB * POOLB
    (s_w, s_cm, s_sp, s_out, s_cst, s_inv, s_sps, s_old, s_st, s_pool, s_z, s_zout, s_rows, s_rowsv, s_dma) = (
        sem("s_pool_" + x) for x in ("w", "cm", "sp", "out", "cst", "inv", "sps", "old", "st", "pool", "z", "zout",
                                 "rows", "rowsv", "dma"))
    with ExitStack() as cw, nc.Block() as block:
        def sb(name, shape, dt=F32):
            return k.sb(name, shape, dt, cw)

        cmap = sb("cmap", [P, 4, P])
        cscale = sb("cscale", [P, 4])
        old = sb("old", [OLD, 512])
        up = sb("up", [P, 4, PAD + SEQ])
        us = sb("us", [P, 4, NB, POOLB + NS])
        un = sb("un", [P, 4, SM])
        sums = sb("sums", [P, 2, PAD + SEQ])
        ssums = sb("ssums", [P, 2, NB, POOLB + NS])
        inv = sb("inv", [P, PAD])
        first = sb("first", [P, PAD])
        pooled = sb("pooled", [P, 2, N])
        tail = sb("tail", [POOLB, 512])
        new = sb("new", [SM, 512])

        @block.sync
        def _(sp):
            sp.dma_start(up[:, :, PAD:], k.aside[0:4, :, 0:SEQ].rearrange("g p n -> p g n")).then_inc(s_w, 16)
            sp.dma_start(un[:], k.aside[0:4, :, SEQ:].rearrange("g p n -> p g n")).then_inc(s_w, 16)
            sp.dma_start(old[:], a["state_pool"][0].rearrange("b r c -> (b r) c")).then_inc(s_sp, 16)
            sp.dma_start(cmap[:], a["c_map"][0].rearrange("g c d -> c g d")).then_inc(s_cm, 16)
            sp.dma_start(cscale[:], a["c_scale"][0].rearrange("(g c) -> c g", g=4)).then_inc(s_cm, 16)
            for b in range(NB):
                sp.dma_start(a["pool_sample"][0, b, 0:POOLB - NS], a["state_pool"][0, b, NS:POOLB]).then_inc(s_dma, 16)
            sp.wait_ge(s_rowsv, 2)
            sp.dma_start(a["pool_prompt"][0, 0], tail[:]).then_inc(s_dma, 16)
            for b in range(NB):
                sp.dma_start(a["pool_sample"][0, b, POOLB - NS:], new[NS * b:NS * b + NS, :]).then_inc(s_dma, 16)
            sp.wait_ge(s_dma, 16 * (2 * NB + 1))

        @block.gpsimd
        def _(pool):
            pool.iota(inv[:], pattern=[[1, PAD]], base=1, channel_multiplier=0,
                      allow_small_or_imprecise_dtypes=True).then_inc(s_cst, 1)

        @block.tensor
        def _(pe):
            pe.wait_ge(s_sp, 16)
            for g in range(4):
                last = pe.transpose(ps[7][:, g * OLD:(g + 1) * OLD], old[:, g * P:(g + 1) * P], ident[0:OLD, 0:OLD])
            last.then_inc(s_sps, 1)
            pe.wait_ge(s_w, 32)
            for g in range(4):
                pe.transpose(ps[5][0:POOLB, g * P:(g + 1) * P], up[:, g, PAD + SEQ - POOLB:], ident[:])
            for g in range(4):
                last = pe.transpose(ps[6][0:SM, g * P:(g + 1) * P], un[:, g, :], ident[:])
            last.then_inc(s_rows, 1)
            pe.wait_ge(s_cm, 32)
            for g in range(4):
                pe.wait_ge(s_pool, g + 1)
                for i, (n0, nn) in enumerate(TOKEN_CHUNKS):
                    j = 3 * g + i
                    if j >= 4:
                        pe.wait_ge(s_zout, j - 3)
                    pe.matmul(ps[j % 4][:, 0:nn], cmap[:, g, :], pooled[:, g % 2, n0:n0 + nn], start=True,
                              stop=True).then_inc(s_z, 1)

        @block.scalar
        def _(act):
            act.wait_ge(s_w, 32)
            for g in range(4):
                act.copy(us[:, g, :, POOLB:], un[:, g, :].rearrange("p (b t) -> p b t", b=NB)).then_inc(s_out, 1)
            act.wait_ge(s_rows, 1)
            act.copy(tail[:], ps[5][0:POOLB, :]).then_inc(s_rowsv, 1)
            act.copy(new[:], ps[6][0:SM, :]).then_inc(s_rowsv, 1)
            for j in range(12):
                g, (n0, nn) = j // 3, TOKEN_CHUNKS[j % 3]
                act.wait_ge(s_z, j + 1)
                act.activation(hT[:, 8 + g, n0:n0 + nn], ps[j % 4][:, 0:nn], ACT.Copy,
                               scale=cscale[:, g:g + 1]).then_inc(s_zout, 1)

        @block.vector
        def _(dve):
            n = 0

            def step(ins):
                nonlocal n
                n += 1
                ins.then_inc(s_st, 1)
                dve.wait_ge(s_st, n)

            dve.wait_ge(s_w, 32)
            dve.memset(up[:, :, 0:PAD], 0.0)
            dve.memset(sums[:, :, 0:PAD], 0.0)
            dve.memset(ssums[:], 0.0)
            dve.wait_ge(s_cst, 1)
            step(dve.reciprocal(inv[:], inv[:]))
            dve.wait_ge(s_sps, 1)
            step(dve.tensor_copy(us[:, :, :, 0:POOLB], ps[7][:, 0:4 * OLD].rearrange("p (g b r) -> p g b r", g=4, b=NB)))
            for g, w_ in enumerate(WINDOWS):
                dve.wait_ge(s_out, g + 1)
                src, ssrc, d, i = up[:, g, :], us[:, g], 1, 0
                while d < w_:
                    dst, sdst = sums[:, i % 2, :], ssums[:, i % 2]
                    dve.tensor_tensor(sdst[:, :, d:], ssrc[:, :, d:], ssrc[:, :, :POOLB + NS - d], ALU.add)
                    step(dve.tensor_tensor(dst[:, PAD:], src[:, PAD:], src[:, PAD - d:PAD + SEQ - d], ALU.add))
                    src, ssrc, d, i = dst, sdst, 2 * d, i + 1
                if g >= 2:
                    dve.wait_ge(s_z, 3 * (g - 1))
                dve.scalar_tensor_tensor(pooled[:, g % 2, 0:SEQ], src[:, PAD:], 1.0 / w_, up[:, g, PAD:], ALU.mult,
                                         ALU.subtract)
                dve.scalar_tensor_tensor(pooled[:, g % 2, SEQ:].rearrange("p (b t) -> p b t", b=NB), ssrc[:, :, POOLB:],
                                         1.0 / w_, us[:, g, :, POOLB:], ALU.mult, ALU.subtract)
                step(dve.tensor_tensor(first[:, 0:w_], src[:, PAD:PAD + w_], inv[:, 0:w_], ALU.mult))
                dve.tensor_tensor(pooled[:, g % 2, 0:w_], first[:, 0:w_], up[:, g, PAD:PAD + w_],
                                  ALU.subtract).then_inc(s_pool, 1)


def build_merge(nc, a, k):
    ps, banks, ident, xT, hT, biasc, sem = k.ps, k.banks, k.ident, k.xT, k.hT, k.biasc, k.sem
    units = [(et, c, x) for et in range(KT) for c in range(3) for x in range(3)]
    s_full, s_sig, s_prod, s_st, s_wo, s_ln = (sem("s_merge_" + x) for x in ("full", "sig", "prod", "st", "wo", "ln"))
    s_wt = [sem("s_merge_p0"), sem("s_merge_p1")]
    s_gt = [sem("s_merge_gates0"), sem("s_merge_gates1")]
    with ExitStack() as cm:
        def sb(name, shape, dt=F32):
            return k.sb(name, shape, dt, cm)

        merged = sb("merged", [P, KT, N])
        wo = sb("w_out_t", [P, KT, D])
        with ExitStack() as cw, nc.Block() as block:
            pt = k.sb("p_mix", [P, 2, 3, 4, P], F32, cw)
            sg = k.sb("sg", [P, 2, 3, N], F32, cw)
            pr = k.sb("prod", [P, 512], F32, cw)

            @block.sync
            def _(sp):
                for et in range(KT):
                    if et >= 2:
                        sp.wait_ge(s_prod, 9 * (et - 1))
                    s, cols = et % 2, slice(et * P, (et + 1) * P)
                    sp.dma_start(pt[:, s, 0], a["p_a"][0].rearrange("(k p) n -> p k n", p=P)[:, :, cols]).then_inc(s_wt[s], 16)
                    for g in range(BKV):
                        sp.dma_start(pt[64 * g:64 * g + 64, s, 1],
                                     a["p_b"][0][256 * g:256 * g + 256].rearrange("(j d) n -> d j n", d=BD)[:, :, cols]
                                     ).then_inc(s_wt[s], 16)
                    sp.dma_start(pt[:, s, 2], a["p_c"][0].rearrange("(k p) n -> p k n", p=P)[:, :, cols]).then_inc(s_wt[s], 16)
                    for x in range(3):
                        sp.dma_start(sg[:, s, x], k.aside[4 + KT * x + et]).then_inc(s_gt[s], 16)
                sp.dma_start(wo[:], a["w_out"][0].rearrange("(k p) n -> p k n", p=P)).then_inc(s_wo, 16)
                sp.wait_ge(s_wo, 16)

            @block.tensor
            def _(pe):
                for n, (et, c, x) in enumerate(units):
                    s, (n0, nn) = et % 2, TOKEN_CHUNKS[c]
                    if c == 0 and x == 0:
                        pe.wait_ge(s_wt[s], 16 * 4 * (et // 2 + 1))
                    if n >= 8:
                        pe.wait_ge(s_prod, n - 7)
                    product(pe, ps[n % 8][:, 0:nn], P, lambda kt: pt[:, s, x, kt, :],
                            lambda kt: hT[:, 4 * x + kt, n0:n0 + nn], 4).then_inc(s_full, 1)

            @block.scalar
            def _(act):
                for et in range(KT):
                    act.wait_ge(s_gt[et % 2], 16 * 3 * (et // 2 + 1))
                    for x in range(3):
                        act.activation(sg[:, et % 2, x, :], sg[:, et % 2, x, :], ACT.Sigmoid).then_inc(s_sig, 1)

            @block.vector
            def _(dve):
                m = 0
                for n, (et, c, x) in enumerate(units):
                    n0, nn = TOKEN_CHUNKS[c]
                    dve.wait_ge(s_full, n + 1)
                    if c == 0:
                        dve.wait_ge(s_sig, 3 * et + x + 1)
                    out = merged[:, et, n0:n0 + nn]
                    if x and m:
                        dve.wait_ge(s_st, m)
                    dve.tensor_tensor(pr[:, 0:nn] if x else out, sg[:, et % 2, x, n0:n0 + nn], ps[n % 8][:, 0:nn],
                                      ALU.mult).then_inc(s_prod, 1)
                    if x:
                        dve.wait_ge(s_prod, n + 1)
                        dve.tensor_tensor(out, out, pr[:, 0:nn], ALU.add).then_inc(s_st, 1)
                        m += 1

        k.x1 = nc.dram_tensor("x1", (N, D), F32, kind="Internal").ap()
        (s_y, s_yst, s_ve, s_rs, s_nb, s_z, s_x1, s_tp, s_tpe, s_ys) = (
            sem("s_norm_" + x) for x in ("y", "yst", "ve", "rs", "nb", "z", "x1", "tp", "tpe", "ys"))
        s_x1d = [sem("s_x1_stored0"), sem("s_x1_stored1")]
        s_full2 = sem("s_lfull")
        s_xr = [sem("s_lxr0"), sem("s_lxr1")]
        with ExitStack() as cw, nc.Block() as block:
            lng = k.sb("ln1g", [P, D], F32, cw)
            lnb = k.sb("ln1b", [P, D], F32, cw)
            xr = k.sb("xr", [P, 2, D], F32, cw)
            y = k.sb("y", [P, 2, D], F32, cw)
            st = k.sb("st", [P, 2, 6], F32, cw)
            mv = k.sb("mv", [P, 2, 4], F32, cw)

            @block.sync
            def _(sp):
                sp.dma_start(lng[:], a["ln1_g"].broadcast_to([P, D])).then_inc(s_ln, 16)
                sp.dma_start(lnb[:], a["ln1_b"].broadcast_to([P, D])).then_inc(s_ln, 16)
                for t in range(NT):
                    if t >= 2:
                        sp.wait_ge(s_y, t - 1)
                    sp.dma_start(xr[0:rows(t), t % 2, :], k.token_rows(k.x_p, k.x_s, t)).then_inc(s_xr[t % 2], 16)
                    if t:
                        sp.wait_ge(s_x1, t)
                        sp.dma_start(k.x1[(t - 1) * P:t * P, :], y[:, (t - 1) % 2, :]).then_inc(s_x1d[(t - 1) % 2], 16)
                sp.wait_ge(s_x1, NT)
                sp.dma_start(k.x1[SEQ:N, :], y[0:SM, (NT - 1) % 2, :]).then_inc(s_x1d[(NT - 1) % 2], 16)
                for s in range(2):
                    sp.wait_ge(s_x1d[s], 16 * ((NT + 1 - s) // 2))

            @block.tensor
            def _(pe):
                def turn(t):
                    pe.wait_ge(s_x1, t + 1)
                    if t:
                        pe.wait_ge(s_tpe, t)
                    for i in range(KT):
                        last = pe.transpose(ps[4 + i // 4][:, (i % 4) * P:(i % 4) * P + rows(t)],
                                            y[0:rows(t), t % 2, i * P:(i + 1) * P], ident[0:rows(t), 0:rows(t)])
                    last.then_inc(s_tp, 1)

                for t in range(NT):
                    if t >= 2:
                        pe.wait_ge(s_y, t - 1)
                    for i in range(2):
                        last = product(pe, ps[2 * (t % 2) + i][0:rows(t), :], P,
                                       lambda kt: merged[:, kt, t * P:t * P + rows(t)],
                                       lambda kt: wo[:, kt, 512 * i:512 * i + 512], KT)
                    last.then_inc(s_full2, 1)
                    if t:
                        turn(t - 1)
                turn(NT - 1)

            @block.scalar
            def _(act):
                def spread(t):
                    act.wait_ge(s_tp, t + 1)
                    act.copy(xT[:, :, t * P:t * P + rows(t)],
                             banks[:, 4:6, :].rearrange("p b (k n) -> p (b k) n", n=P)[:, :, 0:rows(t)]).then_inc(s_tpe, 1)

                for t in range(NT):
                    act.wait_ge(s_nb, t + 1)
                    r = rows(t)
                    act.activation(y[0:r, t % 2, :], y[0:r, t % 2, :], ACT.Identity, bias=mv[0:r, t % 2, 3:4],
                                   scale=mv[0:r, t % 2, 2:3]).then_inc(s_z, 1)
                    if t:
                        spread(t - 1)
                spread(NT - 1)

            @block.gpsimd
            def _(pool):
                for t in range(NT):
                    r = rows(t)
                    pool.wait_ge(s_ve, t + 1)
                    pool.tensor_tensor(mv[0:r, t % 2, 2:3], mv[0:r, t % 2, 1:2], k.neghalf[0:r, 0:1],
                                       ALU.pow).then_inc(s_rs, 1)

            @block.vector
            def _(dve):
                n = 0

                def step(ins):
                    nonlocal n
                    n += 1
                    ins.then_inc(s_yst, 1)
                    dve.wait_ge(s_yst, n)

                dve.wait_ge(s_ln, 32)
                for t in range(NT):
                    r, s = rows(t), t % 2
                    v = y[0:r, s, :]
                    dve.wait_ge(s_xr[s], 16 * (t // 2 + 1))
                    dve.wait_ge(s_full2, t + 1)
                    if t >= 2:
                        dve.wait_ge(s_x1d[s], 16 * (t // 2))
                        dve.wait_ge(s_tp, t - 1)
                    dve.scalar_tensor_tensor(v, xr[0:r, s, :], ALPHA,
                                             banks[0:r, 2 * s:2 * s + 2, :].rearrange("p b n -> p (b n)"), ALU.mult,
                                             ALU.add).then_inc(s_y, 1)
                    dve.wait_ge(s_y, t + 1)
                    for i in range(2):
                        last = dve.bn_stats(st[0:r, i, :], y[0:r, s, 512 * i:512 * i + 512])
                    step(last)
                    step(dve.bn_aggr(mv[0:r, s, 0:2], st[0:r]))
                    dve.tensor_scalar(mv[0:r, s, 1:2], mv[0:r, s, 1:2], EPS, None, ALU.add).then_inc(s_ve, 1)
                    dve.wait_ge(s_rs, t + 1)
                    dve.scalar_tensor_tensor(mv[0:r, s, 3:4], mv[0:r, s, 0:1], -1.0, mv[0:r, s, 2:3], ALU.mult,
                                             ALU.mult).then_inc(s_nb, 1)
                    dve.wait_ge(s_z, t + 1)
                    step(dve.tensor_tensor(v, v, lng[0:r, :], ALU.mult))
                    dve.tensor_tensor(v, v, lnb[0:r, :], ALU.add).then_inc(s_x1, 1)


def build_moe(nc, a, k):
    ps, banks, ident, ones, xT, sem = k.ps, k.banks, k.ident, k.ones, k.xT, k.sem
    ds = bass.ds
    table = nc.dram_tensor("token_of_slot", (E * ECAP, 1), F32, kind="Internal").ap()
    rows_out = nc.dram_tensor("expert_rows", (E * CAP, D), F32, kind="Internal").ap()
    with ExitStack() as cm:
        def sb(name, shape, dt=F32, c=cm):
            return k.sb(name, shape, dt, c)

        acc = sb("acc", [P, NT, D])
        gate8 = sb("gate8", [P, NT, TOPK])
        exp8 = sb("exp8", [P, NT, TOPK])
        rel8 = sb("rel8", [P, NT, TOPK])
        longest = sb("longest", [P, 1], I32)

        s9 = {x: sem("s_route_" + x) for x in ("w", "wsh", "wdn", "zero", "tab", "lg", "sig", "st", "iota", "sel", "pos",
                                               "slot", "scat", "sh", "shs", "shh", "dn", "acc", "xr", "xrm")}
        s_xr = [sem("s_route_xr0"), sem("s_route_xr1")]
        shared = [(m, n0, nn) for n0, nn in TOKEN_CHUNKS for m in range(2)]
        with ExitStack() as cw, nc.Block() as block:
            rw = sb("rw", [P, KT, E], c=cw)
            rb = sb("rb", [P, E], c=cw)
            zero = sb("zero", [E, ECAP], c=cw)
            sgu = sb("sgu", [P, KT, 512], c=cw)
            sdn = sb("sdn", [P, 2, D], c=cw)
            shT = sb("shT", [P, 2, N], c=cw)
            ssg = sb("ssg", [P, 2, 512], c=cw)
            xr = sb("xr9", [P, 2, D], c=cw)
            sc = sb("sc9", [P, NT, E], c=cw)
            bi = sb("bi", [P, NT, E], c=cw)
            sel = sb("sel", [P, NT, E], c=cw)
            t1 = sb("t1", [P, NT, E], c=cw)
            gates = sb("gates", [P, NT, E], c=cw)
            val = sb("val", [P, NT, E], c=cw)
            cum = sb("cum", [P, NT, E], c=cw)
            m8 = sb("m8", [P, NT * EG, 8], c=cw)
            gs = sb("gs", [P, NT * EG], c=cw)
            rank = sb("rank", [P, NT * EG], c=cw)
            lower = sb("lower", [P, EG, EG], c=cw)
            slot0 = sb("slot0", [P, E], c=cw)
            den = sb("den9", [P, NT], c=cw)
            v8 = sb("v8", [P, NT, TOPK], c=cw)
            i8 = sb("i8", [P, NT, TOPK], I32, cw)
            j8 = sb("j8", [P, NT, TOPK], I32, cw)
            slot8 = sb("slot8", [P, NT, TOPK], I32, cw)
            token = sb("token", [P, NT], c=cw)
            lmax = sb("lmax", [P, 1], c=cw)

            @block.sync
            def _(sp):
                sp.dma_start(rw[:], a["router_w"][0].rearrange("(k p) e -> p k e", p=P)).then_inc(s9["w"], 16)
                sp.dma_start(rb[:], a["router_b"].broadcast_to([P, E])).then_inc(s9["w"], 16)
                sp.dma_start(sgu[:], a["sh_gu"][0].rearrange("(k p) n -> p k n", p=P)).then_inc(s9["wsh"], 16)
                sp.dma_start(sdn[:], a["sh_down"][0].rearrange("(k p) n -> p k n", p=P)).then_inc(s9["wdn"], 16)
                sp.wait_ge(s9["zero"], 1)
                sp.dma_start(table.rearrange("(e c) o -> e (c o)", e=E), zero[:]).then_inc(s9["tab"], 16)
                for t in range(NT):
                    if t >= 2:
                        sp.wait_ge(s9["acc"], t - 1)
                    sp.dma_start(xr[0:rows(t), t % 2, :], k.x1[t * P:t * P + rows(t), :]).then_inc(s_xr[t % 2], 16)

            @block.gpsimd
            def _(pool):
                pool.memset(zero[:], 0.0).then_inc(s9["zero"], 1)
                pool.memset(lower[:], 1.0).then_inc(s9["zero"], 1)
                pool.iota(slot0[:], pattern=[[1 << SHIFT, E]], base=1, channel_multiplier=0,
                          allow_small_or_imprecise_dtypes=True).then_inc(s9["iota"], 1)
                pool.iota(token[:], pattern=[[P, NT]], base=0, channel_multiplier=1,
                          allow_small_or_imprecise_dtypes=True).then_inc(s9["iota"], 1)
                pool.wait_ge(s9["zero"], 2)
                pool.affine_select(out=lower[:], in_=lower[:], compare_op=ALU.is_ge, fill=0.0, base=-1,
                                   pattern=[[1, EG], [-1, EG]], channel_multiplier=0).then_inc(s9["iota"], 1)
                pool.wait_ge(s9["tab"], 16)
                pool.wait_ge(s9["slot"], 1)
                pool.wait_ge(s9["iota"], 3)
                for t in range(NT):
                    for i in range(TOPK):
                        pool.indirect_dma_start(table, bass.IndirectOffsetOnAxis(ap=slot8[0:rows(t), t, i:i + 1], axis=0),
                                                token[0:rows(t), t:t + 1], None).then_inc(s9["scat"], 16)
                pool.wait_ge(s9["scat"], 16 * NT * TOPK)

            @block.tensor
            def _(pe):
                pe.wait_ge(s9["w"], 32)
                for t in range(NT):
                    last = product(pe, ps[t // 8][0:rows(t), (t % 8) * E:(t % 8 + 1) * E], P,
                                   lambda kt: xT[:, kt, t * P:t * P + rows(t)], lambda kt: rw[:, kt, :], KT)
                last.then_inc(s9["lg"], 1)
                def places():
                    pe.wait_ge(s9["sel"], 1)
                    for t in range(NT):
                        out = ps[2 + t // 8][:, (t % 8) * E:(t % 8 + 1) * E]
                        pe.matmul(out, k.before[:], sel[:, t, :], start=True, stop=(t == 0))
                        if t:
                            pe.matmul(out, ones[:], cum[:, t - 1, :], start=False, stop=True)
                    pe.matmul(ps[3][:, E:2 * E], ones[:], cum[:, NT - 1, :], start=True, stop=True).then_inc(s9["pos"], 1)

                pe.wait_ge(s9["wsh"], 16)
                for j, (m, n0, nn) in enumerate(shared):
                    if j == 2:
                        places()
                    if j >= 2:
                        pe.wait_ge(s9["shh"], j - 1)
                    b = 4 + 2 * (j % 2)
                    product(pe, ps[b][:, 0:nn], P, lambda kt: sgu[:, kt, m * P:(m + 1) * P],
                            lambda kt: xT[:, kt, n0:n0 + nn], KT)
                    product(pe, ps[b + 1][:, 0:nn], P, lambda kt: sgu[:, kt, F + m * P:F + (m + 1) * P],
                            lambda kt: xT[:, kt, n0:n0 + nn], KT).then_inc(s9["sh"], 1)
                pe.wait_ge(s9["wdn"], 16)
                pe.wait_ge(s9["shh"], len(shared))

                def down(t):
                    if t >= 2:
                        pe.wait_ge(s9["acc"], t - 1)
                    for i in range(2):
                        last = product(pe, ps[4 + 2 * (t % 2) + i][0:rows(t), :], P,
                                       lambda kt: shT[:, kt, t * P:t * P + rows(t)],
                                       lambda kt: sdn[:, kt, 512 * i:512 * i + 512], 2)
                    last.then_inc(s9["dn"], 1)

                down(0)
                down(1)
                for t in range(2, NT):
                    down(t)

            @block.scalar
            def _(act):
                act.wait_ge(s9["lg"], 1)
                act.activation(sc[:, 0:8, :], ps[0].rearrange("p (t e) -> p t e", t=8), ACT.Sigmoid)
                act.activation(sc[0:SM, 8, :], ps[1][0:SM, 0:E], ACT.Sigmoid).then_inc(s9["sig"], 1)
                for j, (m, n0, nn) in enumerate(shared):
                    b = 4 + 2 * (j % 2)
                    act.wait_ge(s9["sh"], j + 1)
                    act.activation(ssg[:, j % 2, 0:nn], ps[b][:, 0:nn], ACT.Silu).then_inc(s9["shs"], 1)
                for t in range(NT):
                    r = rows(t)
                    act.wait_ge(s_xr[t % 2], 16 * (t // 2 + 1))
                    act.activation(acc[0:r, t, :], xr[0:r, t % 2, :], ACT.Copy, scale=ALPHA).then_inc(s9["xrm"], 1)
                    act.wait_ge(s9["acc"], t + 1)

            @block.vector
            def _(dve):
                n = 0

                def step(ins):
                    nonlocal n
                    n += 1
                    ins.then_inc(s9["st"], 1)
                    dve.wait_ge(s9["st"], n)

                def by_group(x):
                    return x[:].rearrange("p t (g e) -> p (t g) e", e=E // EG)

                def pairs(x, at):
                    return x[:].rearrange("p (t g) -> p t g", g=EG).unsqueeze(at).to_broadcast([P, NT, EG, EG])

                step(dve.memset(sc[SM:P, 8, :], 0.5))
                dve.wait_ge(s9["w"], 32)
                dve.wait_ge(s9["sig"], 1)
                step(dve.tensor_tensor(bi[:], sc[:], rb[:].unsqueeze(1).to_broadcast([P, NT, E]), ALU.add))
                for i in range(NT * EG):
                    last = dve.max(m8[:, i, :], by_group(bi)[:, i, :])
                step(last)
                step(dve.tensor_tensor(gs[:].unsqueeze(2), m8[:, :, 0:1], m8[:, :, 1:2], ALU.add))
                dve.wait_ge(s9["iota"], 3)
                p1 = t1[:].rearrange("p t (i j) -> p t i j", i=EG)
                p2 = sel[:].rearrange("p t (i j) -> p t i j", i=EG)
                dve.tensor_tensor(p1, pairs(gs, 2), pairs(gs, 3), ALU.is_gt)
                step(dve.tensor_tensor(p2, pairs(gs, 2), pairs(gs, 3), ALU.is_equal))
                step(dve.tensor_tensor(p2, p2, lower[:].unsqueeze(1).to_broadcast([P, NT, EG, EG]), ALU.mult))
                step(dve.tensor_tensor(p1, p1, p2, ALU.add))
                step(dve.tensor_reduce(rank[:].rearrange("p (t g) -> p t g", g=EG), p1, AX, ALU.add))
                step(dve.tensor_scalar(rank[:], rank[:], float(TOPG), 1.0, ALU.is_lt, ALU.subtract))
                step(dve.tensor_scalar(rank[:], rank[:], BIG, None, ALU.mult))
                step(dve.tensor_tensor(by_group(bi), by_group(bi), rank[:].unsqueeze(2).to_broadcast([P, NT * EG, E // EG]),
                                       ALU.add))
                for t in range(NT):
                    last = dve.max(v8[:, t, :], bi[:, t, :])
                step(last)
                for t in range(NT):
                    last = dve.match_replace(t1[:, t, :], v8[:, t, :], bi[:, t, :], GONE)
                step(last)
                step(dve.tensor_scalar(sel[:], t1[:], GONE, None, ALU.is_equal))
                step(dve.memset(sel[SM:P, 8, :], 0.0))
                step(dve.tensor_copy(cum[:, 0, :], sel[:, 0, :]))
                for t in range(1, NT):
                    step(dve.tensor_tensor(cum[:, t, :], cum[:, t - 1, :], sel[:, t, :], ALU.add))
                dve.sem_inc(s9["sel"], 1)

                def gated(j):
                    m, n0, nn = shared[j]
                    dve.wait_ge(s9["shs"], j + 1)
                    dve.tensor_tensor(shT[:, m, n0:n0 + nn], ssg[:, j % 2, 0:nn], ps[5 + 2 * (j % 2)][:, 0:nn],
                                      ALU.mult).then_inc(s9["shh"], 1)

                gated(0)
                gated(1)
                step(dve.tensor_tensor(gates[:], sc[:], sel[:], ALU.mult))
                step(dve.tensor_reduce(den[:], gates[:], AX, ALU.add))
                step(dve.memset(den[SM:P, 8:9], 1.0))
                step(dve.reciprocal(den[:], den[:]))
                step(dve.tensor_scalar(den[:], den[:], 2.5, None, ALU.mult))
                step(dve.tensor_tensor(gates[:], gates[:], den[:].unsqueeze(2).to_broadcast([P, NT, E]), ALU.mult))
                dve.wait_ge(s9["pos"], 1)
                dve.tensor_tensor(val[:, 0:8, :], ps[2].rearrange("p (t e) -> p t e", t=8),
                                  slot0[:].unsqueeze(1).to_broadcast([P, 8, E]), ALU.add)
                step(dve.tensor_tensor(val[:, 8, :], ps[3][:, 0:E], slot0[:], ALU.add))
                step(dve.tensor_tensor(val[:], val[:], sel[:], ALU.mult))
                step(dve.tensor_scalar(val[:], val[:], 1.0, None, ALU.subtract))
                dve.tensor_reduce(lmax[:], ps[3][:, E:2 * E], AX, ALU.max)
                for t in range(NT):
                    last = dve.max(v8[:, t, :], val[:, t, :])
                step(last)
                dve.tensor_copy(longest[:], lmax[:])
                step(dve.tensor_copy(i8[:], v8[:]))
                dve.tensor_scalar(j8[:], i8[:], SHIFT, None, ALU.arith_shift_right)
                step(dve.tensor_scalar(i8[:], i8[:], (1 << SHIFT) - 1, None, ALU.bitwise_and))
                dve.tensor_copy(rel8[:], i8[:])
                step(dve.tensor_copy(exp8[:], j8[:]))
                step(dve.scalar_tensor_tensor(slot8[:], exp8[:], float(ECAP), rel8[:], ALU.mult, ALU.add))
                dve.sem_inc(s9["slot"], 1)
                step(dve.tensor_scalar(exp8[:], exp8[:], float(CAP), None, ALU.mult))
                for j in range(2, len(shared)):
                    gated(j)
                for i in range(TOPK):
                    step(dve.tensor_tensor(t1[:], val[:], v8[:, :, i:i + 1].to_broadcast([P, NT, E]), ALU.is_equal))
                    step(dve.tensor_tensor(t1[:], t1[:], gates[:], ALU.mult))
                    step(dve.tensor_reduce(gate8[:, :, i:i + 1].rearrange("p t o -> p (t o)"), t1[:], AX, ALU.add))
                for t in range(NT):
                    r, b = rows(t), 4 + 2 * (t % 2)
                    dve.wait_ge(s9["dn"], t + 1)
                    dve.wait_ge(s9["xrm"], t + 1)
                    dve.tensor_tensor(acc[0:r, t, :], acc[0:r, t, :],
                                      banks[0:r, b:b + 2, :].rearrange("p b n -> p (b n)"), ALU.add).then_inc(s9["acc"], 1)

        s_r = {x: sem("s_round_" + x) for x in ("tab", "turn", "ids", "step", "tp", "xev", "gu", "silu", "h", "down",
                                                "yev", "idx", "comb", "seen", "dh", "dl", "hh", "hl")}
        s_w = [[sem(f"s_round_wgu{i}"), sem(f"s_round_wdn{i}")] for i in range(2)]
        s_xg = [sem(f"s_round_xg{i}") for i in range(2)]
        s_ys = [sem(f"s_round_stored{i}") for i in range(2)]
        s_yb = [sem(f"s_round_back{i}") for i in range(4)]
        everything = list(s_r.values()) + s_w[0] + s_w[1] + s_xg + s_ys + s_yb
        count = nc.values_load(longest[0:1, 0:1], min_val=1, max_val=N)
        SLOTS = ((0, P), (P, CAP - P))
        TURNS = ((0, P, 0, 4), (1, CAP - P, 0, KT), (0, P, 4, 4))
        TURN_BANKS, DOWN_BANKS = (0, 1, 7), (4, 5, 6, 4)
        with nc.Fori(0, ROUNDS) as r, nc.If(count > r * CAP):
            with ExitStack() as cw, nc.Block() as block:
                wgu = sb("wgu", [P, 2, KT, 2 * F], c=cw)
                wdn = k.xT[:].rearrange("p k n -> p (k n)")[:, 0:4 * D].rearrange("p (u k n) -> p u k n", u=2, k=2)
                tab = sb("tab", [E, CAP], c=cw)
                ids = sb("ids", [P, 2, E], I32, cw)
                xg = sb("xg", [P, 2, 2, D], c=cw)
                xgT = sb("xgT", [P, 2, KT, CAP], c=cw)
                sg = sb("sgr", [P, 2, 2, CAP], c=cw)
                wdn_h = sb("wdn_h", [P, 2, 2, D], F32R, cw)
                wdn_l = sb("wdn_l", [P, 2, 2, D], F32R, cw)
                hh_h = sb("hh_h", [P, 2, 2, CAP], F32R, cw)
                hh_l = sb("hh_l", [P, 2, 2, CAP], F32R, cw)
                y = sb("yr", [P, 2, 2, D], c=cw)
                gu_view = a["exp_gu"][0].rearrange("e (k p) n -> p e k n", p=P)
                dn_view = a["exp_down"][0].rearrange("e (k p) n -> p e k n", p=P)
                last_pair = E // 2 - 1

                @block.sync
                def _(sp):
                    sp.dma_start(tab[:], table.rearrange("(e c) o -> e (c o)", e=E)[:, ds(r * CAP, CAP)]
                                 ).then_inc(s_r["tab"], 16)

                    def load_gu(e, u):
                        sp.dma_start(wgu[:, u], gu_view[:, ds(e, 1)].rearrange("p o k n -> p (o k) n")).then_inc(s_w[u][0], 16)

                    def load_dn(e, u):
                        sp.dma_start(wdn[:, u], dn_view[:, ds(e, 1)].rearrange("p o k n -> p (o k) n")).then_inc(s_w[u][1], 16)

                    def store(e, u, n):
                        sp.wait_ge(s_r["yev"], n)
                        for i, (at, c) in enumerate(SLOTS):
                            sp.dma_start(rows_out[ds(e * CAP + at, c), :], y[0:c, u, i, :]).then_inc(s_ys[u], 16)

                    for u in range(2):
                        load_gu(u, u)
                        load_dn(u, u)
                    with sp.Fori(0, last_pair) as i:
                        for u in range(2):
                            sp.wait_ge(s_r["dl"], i * 2 + (u + 1))
                            load_dn(i * 2 + (u + 2), u)
                            sp.wait_ge(s_r["gu"], i * 4 + (2 * u + 2))
                            load_gu(i * 2 + (u + 2), u)
                            store(i * 2 + u, u, i * 8 + (4 * u + 4))
                    for u in range(2):
                        store(2 * last_pair + u, u, 8 * last_pair + 4 * u + 4)
                    for u in range(2):
                        sp.wait_ge(s_ys[u], 32 * (last_pair + 1))

                @block.gpsimd
                def _(pool):
                    pool.wait_ge(s_r["ids"], 1)
                    for e in range(E):
                        u, n = e % 2, e // 2
                        if n:
                            pool.wait_ge(s_xg[u], 32 * n)
                            pool.wait_ge(s_r["tp"], 3 * (e - 1))
                        for i, (at, c) in enumerate(SLOTS):
                            pool.indirect_dma_start(xg[0:c, u, i, :], None, k.x1,
                                                    bass.IndirectOffsetOnAxis(ap=ids[0:c, i, e:e + 1], axis=0)
                                                    ).then_inc(s_xg[u], 16)
                    for u in range(2):
                        pool.wait_ge(s_xg[u], 32 * (last_pair + 1))

                @block.tensor
                def _(pe):
                    pe.wait_ge(s_r["tab"], 16)
                    pe.transpose(ps[0][:, 0:E], tab[:, 0:P], ident[0:E, 0:E])
                    pe.transpose(ps[0][0:CAP - P, E:2 * E], tab[:, P:CAP], ident[0:E, 0:E]).then_inc(s_r["turn"], 1)
                    pe.wait_ge(s_r["ids"], 1)

                    def turn(u, n, first):
                        if not first or u:
                            pe.wait_ge(s_r["xev"], n * 6 + 3 * u)
                        pe.wait_ge(s_xg[u], n * 32 + 32)
                        for q in range(3):
                            i, c, k0, kn = TURNS[q]
                            for kt in range(kn):
                                last = pe.transpose(ps[TURN_BANKS[q]][:, kt * c:(kt + 1) * c],
                                                    xg[0:c, u, i, (k0 + kt) * P:(k0 + kt + 1) * P], ident[0:c, 0:c])
                            last.then_inc(s_r["tp"], 1)

                    def gate_up(u, n, first):
                        pe.wait_ge(s_w[u][0], n * 16 + 16)
                        pe.wait_ge(s_r["xev"], n * 6 + (3 * u + 3))
                        for j in range(2):
                            if not (first and u == 0):
                                pe.wait_ge(s_r["h"], n * 4 + (2 * u + j - 1))
                            for i, m in enumerate((j, 2 + j)):
                                last = product(pe, ps[2 + j][:, i * CAP:(i + 1) * CAP], P,
                                               lambda kt: wgu[:, u, kt, m * P:(m + 1) * P], lambda kt: xgT[:, u, kt, :], KT)
                            last.then_inc(s_r["gu"], 1)

                    def down(u, n, first):
                        pe.wait_ge(s_r["dl"], n * 2 + (u + 1))
                        pe.wait_ge(s_r["hl"], n * 4 + (2 * u + 2))
                        for q in range(4):
                            (at, c), i = SLOTS[q // 2], q % 2
                            if q == 3:
                                pe.wait_ge(s_r["yev"], n * 8 + (4 * u + 1))
                            elif not (first and u == 0):
                                pe.wait_ge(s_r["yev"], n * 8 + (4 * u + (0, -2, -1)[q]))
                            last = split_product(
                                pe, ps[DOWN_BANKS[q]][0:c, :],
                                lambda kt: (hh_h[:, u, kt, at:at + c], hh_l[:, u, kt, at:at + c]),
                                lambda kt: (wdn_h[:, u, kt, 512 * i:512 * i + 512],
                                            wdn_l[:, u, kt, 512 * i:512 * i + 512]), 2)
                            last.then_inc(s_r["down"], 1)

                    turn(0, 0, True)
                    gate_up(0, 0, True)
                    turn(1, 0, True)
                    down(0, 0, True)
                    gate_up(1, 0, False)
                    turn(0, 1, False)
                    down(1, 0, False)
                    with pe.Fori(0, last_pair // 2) as two:
                        for i in (two * 2 + 1, two * 2 + 2):
                            gate_up(0, i, False)
                            turn(1, i, False)
                            down(0, i, False)
                            gate_up(1, i, False)
                            turn(0, i + 1, False)
                            down(1, i, False)
                    gate_up(0, last_pair, False)
                    turn(1, last_pair, False)
                    down(0, last_pair, False)
                    gate_up(1, last_pair, False)
                    down(1, last_pair, False)

                @block.scalar
                def _(act):
                    def spread(u, n, first):
                        for q in range(3):
                            at = 3 * u + q
                            act.wait_ge(s_r["tp"], n * 6 + (at + 1))
                            if q == 0 and not first:
                                act.wait_ge(s_r["gu"], n * 4 + (2 * u - 2))
                            if q != 1:
                                act.copy(xgT[:, u, 2 * q:2 * q + 4, 0:P],
                                         ps[TURN_BANKS[q]].rearrange("p (k c) -> p k c", k=4)).then_inc(s_r["xev"], 1)
                            else:
                                act.copy(xgT[:, u, :, P:CAP],
                                         ps[TURN_BANKS[q]][:, 0:KT * (CAP - P)].rearrange("p (k c) -> p k c", k=KT)
                                         ).then_inc(s_r["xev"], 1)

                    def silu(u, n, first):
                        act.wait_ge(s_w[u][1], n * 16 + 16)
                        if not first:
                            act.wait_ge(s_r["down"], n * 8 + (4 * u - 4))
                        act.copy(wdn_h[:, u], wdn[:, u]).then_inc(s_r["dh"], 1)
                        for j in range(2):
                            act.wait_ge(s_r["gu"], n * 4 + (2 * u + j + 1))
                            act.activation(sg[:, u, j, :], ps[2 + j][:, 0:CAP], ACT.Silu).then_inc(s_r["silu"], 1)

                    spread(0, 0, True)
                    silu(0, 0, True)
                    spread(1, 0, True)
                    silu(1, 0, True)
                    spread(0, 1, False)
                    with act.Fori(0, last_pair // 2) as two:
                        for i in (two * 2 + 1, two * 2 + 2):
                            silu(0, i, False)
                            spread(1, i, False)
                            silu(1, i, False)
                            spread(0, i + 1, False)
                    silu(0, last_pair, False)
                    spread(1, last_pair, False)
                    silu(1, last_pair, False)

                @block.vector
                def _(dve):
                    dve.memset(ids[:, 1, :], 0)
                    dve.wait_ge(s_r["turn"], 1)
                    dve.tensor_copy(ids[:, 0, :], ps[0][:, 0:E]).then_inc(s_r["step"], 1)
                    dve.wait_ge(s_r["step"], 1)
                    dve.tensor_copy(ids[0:CAP - P, 1, :], ps[0][0:CAP - P, E:2 * E]).then_inc(s_r["ids"], 1)

                    def expert(u, n, first):
                        dve.wait_ge(s_r["dh"], n * 2 + (u + 1))
                        if not first:
                            dve.wait_ge(s_r["down"], n * 8 + (4 * u - 4))
                        dve.tensor_tensor(wdn_l[:, u], wdn[:, u], wdn_h[:, u].bitcast(F32), ALU.subtract
                                          ).then_inc(s_r["dl"], 1)
                        for j in range(2):
                            now, g = n * 4 + (2 * u + j + 1), sg[:, u, j, :]
                            dve.wait_ge(s_r["silu"], now)
                            dve.tensor_tensor(g, g, ps[2 + j][:, CAP:2 * CAP], ALU.mult).then_inc(s_r["h"], 1)
                            dve.wait_ge(s_r["h"], now)
                            dve.tensor_copy(hh_h[:, u, j, :], g).then_inc(s_r["hh"], 1)
                            dve.wait_ge(s_r["hh"], now)
                            dve.tensor_tensor(hh_l[:, u, j, :], g, hh_h[:, u, j, :].bitcast(F32), ALU.subtract
                                              ).then_inc(s_r["hl"], 1)
                        if not first:
                            dve.wait_ge(s_ys[u], n * 32)
                        for q in range(4):
                            (at, c), i = SLOTS[q // 2], q % 2
                            dve.wait_ge(s_r["down"], n * 8 + (4 * u + q + 1))
                            dve.tensor_copy(y[0:c, u, q // 2, 512 * i:512 * i + 512], ps[DOWN_BANKS[q]][0:c, :]
                                            ).then_inc(s_r["yev"], 1)

                    expert(0, 0, True)
                    expert(1, 0, True)
                    with dve.Fori(1, last_pair + 1) as i:
                        expert(0, i, False)
                        expert(1, i, False)

            with ExitStack() as cw, nc.Block() as block:
                lo = sb("lo", [P, NT, TOPK], c=cw)
                gw = sb("gw", [P, NT, TOPK], c=cw)
                at8 = sb("at8", [P, NT, TOPK], I32, cw)
                back = sb("back", [P, 4, D], c=cw)
                rounds = [(t, i) for t in range(NT) for i in range(TOPK)]

                @block.gpsimd
                def _(pool):
                    pool.wait_ge(s_r["idx"], 1)
                    for n, (t, i) in enumerate(rounds):
                        if n >= 4:
                            pool.wait_ge(s_r["comb"], n - 3)
                        pool.indirect_dma_start(back[0:rows(t), n % 4, :], None, rows_out,
                                                bass.IndirectOffsetOnAxis(ap=at8[0:rows(t), t, i:i + 1], axis=0)
                                                ).then_inc(s_yb[n % 4], 16)
                    for i in range(4):
                        pool.wait_ge(s_yb[i], 16 * len(rounds) // 4)

                @block.vector
                def _(dve):
                    dve.tensor_scalar(lo[:], rel8[:], 0.0, None, ALU.is_ge)
                    dve.tensor_scalar(gw[:], rel8[:], float(CAP), None, ALU.is_lt).then_inc(s_r["seen"], 1)
                    dve.wait_ge(s_r["seen"], 1)
                    dve.tensor_tensor(gw[:], gw[:], lo[:], ALU.mult).then_inc(s_r["seen"], 1)
                    dve.wait_ge(s_r["seen"], 2)
                    dve.tensor_scalar(lo[:], rel8[:], 0.0, float(CAP - 1), ALU.max, ALU.min)
                    dve.tensor_tensor(gw[:], gw[:], gate8[:], ALU.mult).then_inc(s_r["seen"], 1)
                    dve.wait_ge(s_r["seen"], 3)
                    dve.tensor_tensor(at8[:], lo[:], exp8[:], ALU.add).then_inc(s_r["idx"], 1)
                    dve.tensor_scalar(rel8[:], rel8[:], float(CAP), None, ALU.subtract).then_inc(s_r["seen"], 1)
                    for n, (t, i) in enumerate(rounds):
                        dve.wait_ge(s_yb[n % 4], 16 * (n // 4 + 1))
                        if n:
                            dve.wait_ge(s_r["comb"], n)
                        rr = rows(t)
                        dve.scalar_tensor_tensor(acc[0:rr, t, :], back[0:rr, n % 4, :], gw[0:rr, t, i:i + 1],
                                                 acc[0:rr, t, :], ALU.mult, ALU.add).then_inc(s_r["comb"], 1)
                    dve.wait_ge(s_r["comb"], len(rounds))

            with nc.Block() as block:
                @block.gpsimd
                def _(pool):
                    pool.dma_reset()
                    for s in everything:
                        pool.sem_clear(s)
            nc.all_engine_barrier()

        s_f = {x: sem("s_last_" + x) for x in ("ln", "st", "ve", "rs", "nb", "z", "g", "y", "out")}
        with ExitStack() as cw, nc.Block() as block:
            lng = sb("ln2g", [P, D], c=cw)
            lnb = sb("ln2b", [P, D], c=cw)
            st = sb("st2", [P, 2, 6], c=cw)
            mv = sb("mv2", [P, NT, 4], c=cw)

            @block.sync
            def _(sp):
                sp.dma_start(lng[:], a["ln2_g"].broadcast_to([P, D])).then_inc(s_f["ln"], 16)
                sp.dma_start(lnb[:], a["ln2_b"].broadcast_to([P, D])).then_inc(s_f["ln"], 16)
                y_p = a["y_prompt"].rearrange("b t d -> (b t) d")
                y_s = a["y_sample"].rearrange("b t d -> (b t) d")
                for t in range(NT):
                    sp.wait_ge(s_f["y"], t + 1)
                    sp.dma_start(k.token_rows(y_p, y_s, t), acc[0:rows(t), t, :]).then_inc(s_f["out"], 16)
                sp.wait_ge(s_f["out"], 16 * NT)

            @block.gpsimd
            def _(pool):
                def add_bias(t):
                    v, r = acc[0:rows(t), t, :], rows(t)
                    pool.wait_ge(s_f["g"], t + 1)
                    pool.tensor_tensor(v, v, lnb[0:r, :], ALU.add).then_inc(s_f["y"], 1)

                pool.wait_ge(s_f["ln"], 32)
                for t in range(NT):
                    pool.wait_ge(s_f["ve"], t + 1)
                    pool.tensor_tensor(mv[0:rows(t), t, 2:3], mv[0:rows(t), t, 1:2], k.neghalf[0:rows(t), 0:1],
                                       ALU.pow).then_inc(s_f["rs"], 1)
                    if t:
                        add_bias(t - 1)
                add_bias(NT - 1)

            @block.scalar
            def _(act):
                for t in range(NT):
                    act.wait_ge(s_f["nb"], t + 1)
                    r = rows(t)
                    act.activation(acc[0:r, t, :], acc[0:r, t, :], ACT.Identity, bias=mv[0:r, t, 3:4],
                                   scale=mv[0:r, t, 2:3]).then_inc(s_f["z"], 1)

            @block.vector
            def _(dve):
                n = 0

                def step(ins):
                    nonlocal n
                    n += 1
                    ins.then_inc(s_f["st"], 1)
                    dve.wait_ge(s_f["st"], n)

                def gain(t):
                    v, r = acc[0:rows(t), t, :], rows(t)
                    dve.wait_ge(s_f["z"], t + 1)
                    dve.tensor_tensor(v, v, lng[0:r, :], ALU.mult).then_inc(s_f["g"], 1)

                for t in range(NT):
                    v, r = acc[0:rows(t), t, :], rows(t)
                    for i in range(2):
                        last = dve.bn_stats(st[0:r, i, :], acc[0:r, t, 512 * i:512 * i + 512])
                    step(last)
                    step(dve.bn_aggr(mv[0:r, t, 0:2], st[0:r]))
                    dve.tensor_scalar(mv[0:r, t, 1:2], mv[0:r, t, 1:2], EPS, None, ALU.add).then_inc(s_f["ve"], 1)
                    if t == 0:
                        dve.wait_ge(s_f["ln"], 32)
                    else:
                        gain(t - 1)
                    dve.wait_ge(s_f["rs"], t + 1)
                    dve.scalar_tensor_tensor(mv[0:r, t, 3:4], mv[0:r, t, 0:1], -1.0, mv[0:r, t, 2:3], ALU.mult,
                                             ALU.mult).then_inc(s_f["nb"], 1)
                gain(NT - 1)


OUTS = (("y_prompt", (1, SEQ, D)), ("y_sample", (NB, NS, D)),
        ("k_prompt", (1, 1, SEQ, BKV, BD)), ("k_sample", (1, NB, NS, BKV, BD)),
        ("v_prompt", (1, 1, SEQ, BKV, BD)), ("v_sample", (1, NB, NS, BKV, BD)),
        ("kidx_prompt", (1, 1, SEQ, BD)), ("kidx_sample", (1, NB, NS, BD)),
        ("C_prompt", (1, 1, H, HD, HD)), ("C_sample", (1, NB, H, HD, HD)),
        ("n_prompt", (1, 1, H, HD)), ("n_sample", (1, NB, H, HD)),
        ("m_prompt", (1, 1, H)), ("m_sample", (1, NB, H)),
        ("pool_prompt", (1, 1, POOLB, 512)), ("pool_sample", (1, NB, POOLB, 512)))


def kernel(**inputs):
    import concourse.bacc as bacc
    from concourse.bass_utils import run_bass_kernel_spmd

    nc = bacc.Bacc("TRN2", target_bir_lowering=False, num_devices=1)
    arrays, io = {}, {}
    for name, value in inputs.items():
        arrays[f"in_{name}"] = np.ascontiguousarray(value)
        io[name] = nc.dram_tensor(f"in_{name}", arrays[f"in_{name}"].shape,
                                  mybir.dt.from_np(arrays[f"in_{name}"].dtype), kind="ExternalInput").ap()
    for name, shape in OUTS:
        io[name] = nc.dram_tensor(f"out_{name}", shape, F32, kind="ExternalOutput").ap()
    build(nc, io)
    r = run_bass_kernel_spmd(nc, [arrays], core_ids=[0])
    return tuple(r.results[0][f"out_{name}"] for name, _ in OUTS)
```
